# Optimizing a Trainium2 kernel written in Bass

```python
import math
import jax, jax.numpy as jnp
from jax import lax
import numpy as np

D_MODEL = 1024
BATCH = 1
SEQ = 128
DEPTH = 2
DEC_BATCH = 1
DEC_SEQ = 256
PAST_LEN = 128

GRID_W = 64
N_RG = (DEPTH + 1) // 2
N_GLA = DEPTH // 2
N_ADA = 6
EPS = 1e-6
D_RNN = D_MODEL
CONV_W = 4
CONV_LEFT = 2
RG_BLOCKS = 16
RG_BW = D_RNN // RG_BLOCKS
RG_C = 8.0
GLA_HEADS = 4
GLA_DK = D_MODEL // 2 // GLA_HEADS
GLA_DV = D_MODEL // GLA_HEADS
GLA_QK = GLA_HEADS * GLA_DK
GLA_V = GLA_HEADS * GLA_DV
GLA_RANK = 16
GLA_TAU = 16.0
GLA_CHUNK = 64
GLA_IN = 2 * GLA_QK + 2 * GLA_V + 2 * GLA_RANK
PEER_HEADS = 8
PEER_NKEYS = 128
PEER_N = PEER_NKEYS * PEER_NKEYS
PEER_DKEY = 256
PEER_HALF = PEER_DKEY // 2
PEER_TOPK = 16
PEER_BLOCK = 128

kernel_name = 'hybrid_rglru_gla_peer_diffusion_step'

def rmsnorm(x, g):
    xf = x.astype(jnp.float32)
    y = xf * lax.rsqrt(jnp.mean(xf * xf, axis=-1, keepdims=True) + EPS)
    return (y * g.astype(jnp.float32)).astype(x.dtype)

def pre_mod(x, g, shift, scale):
    return rmsnorm(x, g) * (1 + scale) + shift

def ada_mod(cond, w, b):
    m = (jax.nn.silu(cond) @ w + b).reshape(cond.shape[0], N_ADA, cond.shape[-1])
    return [m[:, i, None, :] for i in range(N_ADA)]

def grid_pos_embed(rows, dim):
    t = jnp.arange(rows * GRID_W)
    r = (t // GRID_W).astype(jnp.float32)
    col = (t % GRID_W).astype(jnp.float32)
    nf = dim // 4
    freq = 1.0 / (10000.0 ** (jnp.arange(nf, dtype=jnp.float32) / nf))
    ar = r[:, None] * freq
    ac = col[:, None] * freq
    return jnp.concatenate([jnp.sin(ar), jnp.cos(ar), jnp.sin(ac), jnp.cos(ac)], axis=-1)

def to_col_major(x, rows):
    b, n, d = x.shape
    return x.reshape(b, rows, GRID_W, d).swapaxes(1, 2).reshape(b, n, d)

def from_col_major(x, rows):
    b, n, d = x.shape
    return x.reshape(b, GRID_W, rows, d).swapaxes(1, 2).reshape(b, n, d)

def centred_conv(x, w, b):
    L = x.shape[1]
    xp = jnp.pad(x, ((0, 0), (CONV_LEFT, CONV_W - 1 - CONV_LEFT), (0, 0)))
    return sum(xp[:, j:j + L] * w[j] for j in range(CONV_W)) + b

def block_diag(x, w, b):
    xb = x.reshape(x.shape[:-1] + (RG_BLOCKS, RG_BW))
    return jnp.einsum('blni,nij->blnj', xb, w).reshape(x.shape) + b

def linear_scan(a, b, h0):
    b = b.at[:, 0].add(a[:, 0] * h0)
    def comb(l, r):
        return (l[0] * r[0], r[0] * l[1] + r[1])
    _, h = lax.associative_scan(comb, (a, b), axis=1)
    return h

def rglru_dir(xc, wa, ba, wi, bi, lam, h0):
    r = jax.nn.sigmoid(block_diag(xc, wa, ba).astype(jnp.float32))
    i = jax.nn.sigmoid(block_diag(xc, wi, bi).astype(jnp.float32))
    log_a = -RG_C * r * jax.nn.softplus(-lam.astype(jnp.float32))
    a = jnp.exp(log_a)
    b = jnp.sqrt(-jnp.expm1(2.0 * log_a)) * (i * xc)
    h = linear_scan(a, b, h0.astype(jnp.float32))
    return h, h[:, -1]

def rglru_mixer(xm, p, h0):
    w_in, conv_w, conv_b, wa, ba, wi, bi, lam, w_out = p
    proj = xm @ w_in
    gate_br = jax.nn.gelu(proj[..., :D_RNN])
    xr = centred_conv(proj[..., D_RNN:], conv_w, conv_b).astype(jnp.float32)
    hf, sf = rglru_dir(xr, wa[0], ba[0], wi[0], bi[0], lam[0], h0[:, 0])
    hb, sb = rglru_dir(xr[:, ::-1], wa[1], ba[1], wi[1], bi[1], lam[1], h0[:, 1])
    h = hf + hb[:, ::-1]
    out = (gate_br * h.astype(gate_br.dtype)) @ w_out
    return out, jnp.stack([sf, sb], axis=1)

def gla_dir(q, k, v, log_a, s0):
    B, H, L, _ = q.shape
    C = GLA_CHUNK
    n = L // C
    q, k, v, log_a = [t.reshape(B, H, n, C, t.shape[-1]) for t in (q, k, v, log_a)]
    bcum = jnp.cumsum(log_a, axis=3)
    blast = bcum[:, :, :, -1:]
    q_in = q * jnp.exp(bcum)
    k_in = k * jnp.exp(-bcum)
    k_st = k * jnp.exp(blast - bcum)
    mask = jnp.tril(jnp.ones((C, C), dtype=bool))
    att = jnp.where(mask, jnp.einsum('bhnik,bhnjk->bhnij', q_in, k_in), 0.0)
    o_intra = jnp.einsum('bhnij,bhnjv->bhniv', att, v)
    u = jnp.einsum('bhnck,bhncv->bhnkv', k_st, v)
    g = jnp.exp(blast[:, :, :, 0])
    def step(s, inp):
        g_n, u_n = inp
        return g_n[..., None] * s + u_n, s
    s_fin, s_in = lax.scan(step, s0.astype(jnp.float32), (jnp.moveaxis(g, 2, 0), jnp.moveaxis(u, 2, 0)))
    s_in = jnp.moveaxis(s_in, 0, 2)
    o = o_intra + jnp.einsum('bhnck,bhnkv->bhncv', q_in, s_in)
    return o.reshape(B, H, L, -1), s_fin

def gla_mixer(xm, p, s0):
    w_in, w_al, b_al, norm_g, w_out = p
    B, L, _ = xm.shape
    proj = xm @ w_in
    q, k, v, g, z = jnp.split(proj, [GLA_QK, 2 * GLA_QK, 2 * GLA_QK + GLA_V, 2 * GLA_QK + 2 * GLA_V], axis=-1)
    def heads(t, d):
        return t.reshape(B, L, GLA_HEADS, d).transpose(0, 2, 1, 3).astype(jnp.float32)
    qh = heads(q, GLA_DK) * (GLA_DK ** -0.5)
    kh = heads(k, GLA_DK)
    vh = heads(v, GLA_DV)
    z = z.reshape(B, L, 2, GLA_RANK).astype(jnp.float32)
    log_a = jax.nn.log_sigmoid(jnp.einsum('bldr,drk->bldk', z, w_al.astype(jnp.float32)) + b_al.astype(jnp.float32)) / GLA_TAU
    la = log_a.reshape(B, L, 2, GLA_HEADS, GLA_DK).transpose(2, 0, 3, 1, 4)
    of, sf = gla_dir(qh, kh, vh, la[0], s0[:, 0])
    flip = lambda t: t[:, :, ::-1]
    ob, sb = gla_dir(flip(qh), flip(kh), flip(vh), flip(la[1]), s0[:, 1])
    o = (of + flip(ob)).transpose(0, 2, 1, 3)
    o = o * lax.rsqrt(jnp.mean(o * o, axis=-1, keepdims=True) + EPS)
    o = o.reshape(B, L, GLA_V) * norm_g.astype(jnp.float32)
    out = (jax.nn.silu(g.astype(jnp.float32)) * o).astype(xm.dtype) @ w_out
    return out, jnp.stack([sf, sb], axis=1)

def gla_mixer_grid(xm, p, s0, rows):
    out, st = gla_mixer(to_col_major(xm, rows), p, s0)
    return from_col_major(out, rows), st

def peer(xm, wq, k1, k2, u_tab, v_tab):
    B, L, D = xm.shape
    xt = xm.reshape(-1, D)
    T = xt.shape[0]
    q = (xt @ wq).reshape(T, PEER_HEADS, 2, PEER_HALF).astype(jnp.float32)
    s1 = jnp.einsum('thd,hnd->thn', q[:, :, 0], k1.astype(jnp.float32))
    s2 = jnp.einsum('thd,hnd->thn', q[:, :, 1], k2.astype(jnp.float32))
    v1, i1 = lax.top_k(s1, PEER_TOPK)
    v2, i2 = lax.top_k(s2, PEER_TOPK)
    cand = (v1[..., :, None] + v2[..., None, :]).reshape(T, PEER_HEADS, -1)
    cid = (i1[..., :, None] * PEER_NKEYS + i2[..., None, :]).reshape(T, PEER_HEADS, -1)
    sc, pos = lax.top_k(cand, PEER_TOPK)
    eid = jnp.take_along_axis(cid, pos, axis=-1)
    gate = jax.nn.softmax(sc, axis=-1)
    nb = T // PEER_BLOCK
    def block(args):
        xb, eb, gb = args
        ub = jnp.take(u_tab, eb, axis=0)
        act = jax.nn.gelu(jnp.einsum('td,thkd->thk', xb, ub).astype(jnp.float32))
        vb = jnp.take(v_tab, eb, axis=0)
        return jnp.einsum('thk,thkd->td', (gb * act).astype(vb.dtype), vb)
    out = lax.map(block, (xt.reshape(nb, PEER_BLOCK, D),
                          eid.reshape(nb, PEER_BLOCK, PEER_HEADS, PEER_TOPK),
                          gate.reshape(nb, PEER_BLOCK, PEER_HEADS, PEER_TOPK)))
    return out.reshape(B, L, D).astype(xm.dtype)

def setup_inputs(seed: int = 0) -> dict:
    key = jax.random.key(seed)
    ks = jax.random.split(key, 32)
    nrm = lambda k, s, sc: jax.random.normal(k, s, jnp.float32) * sc
    D = D_MODEL
    u = jax.random.uniform(ks[20], (N_RG, 2, D_RNN), jnp.float32, minval=0.9, maxval=0.999)
    s = u ** (1.0 / RG_C)
    rg_lambda = jnp.log(s) - jnp.log1p(-s)
    return {
        'x_prompt': nrm(ks[0], (BATCH, SEQ, D), 1.0),
        'x_sample': nrm(ks[1], (DEC_BATCH, DEC_SEQ, D), 1.0),
        'state_rglru': nrm(ks[2], (DEC_BATCH, N_RG, 2, D_RNN), 1.0),
        'state_gla': nrm(ks[3], (DEC_BATCH, N_GLA, 2, GLA_HEADS, GLA_DK, GLA_DV), 0.5),
        'c': nrm(ks[4], (DEC_BATCH, D), 1.0),
        'c_ctx': nrm(ks[5], (D,), 1.0),
        'norm1_g': 1.0 + nrm(ks[6], (DEPTH, D), 0.02),
        'norm2_g': 1.0 + nrm(ks[7], (DEPTH, D), 0.02),
        'ada_w': nrm(ks[8], (DEPTH, D, N_ADA * D), 0.5 * D ** -0.5),
        'ada_b': nrm(ks[9], (DEPTH, N_ADA * D), 0.02),
        'peer_wq': nrm(ks[10], (DEPTH, D, PEER_HEADS * PEER_DKEY), D ** -0.5),
        'peer_k1': nrm(ks[11], (DEPTH, PEER_HEADS, PEER_NKEYS, PEER_HALF), PEER_HALF ** -0.5),
        'peer_k2': nrm(ks[12], (DEPTH, PEER_HEADS, PEER_NKEYS, PEER_HALF), PEER_HALF ** -0.5),
        'peer_u': nrm(ks[13], (DEPTH, PEER_N, D), D ** -0.5),
        'peer_v': nrm(ks[14], (DEPTH, PEER_N, D), PEER_HEADS ** -0.5),
        'rg_w_in': nrm(ks[15], (N_RG, D, 2 * D_RNN), D ** -0.5),
        'rg_conv_w': nrm(ks[16], (N_RG, CONV_W, D_RNN), CONV_W ** -0.5),
        'rg_conv_b': nrm(ks[17], (N_RG, D_RNN), 0.02),
        'rg_wa': nrm(ks[18], (N_RG, 2, RG_BLOCKS, RG_BW, RG_BW), RG_BW ** -0.5),
        'rg_ba': nrm(ks[19], (N_RG, 2, D_RNN), 0.02),
        'rg_wi': nrm(ks[21], (N_RG, 2, RG_BLOCKS, RG_BW, RG_BW), RG_BW ** -0.5),
        'rg_bi': nrm(ks[22], (N_RG, 2, D_RNN), 0.02),
        'rg_lambda': rg_lambda,
        'rg_w_out': nrm(ks[23], (N_RG, D_RNN, D), D_RNN ** -0.5),
        'gla_w_in': nrm(ks[24], (N_GLA, D, GLA_IN), D ** -0.5),
        'gla_w_alpha': nrm(ks[25], (N_GLA, 2, GLA_RANK, GLA_QK), GLA_RANK ** -0.5),
        'gla_b_alpha': nrm(ks[26], (N_GLA, 2, GLA_QK), 0.1),
        'gla_norm_g': 1.0 + nrm(ks[27], (N_GLA, GLA_V), 0.02),
        'gla_w_out': nrm(ks[28], (N_GLA, GLA_V, D), GLA_V ** -0.5),
        'final_norm_g': 1.0 + nrm(ks[29], (D,), 0.02),
    }

def reference(x_prompt, x_sample, state_rglru, state_gla, c, c_ctx, norm1_g, norm2_g, ada_w, ada_b,
              peer_wq, peer_k1, peer_k2, peer_u, peer_v, rg_w_in, rg_conv_w, rg_conv_b, rg_wa, rg_ba,
              rg_wi, rg_bi, rg_lambda, rg_w_out, gla_w_in, gla_w_alpha, gla_b_alpha, gla_norm_g,
              gla_w_out, final_norm_g):
    bp = x_prompt.shape[0]
    rows = x_sample.shape[1] // GRID_W
    xp = x_prompt
    xs = x_sample + grid_pos_embed(rows, x_sample.shape[-1]).astype(x_sample.dtype)[None]
    rg_new = []
    gla_new = []
    for l in range(DEPTH):
        mod_p = ada_mod(c_ctx[None], ada_w[l], ada_b[l])
        mod_s = ada_mod(c, ada_w[l], ada_b[l])
        j = l // 2
        hp = pre_mod(xp, norm1_g[l], mod_p[0], mod_p[1])
        hs = pre_mod(xs, norm1_g[l], mod_s[0], mod_s[1])
        if l % 2 == 0:
            p = (rg_w_in[j], rg_conv_w[j], rg_conv_b[j], rg_wa[j], rg_ba[j], rg_wi[j], rg_bi[j],
                 rg_lambda[j], rg_w_out[j])
            op, st = rglru_mixer(hp, p, jnp.zeros((bp, 2, D_RNN), jnp.float32))
            rg_new.append(st)
            os_, _ = rglru_mixer(hs, p, state_rglru[:, j])
        else:
            p = (gla_w_in[j], gla_w_alpha[j], gla_b_alpha[j], gla_norm_g[j], gla_w_out[j])
            op, st = gla_mixer(hp, p, jnp.zeros((bp, 2, GLA_HEADS, GLA_DK, GLA_DV), jnp.float32))
            gla_new.append(st)
            os_, _ = gla_mixer_grid(hs, p, state_gla[:, j], rows)
        xp = xp + mod_p[2] * op
        xs = xs + mod_s[2] * os_
        pp = (peer_wq[l], peer_k1[l], peer_k2[l], peer_u[l], peer_v[l])
        xp = xp + mod_p[5] * peer(pre_mod(xp, norm2_g[l], mod_p[3], mod_p[4]), *pp)
        xs = xs + mod_s[5] * peer(pre_mod(xs, norm2_g[l], mod_s[3], mod_s[4]), *pp)
    y_prompt = rmsnorm(xp, final_norm_g)
    y_sample = rmsnorm(xs, final_norm_g)
    new_state_rglru = jnp.stack(rg_new, axis=1)
    new_state_gla = jnp.stack(gla_new, axis=1)
    return (y_prompt, y_sample, new_state_rglru, new_state_gla)


_drawn_inputs = setup_inputs


def setup_inputs(seed=0):
    import zlib

    import numpy as np

    out = dict(_drawn_inputs(seed))
    spreads = {}
    factors = {'state_gla': 8.0,
     'norm2_g': 4.61,
     'rg_ba': 8.0,
     'rg_bi': 7.318,
     'gla_norm_g': 8.0,
     'final_norm_g': 2.813}
    for name, (base, spread) in spreads.items():
        noise = np.random.default_rng([zlib.crc32(name.encode()), seed]).standard_normal(out[name].shape)
        drawn = base * np.exp(spread * noise) if base else spread * noise
        out[name] = __import__('jax').numpy.asarray(drawn.astype(out[name].dtype))
    for name, factor in factors.items():
        out[name] = (out[name] * factor).astype(out[name].dtype)
    return out
```

```python
from contextlib import ExitStack

import concourse.bass as bass
from concourse import mybir

P = 128
D = 1024
C = D // P
TP, TS = 128, 256
T = TP + TS
NT = T // P
DEPTH = 2
NMOD = 6
GRID_W = 64
ROWS = TS // GRID_W
EPS_COL = 0
SLABS = 4
SW = 256
PAD_L, PAD_R = 2, 1
WX = T + PAD_L + PAD_R
WPAD = WX + PAD_L + PAD_R
S0 = TP + PAD_L + PAD_R
HEADS, DK, DV = 4, 128, 256
CH = 64
NCH = T // CH
RANK = 16
TAU = 16.0
PH, NK, TOPK = 8, 128, 16
NEXP = NK * NK
NB = NT * PH
US, VS, DS = 8, 16, 8
RG_C = 8.0
GELU_C = 0.7978845608028654
AW = 3120
NEG = -3.0e38

F32 = mybir.dt.float32
U32 = mybir.dt.uint32
ALU = mybir.AluOpType
ACT = mybir.ActivationFunctionType
AX_X = mybir.AxisListType.X

V_COND, V_N1, V_N2, V_ADAB = 0, 16, 32, 48
V_CW, V_CB, V_BA, V_BI, V_LAM, V_H0, V_BAL, V_GNG, V_FG, V_EPS, V_END = (
    144, 176, 184, 200, 216, 232, 248, 256, 264, 272, 273)

STREAM = [("ada0", 24), ("rg_in", 8), ("rg_out", 4), ("wq0", 8), ("ada1", 24), ("gla_in", 12),
          ("gla_out", 4), ("wq1", 8)]
FIRST = {}
_n = 0
for _name, _k in STREAM:
    FIRST[_name] = _n
    _n += _k
FIRST_ADA = {"ada0": 0, "ada1": 24}


class Chain:

    def __init__(self, eng, sem):
        self.eng, self.sem, self.base, self.n = eng, sem, 0, 0

    def __call__(self, ins, apart=None):
        self.n += 1
        ins.then_inc(self.sem, 1)
        self.eng.wait_ge(self.sem, self.base + self.n)
        if apart:
            apart(self.eng)

    def enter(self, rounds_before, per_round):
        self.start, self.per, self.n = self.base + self.n, per_round, 0
        self.base = self.start + rounds_before * per_round

    def leave(self, rounds):
        assert self.n == self.per, (self.n, self.per)
        self.base, self.n = self.start + rounds * self.per, 0


def build(nc, x_t, pos_t, vecs, ident_d, mask_d, iota_d, keys_t, ada_w, peer_wq, peer_u, peer_v, rg_w_in,
          rg_wa, rg_wi, rg_w_out, gla_w_in, w_alpha, state_gla, gla_w_out, y_t, st_rg, st_gla):
    ctx = ExitStack()
    with ctx:
        def sb(name, shape, dt=F32):
            return ctx.enter_context(nc.sbuf_tensor(name, shape, dt))

        sems = {}

        def sem(name):
            if name not in sems:
                sems[name] = ctx.enter_context(nc.semaphore(name))
            return sems[name]

        xT = sb("xT", [P, C, T])
        slab = [sb(f"slab{i}", [P, C, SW]) for i in range(SLABS)]
        arena = sb("arena", [P, 8 * AW])
        xtok = sb("xtok", [P, NT * D])
        scores = sb("scores", [P, (NB + 2) * 2 * NK])
        keys = sb("keys", [P, 2 * PH * NK])
        vec = sb("vec", [P, V_END])
        ident = sb("ident", [P, P])
        ones = sb("ones", [P, P])
        zrow = sb("zrow", [1, 512])
        iota16 = sb("iota16", [P, TOPK])
        cond = sb("cond", [P, C, 2])
        mods = sb("mods", [P, NMOD * C, 2])
        gs = sb("gs", [P, 2, C, 2])
        sd = sb("sd", [P, T])
        rstd = sb("rstd", [P, T])
        lamv = sb("lamv", [P, 5, 2 * C])
        dec8 = sb("dec8", [P, 2 * C])
        ndec8 = sb("ndec8", [P, 2 * C])
        rgfin = sb("rgfin", [P, 2, C])
        wz = sb("wz", [P, C, 2 * RANK])
        small = sb("small", [P, 2 * T + 2 * HEADS * NCH])

        A = [arena[:, i * AW:(i + 1) * AW] for i in range(8)]

        def cols(a, n=T):
            return a[:, 0:C * n].rearrange("p (c t) -> p c t", c=C)

        hT = cols(A[0])
        gate_br = cols(A[1])
        xpad = cols(A[2], WPAD)[:, :, :]
        xr = cols(A[3], WX)
        g_r, g_i, g_a, g_b = (cols(A[i], WX) for i in (4, 5, 6, 7))
        scan_out = [cols(A[0], WX), cols(A[2], WX)]
        sq = cols(A[7])
        xn = cols(A[6])
        bd = scores[:, 0:4 * C * P].rearrange("p (k c m) -> p k c m", k=4, c=C)
        vtok = A[1][:, 0:NT * D].rearrange("p (t v) -> p t v", t=NT)
        silu_g = cols(A[2])
        qk = cols(A[3])
        la, labs, bc, qin = A[4][:, 0:C * T], A[5][:, 0:C * T], A[6][:, 0:C * T], A[7][:, 0:C * T]
        kin = scores[:, 0:C * T]
        kst = labs
        kst_tok = A[0][:, 0:C * T].rearrange("p (d t f) -> p d t f", d=2, t=NT)
        state = [A[4][:, 0:2 * NCH * DV].rearrange("p (d n v) -> p d n v", d=2, n=NCH),
                 scores[:, C * T:C * T + 2 * NCH * DV].rearrange("p (d n v) -> p d n v", d=2, n=NCH)]
        oT = cols(A[6])
        osq = cols(A[3])
        s0_all = xtok[:, 0:2 * HEADS * DV].rearrange("p (d h v) -> p d h v", d=2, h=HEADS)
        wal = xtok[0:RANK, 2 * D:3 * D].rearrange("r (d k) -> r d k", d=2)
        zT = small[0:RANK, 0:2 * T].rearrange("p (d t) -> p d t", d=2)
        gdec = small[:, 768:768 + 2 * HEADS * NCH]
        mask = keys[:, 0:8 * CH].bitcast(U32)
        attm = scores[:, 2 * C * T:2 * C * T + 8 * CH]
        att2 = keys[:, 8 * CH:8 * CH + NT * HEADS * P].rearrange("p (t h i) -> p t h i", t=NT, h=HEADS)
        ubuf = [arena[:, i * D:(i + 1) * D] for i in range(US)]
        vbuf = [arena[:, (US + i) * D:(US + i + 1) * D] for i in range(VS)]
        qT = [A[3][:, i * T:(i + 1) * T] for i in range(2)]
        diag = [keys[:, i * P:(i + 1) * P] for i in range(DS)]
        stage = sb("stage", [P, 2 * NK])
        work = sb("work", [P, 2 * NK])
        cand, cand2 = (keys[:, o:o + TOPK * TOPK] for o in (1024, 1280))
        v12 = sb("v12", [P, 2, TOPK])
        i12u = sb("i12u", [P, 2, TOPK], U32)
        i12 = sb("i12", [P, 2, TOPK])
        posu = sb("posu", [P, TOPK], U32)
        abu = sb("abu", [P, 2, TOPK], U32)
        ab = sb("ab", [P, 2, TOPK])
        onehot = keys[:, 1536:2048]
        e12 = sb("e12", [P, 2, TOPK])
        sc = [sb(f"sc{i}", [P, TOPK]) for i in range(2)]
        nmax = [sb(f"nmax{i}", [P, 1]) for i in range(2)]
        esum = [sb(f"esum{i}", [P, 1]) for i in range(2)]
        rz = [sb(f"rz{i}", [P, 1]) for i in range(2)]
        ex = [sb(f"ex{i}", [P, TOPK]) for i in range(2)]
        idx = [sb(f"idx{i}", [P, TOPK], U32) for i in range(2)]
        dots = [sb(f"dots{i}", [P, TOPK]) for i in range(2)]
        inner = [sb(f"inner{i}", [P, TOPK]) for i in range(2)]
        tanh = [sb(f"tanh{i}", [P, TOPK]) for i in range(2)]
        wts = [sb(f"wts{i}", [P, TOPK]) for i in range(2)]

        bank = [ctx.enter_context(nc.psum_tensor(f"bank{i}", [P, 512], F32)) for i in range(6)]
        acc = ctx.enter_context(nc.psum_tensor("acc", [P, D], F32))

        slab_in = [sem(f"slab_in{i}") for i in range(SLABS)]
        u_in = [sem(f"u_in{i}") for i in range(US)]
        v_in = [sem(f"v_in{i}") for i in range(VS)]
        u_free, v_free = sem("u_free"), sem("v_free")
        (vec_in, const_in, x_in, pos_in, bd_in, gla_small_in, mask_in, s0_in) = (
            sem(n) for n in ("vec_in", "const_in", "x_in", "pos_in", "bd_in", "gla_small_in", "mask_in", "s0_in"))
        keys_in = sem("keys_in")

        SEG = [(0, TP), (TP, T)]

        def slab_chunk(first, n):
            k = first + n // 2
            return k, slab[k % SLABS][:, :, (n % 2) * P:(n % 2 + 1) * P]

        def apart(eng):
            eng.sem_inc(sem("waited"), 1)

        block = ctx.enter_context(nc.Block())

        @block.sync
        def _(sp):
            def wait_used(k):
                name = max((m for m in FIRST if FIRST[m] <= k), key=FIRST.get)
                j = k - FIRST[name]
                if name.startswith("ada"):
                    sp.wait_ge(sem("ada_used"), FIRST_ADA[name] + j + 1)
                elif name.startswith("wq"):
                    sp.wait_ge(sem("q_mm"), 16 * int(name[2]) + 2 * j + 2)
                elif name != "gla_in":
                    sp.wait_ge(sem(name + "_mm"), 2 * j + 2)
                elif j < 4:
                    sp.wait_ge(sem("qk_mm"), 2 * j + 2)
                elif j < 8:
                    sp.wait_ge(sem("v_mm"), NT * (j - 3))
                else:
                    sp.wait_ge(sem("g_mm"), 2 * (j - 8) + 2)

            def load(k, src):
                sp.dma_start(slab[k % SLABS][:, :, :], src).then_inc(slab_in[k % SLABS], 16)

            def stream(name, w, width):
                src = w.rearrange("(c p) n -> p c n", p=P)
                for j in range(width // SW):
                    wait_used(FIRST[name] + j - SLABS)
                    load(FIRST[name] + j, src[:, :, j * SW:(j + 1) * SW])

            def stream_ada(layer):
                src = ada_w[layer].rearrange("(c p) n -> p c n", p=P)
                first = FIRST[f"ada{layer}"]
                for s in range(SLABS):
                    if first:
                        wait_used(first + s - SLABS)
                    load(s, src[:, :, s * SW:(s + 1) * SW])
                with sp.Fori(1, NMOD) as m:
                    for s in range(SLABS):
                        sp.wait_ge(sem("ada_used"), m * SLABS + (24 * layer + s - SLABS + 1))
                        load(s, src[:, :, bass.ds(m * D + s * SW, SW)])

            stream_ada(0)
            stream("rg_in", rg_w_in[0], 2 * D)
            stream("rg_out", rg_w_out[0], D)
            stream("wq0", peer_wq[0], 2 * D)
            sp.wait_ge(sem("rg_fin"), 1)
            sp.dma_start(st_rg, rgfin[:, :, :]).then_inc(sem("st_rg_out"), 16)
            stream_ada(1)
            stream("gla_in", gla_w_in[0, :, 0:3 * D], 3 * D)
            stream("gla_out", gla_w_out[0], D)
            for h in range(HEADS):
                sp.wait_ge(sem("gla_state"), 10 * (h + 1))
                for d in range(2):
                    sp.dma_start(st_gla[d, h], state[h % 2][:, d, d, :]).then_inc(sem(f"st_gla_out{h % 2}"), 16)
            sp.wait_ge(sem("att_used"), 1)
            sp.dma_start(keys[:, :], keys_t[:, 1, :]).then_inc(keys_in, 16)
            stream("wq1", peer_wq[1], 2 * D)
            sp.wait_ge(sem("y_ready"), 1)
            sp.dma_start(y_t, hT).then_inc(sem("y_out"), 16)
            sp.wait_ge(sem("y_out"), 16)
            sp.wait_ge(sem("st_rg_out"), 16)
            for i in range(2):
                sp.wait_ge(sem(f"st_gla_out{i}"), 16 * HEADS)

        @block.gpsimd
        def _(pool):
            pool.memset(scores[:, 0:4 * C * P], 0.0).then_inc(sem("bd_zero"), 1)
            pool.memset(ones[:, :], 1.0).then_inc(sem("ones_set"), 1)
            pool.memset(zrow[:, :], 0.0).then_inc(sem("ones_set"), 1)

            def gathers(layer):
                u_rows = peer_u.rearrange("l n d -> (l n) d")
                v_rows = peer_v.rearrange("l n d -> (l n) d")
                pool.wait_ge(sem("s_mm"), 16 * (layer + 1))
                pool.wait_ge(sem("xt_ev"), 6 * (layer + 1))
                pool.sem_inc(u_free, US)
                pool.sem_inc(v_free, VS)
                ur = layer * (US + NB * TOPK)
                vr = layer * (VS + NB * TOPK)
                with pool.Fori(0, NB // 2) as pr:
                    for par in range(2):
                        pool.wait_ge(sem("idx_ready"), pr * 2 + (layer * (NB + 1) + par + 1))
                        for j in range(TOPK):
                            pool.wait_ge(u_free, pr * (2 * TOPK) + (ur + par * TOPK + j + 1))
                            pool.sem_inc(sem("pool_waited"), 1)
                            pool.indirect_dma_start(
                                ubuf[j % US], None, u_rows,
                                bass.IndirectOffsetOnAxis(ap=idx[par][:, j:j + 1], axis=0)).then_inc(u_in[j % US], 16)
                        for j in range(TOPK):
                            pool.wait_ge(v_free, pr * (2 * TOPK) + (vr + par * TOPK + j + 1))
                            pool.sem_inc(sem("pool_waited"), 1)
                            pool.indirect_dma_start(
                                vbuf[j], None, v_rows,
                                bass.IndirectOffsetOnAxis(ap=idx[par][:, j:j + 1], axis=0)).then_inc(v_in[j], 16)

            gathers(0)
            gathers(1)

        @block.scalar
        def _(act):
            link = Chain(act, sem("act_step"))
            act.dma_start(vec[:, :], vecs).then_inc(vec_in, 16)
            act.dma_start(xT[:, :, :], x_t).then_inc(x_in, 16)
            act.dma_start(A[1][:, 0:C * TS].rearrange("p (c t) -> p c t", c=C), pos_t).then_inc(pos_in, 16)
            act.dma_start(ident[:, :], ident_d).then_inc(const_in, 16)
            act.dma_start(iota16[:, :], iota_d).then_inc(const_in, 16)
            act.dma_start(wz[:, :, :], gla_w_in[0].rearrange("(c p) n -> p c n", p=P)[:, :, 3 * D:3 * D + 2 * RANK]
                          ).then_inc(gla_small_in, 16)
            act.dma_start(keys[:, :], keys_t[:, 0, :]).then_inc(keys_in, 16)
            act.wait_ge(sem("bd_zero"), 1)
            for kind, w in enumerate((rg_wa, rg_wi)):
                for d in range(2):
                    for half in range(2):
                        act.dma_start(bd[64 * half:64 * half + 64, 2 * d + kind, :, 64 * half:64 * half + 64],
                                      w[0, d].rearrange("(c two) i j -> two i c j", two=2)[half]).then_inc(bd_in, 16)
            act.wait_ge(vec_in, 16)
            act.activation(cond[:, :, :].rearrange("p c s -> p s c"),
                           vec[:, V_COND:V_COND + 16].rearrange("p (s c) -> p s c", s=2),
                           ACT.Silu).then_inc(sem("cond_ready"), 1)
            link(act.activation(lamv[:, 0, :], vec[:, V_LAM:V_LAM + 2 * C], ACT.Abs))
            act.activation(lamv[:, 1, :], lamv[:, 0, :], ACT.Exp, scale=-1.0).then_inc(sem("lam_exp"), 1)

            def norm(n, modded=True, permuted=False):
                act.wait_ge(sem("x_ready"), n + 1)
                act.activation(sq, xT[:, :, :], ACT.Square).then_inc(sem("sq_ready"), 1)
                act.wait_ge(sem("ss_ready"), n + 1)
                act.activation(sd[:, :], bank[5][:, 0:T], ACT.Sqrt, scale=1.0 / D,
                               bias=vec[:, V_EPS:V_EPS + 1]).then_inc(sem("sd_ready"), 1)
                if not modded:
                    return
                act.wait_ge(sem("xn_ready"), n + 1)
                part = n % 2
                act.wait_ge(sem("gs_ready"), n // 2 + 1)
                for c in range(C):
                    for s, (a, b) in enumerate(SEG):
                        src, dst = xn[:, c, a:b], hT[:, c, a:b]
                        if permuted and s == 1:
                            src = src.rearrange("p (r w) -> p r w", r=ROWS)
                            dst = dst.rearrange("p (w r) -> p r w", r=ROWS)
                        act.activation(dst, src, ACT.Identity, scale=gs[:, part, c, s:s + 1],
                                       bias=mods[:, 3 * part * C + c, s:s + 1]).then_inc(sem("h_ready"), 1)

            def peer(layer):
                for g in range(6):
                    act.wait_ge(sem("xt_mm"), 6 * layer + g + 1)
                    act.activation(xtok[:, g * 512:(g + 1) * 512], bank[4 + g % 2][:, :], ACT.Copy
                                   ).then_inc(sem("xt_ev"), 1)
                for n in range(16):
                    act.wait_ge(sem("q_mm"), 16 * layer + n + 1)
                    if n >= 2:
                        act.wait_ge(sem("s_mm"), 16 * layer + n - 1)
                    act.activation(qT[n % 2], bank[n % 2][:, 0:T], ACT.Copy).then_inc(sem("q_ev"), 1)
                act.wait_ge(sem("s_ev"), 16 * (layer + 1))
                ib, vr = layer * (NB + 1), layer * (VS + NB * TOPK)

                def copy_scores(block_col):
                    act.activation(stage[:, :], scores[:, block_col], ACT.Copy).then_inc(sem("staged"), 1)

                def exps(q):
                    act.activation(ex[q][:, :], sc[q][:, :], ACT.Exp, bias=nmax[q][:, 0:1],
                                   accum_out=esum[q][:, 0:1]).then_inc(sem("exp_ready"), 1)

                copy_scores(bass.ds(0, 2 * NK))
                act.wait_ge(sem("idx_ready"), ib + 1)
                exps(0)
                copy_scores(bass.ds(2 * NK, 2 * NK))
                with act.Fori(0, NT) as t:
                    with act.Fori(0, PH // 2) as pr:
                        for par in range(2):
                            blk = t * PH + pr * 2 + par
                            act.wait_ge(sem("inner_ready"), blk + (layer * NB + 1))
                            act.activation(tanh[par][:, :], inner[par][:, :], ACT.Tanh, scale=GELU_C
                                           ).then_inc(sem("tanh_ready"), 1)
                            act.wait_ge(sem("w_ready"), blk + (layer * NB + 1))
                            for j in range(TOPK):
                                act.wait_ge(v_free, blk * TOPK + (vr + j + 1 + VS - DS))
                                act.activation(diag[j % DS][:, :], ident[:, :], ACT.Copy,
                                               scale=wts[par][:, j:j + 1]).then_inc(sem("diag_ready"), 1)
                            act.wait_ge(sem("idx_ready"), blk + (ib + 2))
                            exps(1 - par)
                            copy_scores(bass.ds(blk * (2 * NK) + 4 * NK, 2 * NK))
                    act.wait_ge(v_free, t * (PH * TOPK) + (vr + VS + PH * TOPK))
                    act.activation(xtok[:, bass.ds(t * D, D)], acc[:, :], ACT.Copy).then_inc(sem("acc_ev"), 1)

            norm(0)
            for n in range(2 * C):
                act.wait_ge(sem("rg_in_mm"), n + 1)
                if n < C:
                    act.activation(gate_br[:, n, :], bank[n % 4][:, 0:T], ACT.Gelu_apprx_tanh
                                   ).then_inc(sem("rg_in_ev"), 1)
                else:
                    if n == C:
                        act.wait_ge(sem("xpad_zero"), 1)
                    act.activation(xpad[:, n - C, PAD_L:PAD_L + TP], bank[n % 4][:, 0:TP], ACT.Copy)
                    act.activation(xpad[:, n - C, S0 + PAD_L:S0 + PAD_L + TS], bank[n % 4][:, TP:T], ACT.Copy
                                   ).then_inc(sem("rg_in_ev"), 1)
            for d in range(2):
                if d == 1:
                    act.wait_ge(sem("rg_b"), 1)
                for kind, dst, col in ((0, g_r, V_BA), (1, g_i, V_BI)):
                    for c in range(C):
                        n = (2 * d + kind) * C + c
                        act.wait_ge(sem("rg_gate_mm"), n + 1)
                        ins = act.activation(dst[:, c, :], bank[n % 4][:, 0:WX], ACT.Sigmoid,
                                             bias=vec[:, col + d * C + c:col + d * C + c + 1])
                        ins.then_inc(sem("rg_gate_ev"), 1)
                act.wait_ge(sem("rg_gate_ev"), 32 * (d + 1) // 2)
                act.wait_ge(sem("dec_ready"), 1)
                if d == 1:
                    act.wait_ge(sem("rg_scan"), 2 * C)
                for c in range(C):
                    act.activation(g_b[:, c, :], g_r[:, c, :], ACT.Tanh, scale=dec8[:, d * C + c:d * C + c + 1]
                                   ).then_inc(sem("rg_tanh"), 1)
                for c in range(C):
                    act.activation(g_a[:, c, :], g_r[:, c, :], ACT.Exp, scale=ndec8[:, d * C + c:d * C + c + 1]
                                   ).then_inc(sem("rg_a"), 1)
                act.wait_ge(sem("rg_ratio"), d + 1)
                act.activation(g_b, g_b, ACT.Sqrt, scale=2.0).then_inc(sem("rg_sqrt"), 1)
            norm(1)
            peer(0)

            act.wait_ge(sem("peer_mm"), C)
            act.dma_start(mask, mask_d).then_inc(mask_in, 16)
            act.dma_start(s0_all, state_gla.rearrange("d h k v -> k d h v")).then_inc(s0_in, 16)
            act.dma_start(wal, w_alpha[0].rearrange("d r k -> r d k")).then_inc(gla_small_in, 16)
            norm(2, permuted=True)
            for i in range(8):
                bk = (2 + i) % 4
                act.wait_ge(sem("la_mm"), i + 1)
                act.activation(la[:, i * T:(i + 1) * T], bank[bk][:, 0:T], ACT.Identity,
                               bias=vec[:, V_BAL + i:V_BAL + i + 1]).then_inc(sem("la_ev"), 1)
            act.wait_ge(sem("la_ev"), 8)
            link(act.activation(labs, la, ACT.Abs))
            link(act.activation(labs, labs, ACT.Exp, scale=-1.0))
            act.activation(labs, labs, ACT.Ln, bias=1.0).then_inc(sem("la_ln"), 1)
            for i in range(8):
                bk = (10 + i) % 4
                act.wait_ge(sem("qk_mm"), i + 1)
                act.activation(qk[:, i, :], bank[bk][:, 0:T], ACT.Copy, scale=DK ** -0.5 if i < 4 else 1.0
                               ).then_inc(sem("qk_ev"), 1)
            act.wait_ge(sem("bc_ready"), 2)
            act.activation(la, bc, ACT.Exp, scale=1.0 / TAU).then_inc(sem("gla_e"), 1)
            act.activation(kin, bc, ACT.Exp, scale=-1.0 / TAU).then_inc(sem("gla_e"), 1)
            act.wait_ge(sem("dd_ready"), 2)
            act.activation(labs, labs, ACT.Exp, scale=1.0 / TAU).then_inc(sem("gla_e"), 1)
            for d in range(2):
                last = CH - 1 if d == 0 else 0
                act.activation(gdec[:, d * 24:(d + 1) * 24],
                               bc[:, d * 1536:(d + 1) * 1536].rearrange("p (n i) -> p n i", i=CH)[:, :, last],
                               ACT.Exp, scale=1.0 / TAU).then_inc(sem("gla_e"), 1)
            for i in range(8):
                act.wait_ge(sem("g_mm"), i + 1)
                act.activation(silu_g[:, i, :], bank[(2 + i) % 4][:, 0:T], ACT.Silu).then_inc(sem("g_ev"), 1)
            for n in range(6):
                act.wait_ge(sem("kt_mm"), n + 1)
                act.activation(kst_tok[:, n // 3, n % 3, :], bank[n % 2][:, :], ACT.Copy).then_inc(sem("kt_ev"), 1)
            for h in range(HEADS):
                act.wait_ge(sem("o_mm"), h + 1)
                if h == 0:
                    act.wait_ge(sem("kst_used"), 1)
                for v2 in range(2):
                    act.activation(oT[:, 2 * h + v2, :], bank[4 + v2][:, 0:T], ACT.Copy).then_inc(sem("o_ev"), 1)
                    act.activation(osq[:, 2 * h + v2, :], bank[4 + v2][:, 0:T], ACT.Square).then_inc(sem("o_ev"), 1)
                act.wait_ge(sem("oss_mm"), h + 1)
                if h >= 1:
                    act.wait_ge(sem("o_rstd"), h)
                act.activation(sd[:, :], acc[:, 0:T], ACT.Sqrt, scale=1.0 / DV,
                               bias=vec[:, V_EPS:V_EPS + 1]).then_inc(sem("o_sd"), 1)
            norm(3)
            peer(1)
            norm(4, modded=False)

        @block.tensor
        def _(pe):
            def wait_slab(k):
                pe.wait_ge(slab_in[k % SLABS], 16 * (k // SLABS + 1))

            def ada(layer):
                first = FIRST[f"ada{layer}"]
                pe.wait_ge(sem("cond_ready"), 1)
                modps = acc[:, 0:NMOD * C * 2]
                with pe.Fori(0, NMOD) as m:
                    for s in range(SLABS):
                        pe.wait_ge(slab_in[s], m * 16 + 16 * (first // SLABS + 1))
                        for half in range(2):
                            for k in range(C):
                                mm = pe.matmul(modps[:, bass.ds(m * (2 * C) + 4 * s + 2 * half, 2)],
                                               slab[s][:, k, half * P:(half + 1) * P], cond[:, k, :],
                                               start=(k == 0), stop=(k == C - 1), skip_group_check=True)
                        mm.then_inc(sem("ada_used"), 1)

            def norm(n):
                if n == 0:
                    pe.wait_ge(sem("ones_set"), 2)
                pe.wait_ge(sem("sq_ready"), n + 1)
                for c in range(C):
                    mm = pe.matmul(bank[5][:, 0:T], ones[:, :], sq[:, c, :], start=(c == 0), stop=(c == C - 1))
                mm.then_inc(sem("ss_ready"), 1)

            def project(first, n, out, rhs, signal):
                k, w = slab_chunk(first, n)
                if n % 2 == 0:
                    wait_slab(k)
                for c in range(C):
                    mm = pe.matmul(out, w[:, c, :], rhs[:, c, :], start=(c == 0), stop=(c == C - 1))
                mm.then_inc(signal, 1)

            def routing(layer):
                pe.wait_ge(sem("h_ready"), 16 * (2 * layer + 2))
                if layer == 0:
                    pe.wait_ge(const_in, 32)
                for g in range(6):
                    if g >= 2:
                        pe.wait_ge(sem("xt_ev"), 6 * layer + g - 1)
                    elif g == 1:
                        pe.wait_ge(sem("sd_ready"), 2 * layer + 2)
                    for i in range(4):
                        mm = pe.transpose(bank[4 + g % 2][:, i * P:(i + 1) * P],
                                          hT[:, (g % 2) * 4 + i, (g // 2) * P:(g // 2 + 1) * P], ident[:, :])
                    mm.then_inc(sem("xt_mm"), 1)

                def score(n):
                    if n == 0:
                        pe.wait_ge(keys_in, 16 * (layer + 1))
                    pe.wait_ge(sem("q_ev"), 16 * layer + n + 1)
                    if n >= 2:
                        pe.wait_ge(sem("s_ev"), 16 * layer + n - 1)
                    for t in range(NT):
                        mm = pe.matmul(bank[2 + n % 2][:, t * P:(t + 1) * P], qT[n % 2][:, t * P:(t + 1) * P],
                                       keys[:, n * NK:(n + 1) * NK], start=True, stop=True)
                    mm.then_inc(sem("s_mm"), 1)

                for n in range(16):
                    if n >= 2:
                        pe.wait_ge(sem("q_ev"), 16 * layer + n - 1)
                    project(FIRST[f"wq{layer}"], n, bank[n % 2][:, 0:T], hT, sem("q_mm"))
                    if n >= 1:
                        score(n - 1)
                score(15)

            def peer(layer):
                with pe.Fori(0, NT) as t:
                    pe.wait_ge(sem("acc_ev"), t + layer * NT)
                    for half in range(2):
                        pe.matmul(acc[:, half * 512:(half + 1) * 512], zrow[0:1, 0:P], zrow[0:1, :],
                                  start=True, stop=True, skip_group_check=True)
                    with pe.Fori(0, PH // 2) as pr:
                        for par in range(2):
                            blk = t * PH + pr * 2 + par
                            for j in range(TOPK):
                                pe.wait_ge(v_in[j], blk * 16 + 16 * (layer * NB + 1))
                                pe.wait_ge(sem("diag_ready"), blk * TOPK + (layer * NB * TOPK + j + 1))
                                for half in range(2):
                                    mm = pe.matmul(acc[:, half * 512:(half + 1) * 512], diag[j % DS][:, :],
                                                   vbuf[j][:, half * 512:(half + 1) * 512], start=False, stop=True,
                                                   skip_group_check=True)
                                mm.then_inc(v_free, 1)
                pe.wait_ge(sem("acc_ev"), NT * (layer + 1))
                for c in range(C):
                    if c >= 4:
                        pe.wait_ge(sem("peer_add"), C * layer + c - 3)
                    for t in range(NT):
                        mm = pe.transpose(bank[c % 4][:, t * P:(t + 1) * P],
                                          xtok[:, t * D + c * P:t * D + (c + 1) * P], ident[:, :])
                    mm.then_inc(sem("peer_mm"), 1)

            ada(0)
            norm(0)
            pe.wait_ge(sem("h_ready"), 16)
            for n in range(2 * C):
                if n >= 4:
                    pe.wait_ge(sem("rg_in_ev"), n - 3)
                project(FIRST["rg_in"], n, bank[n % 4][:, 0:T], hT, sem("rg_in_mm"))
            pe.wait_ge(bd_in, 16 * 8)
            for d in range(2):
                for kind in range(2):
                    for c in range(C):
                        n = (2 * d + kind) * C + c
                        if n < C:
                            pe.wait_ge(sem("xr_ready"), c + 1)
                        if n >= 4:
                            pe.wait_ge(sem("rg_gate_ev"), n - 3)
                        else:
                            pe.wait_ge(sem("rg_in_ev"), 2 * C - 3 + n)
                        pe.matmul(bank[n % 4][:, 0:WX], bd[:, 2 * d + kind, c, :], xr[:, c, :], start=True,
                                  stop=True).then_inc(sem("rg_gate_mm"), 1)
            pe.wait_ge(sem("hg_ready"), 1)
            for n in range(C):
                if n >= 4:
                    pe.wait_ge(sem("rg_out_ev"), n - 3)
                project(FIRST["rg_out"], n, bank[n % 4][:, 0:T], gate_br, sem("rg_out_mm"))
            norm(1)
            routing(0)
            peer(0)

            ada(1)
            norm(2)
            pe.wait_ge(sem("h_ready"), 48)
            pe.wait_ge(gla_small_in, 32)
            for d in range(2):
                for c in range(C):
                    mm = pe.matmul(bank[d][0:RANK, 0:T], wz[:, c, d * RANK:(d + 1) * RANK], hT[:, c, :],
                                   start=(c == 0), stop=(c == C - 1))
                mm.then_inc(sem("z_mm"), 1)
            pe.wait_ge(sem("z_ev"), 2)
            for i in range(8):
                if i >= 4:
                    pe.wait_ge(sem("la_ev"), i - 3)
                pe.matmul(bank[(2 + i) % 4][:, 0:T], wal[:, i // 4, (i % 4) * DK:(i % 4 + 1) * DK],
                          zT[:, i // 4, :], start=True, stop=True).then_inc(sem("la_mm"), 1)
            for i in range(8):
                if i < 4:
                    pe.wait_ge(sem("la_ev"), i + 5)
                else:
                    pe.wait_ge(sem("qk_ev"), i - 3)
                project(FIRST["gla_in"], i, bank[(10 + i) % 4][:, 0:T], hT, sem("qk_mm"))
            for i in range(HEADS * NT):
                if i < 4:
                    pe.wait_ge(sem("qk_ev"), i + 5)
                else:
                    pe.wait_ge(sem("v_ev"), i - 3)
                k = FIRST["gla_in"] + 4 + i // NT
                t = i % NT
                if t == 0:
                    wait_slab(k)
                for c in range(C):
                    mm = pe.matmul(bank[(2 + i) % 4][:, 0:SW], hT[:, c, t * P:(t + 1) * P], slab[k % SLABS][:, c, :],
                                   start=(c == 0), stop=(c == C - 1))
                mm.then_inc(sem("v_mm"), 1)
            for i in range(8):
                if i < 4:
                    pe.wait_ge(sem("v_ev"), i + 9)
                else:
                    pe.wait_ge(sem("g_ev"), i - 3)
                project(FIRST["gla_in"] + 8, i, bank[(2 + i) % 4][:, 0:T], hT, sem("g_mm"))
            pe.wait_ge(sem("kst_ready"), 2)
            pe.wait_ge(sem("g_ev"), 8)
            for n in range(6):
                if n >= 2:
                    pe.wait_ge(sem("kt_ev"), n - 1)
                d, t = n // 3, n % 3
                for h in range(HEADS):
                    o = d * 1536 + h * T + t * P
                    mm = pe.transpose(bank[n % 2][:, h * P:(h + 1) * P], kst[:, o:o + P], ident[:, :])
                mm.then_inc(sem("kt_mm"), 1)
            pe.wait_ge(sem("qin_ready"), 2)
            pe.wait_ge(sem("kin_ready"), 2)
            for t in range(NT):
                bk = bank[2 + t % 2]
                if t >= 2:
                    pe.wait_ge(sem("att_ev"), t - 1)
                for odd in range(2):
                    for d in range(2):
                        for h in range(HEADS):
                            o = d * 1536 + h * T + t * P + odd * CH
                            mm = pe.matmul(bk[odd * CH:(odd + 1) * CH, (4 * d + h) * CH:(4 * d + h + 1) * CH],
                                           kin[:, o:o + CH], qin[:, o:o + CH], start=True, stop=True)
                mm.then_inc(sem("att_mm"), 1)
            pe.wait_ge(sem("kt_ev"), 6)
            pe.wait_ge(s0_in, 16)
            n_u = 0

            def updates(h):
                nonlocal n_u
                for d, chunks in ((0, (0, 1, 2, 3, 4)), (1, (1, 0, 5, 4, 3))):
                    for n in chunks:
                        if n_u >= 4:
                            pe.wait_ge(sem("gla_state"), n_u - 3)
                        elif n_u < 2:
                            pe.wait_ge(sem("kt_ev"), 6)
                        else:
                            pe.wait_ge(sem("att_ev"), 3)
                        r = (n % 2) * CH
                        pe.matmul(bank[n_u % 4][:, 0:DV], kst_tok[r:r + CH, d, n // 2, h * P:(h + 1) * P],
                                  vtok[r:r + CH, n // 2, h * DV:(h + 1) * DV], start=True, stop=True
                                  ).then_inc(sem("u_mm"), 1)
                        n_u += 1

            def outputs(h):
                pe.wait_ge(sem("gla_state"), 10 * (h + 1))
                if h >= 1:
                    pe.wait_ge(sem("o_ev"), 4 * h)
                st = state[h % 2]
                for v2 in range(2):
                    vs = slice(v2 * P, (v2 + 1) * P)
                    for t in range(NT):
                        terms = [(t * P, P, vtok[:, t, h * DV + v2 * P:h * DV + (v2 + 1) * P], att2[:, t, h, :])]
                        for n in (2 * t, 2 * t + 1):
                            for d in range(2):
                                o = d * 1536 + h * T + n * CH
                                if n == (2, 5)[d]:
                                    terms.append((n * CH, CH, s0_all[:, d, h, vs], qin[:, o:o + CH]))
                                elif n != d:
                                    terms.append((n * CH, CH, st[:, d, n, vs], qin[:, o:o + CH]))
                        for i, (o, width, l, r) in enumerate(terms):
                            mm = pe.matmul(bank[4 + v2][:, o:o + width], l, r, start=(i == 0),
                                           stop=(i == len(terms) - 1), skip_group_check=True)
                mm.then_inc(sem("o_mm"), 1)

            def head_norm(h):
                pe.wait_ge(sem("o_ev"), 4 * (h + 1))
                if h >= 1:
                    pe.wait_ge(sem("o_sd"), h)
                for v2 in range(2):
                    mm = pe.matmul(acc[:, 0:T], ones[:, :], osq[:, 2 * h + v2, :], start=(v2 == 0), stop=(v2 == 1))
                mm.then_inc(sem("oss_mm"), 1)

            updates(0)
            for h in range(HEADS):
                outputs(h)
                if h + 1 < HEADS:
                    updates(h + 1)
                head_norm(h)
            pe.wait_ge(sem("og_ready"), HEADS)
            for n in range(C):
                if n >= 4:
                    pe.wait_ge(sem("gla_out_ev"), n - 3)
                project(FIRST["gla_out"], n, bank[n % 4][:, 0:T], oT, sem("gla_out_mm"))
            norm(3)
            routing(1)
            peer(1)
            norm(4)

        @block.vector
        def _(dve):
            link = Chain(dve, sem("dve_step"))

            dve.wait_ge(sem("lam_exp"), 1)
            e, den, w, w2, s = (lamv[:, i, :] for i in (1, 2, 3, 4, 0))
            link(dve.tensor_scalar(den, e, 2.0, None, ALU.add))
            link(dve.reciprocal(den, den))
            link(dve.tensor_tensor(w, e, den, ALU.mult))
            link(dve.tensor_tensor(w2, w, w, ALU.mult))
            link(dve.tensor_scalar(s, w2, 1.0 / 17, 1.0 / 15, ALU.mult, ALU.add))
            for k in (13, 11, 9, 7, 5, 3, 1):
                link(dve.tensor_tensor(s, s, w2, ALU.mult))
                link(dve.tensor_scalar(s, s, 1.0 / k, None, ALU.add))
            link(dve.tensor_tensor(s, s, w, ALU.mult))
            link(dve.tensor_scalar(den, vec[:, V_LAM:V_LAM + 2 * C], -1.0, 0.0, ALU.mult, ALU.max))
            link(dve.scalar_tensor_tensor(s, s, 2.0, den, ALU.mult, ALU.add))
            dve.tensor_scalar(ndec8[:, :], s, -RG_C, None, ALU.mult)
            dve.tensor_scalar(dec8[:, :], s, RG_C, None, ALU.mult).then_inc(sem("dec_ready"), 1)

            dve.wait_ge(x_in, 16)
            dve.wait_ge(pos_in, 16)
            dve.tensor_tensor(xT[:, :, TP:T], xT[:, :, TP:T], A[1][:, 0:C * TS].rearrange("p (c t) -> p c t", c=C),
                              ALU.add).then_inc(sem("x_ready"), 1)

            def ada(layer):
                dve.wait_ge(sem("ada_used"), 24 * (layer + 1))
                b = vec[:, V_ADAB + layer * 48:V_ADAB + (layer + 1) * 48]
                link(dve.tensor_tensor(mods[:, :, :], acc[:, 0:96].rearrange("p (m s) -> p m s", s=2),
                                       b.unsqueeze(2).to_broadcast([P, 48, 2]), ALU.add))
                for part, col in ((0, V_N1), (1, V_N2)):
                    g = vec[:, col + layer * C:col + (layer + 1) * C].unsqueeze(2).to_broadcast([P, C, 2])
                    r = (1 + 3 * part) * C
                    ins = dve.scalar_tensor_tensor(gs[:, part, :, :], mods[:, r:r + C, :], 1.0, g, ALU.add, ALU.mult)
                ins.then_inc(sem("gs_ready"), 1)

            def norm(n, final=False):
                dve.wait_ge(sem("sd_ready"), n + 1)
                link(dve.reciprocal(rstd[:, :], sd[:, :]))
                ins = dve.tensor_tensor(xn, xT[:, :, :], rstd[:, :].unsqueeze(1).to_broadcast([P, C, T]), ALU.mult)
                if final:
                    link(ins)
                    ins = dve.tensor_tensor(hT, xn, vec[:, V_FG:V_FG + C].unsqueeze(2).to_broadcast([P, C, T]),
                                            ALU.mult)
                    ins.then_inc(sem("y_ready"), 1)
                else:
                    ins.then_inc(sem("xn_ready"), 1)

            def top16(vals, spare, out_v, out_i):
                link(dve.max(out_v[:, 0:8], vals), apart)
                dve.max_index(out_i[:, 0:8], out_v[:, 0:8], vals)
                link(dve.match_replace(spare, out_v[:, 0:8], vals, NEG), apart)
                link(dve.max(out_v[:, 8:16], spare), apart)
                return dve.max_index(out_i[:, 8:16], out_v[:, 8:16], spare)

            def choose(layer, q, staged_at, before=None):
                dve.wait_ge(sem("staged"), staged_at)
                apart(dve)
                for half in range(2):
                    r = slice(half * NK, (half + 1) * NK)
                    link(top16(stage[:, r], work[:, r], v12[:, half, :], i12u[:, half, :]), apart)
                link(dve.tensor_tensor(cand[:, :].rearrange("p (a b) -> p a b", a=TOPK),
                                       v12[:, 0, :].unsqueeze(2).to_broadcast([P, TOPK, TOPK]),
                                       v12[:, 1, :].unsqueeze(1).to_broadcast([P, TOPK, TOPK]), ALU.add))
                dve.tensor_scalar(i12[:, 0, :], i12u[:, 0, :], float(NK * layer), None, ALU.add)
                dve.tensor_copy(i12[:, 1, :], i12u[:, 1, :])
                link(top16(cand[:, :], cand2[:, :], sc[q], posu))
                dve.tensor_scalar(nmax[q][:, :], sc[q][:, 0:1], -1.0, None, ALU.mult)
                dve.tensor_scalar(abu[:, 0, :], posu[:, :], 4, None, ALU.logical_shift_right)
                link(dve.tensor_scalar(abu[:, 1, :], posu[:, :], 15, None, ALU.bitwise_and))
                link(dve.tensor_copy(ab[:, :, :], abu[:, :, :]))
                oh = onehot[:, :].rearrange("p (h j a) -> p h j a", h=2, j=TOPK)
                link(dve.tensor_tensor(oh, ab[:, :, :].unsqueeze(3).to_broadcast([P, 2, TOPK, TOPK]),
                                       iota16[:, :].unsqueeze(1).unsqueeze(1).to_broadcast([P, 2, TOPK, TOPK]),
                                       ALU.is_equal))
                link(dve.tensor_tensor(oh, oh, i12[:, :, :].unsqueeze(2).to_broadcast([P, 2, TOPK, TOPK]), ALU.mult))
                link(dve.tensor_reduce(e12[:, :, :], oh, AX_X, ALU.add))
                if before is not None:
                    for j in range(VS):
                        dve.wait_ge(v_in[j], before)
                dve.scalar_tensor_tensor(idx[q][:, :], e12[:, 0, :], float(NK), e12[:, 1, :], ALU.mult, ALU.add
                                         ).then_inc(sem("idx_ready"), 1)

            CHOOSE = 18

            def residual_peer(layer):
                for c in range(C):
                    dve.wait_ge(sem("peer_mm"), C * layer + c + 1)
                    for sgm, (a, b) in enumerate(SEG):
                        ins = dve.scalar_tensor_tensor(xT[:, c, a:b], bank[c % 4][:, a:b],
                                                       mods[:, 5 * C + c, sgm:sgm + 1], xT[:, c, a:b],
                                                       ALU.mult, ALU.add)
                    ins.then_inc(sem("peer_add"), 1)
                dve.wait_ge(sem("peer_add"), C * (layer + 1))
                dve.memset(work[:, 0:1], 0.0).then_inc(sem("x_ready"), 1)

            def peer(layer):
                for n in range(16):
                    dve.wait_ge(sem("s_mm"), 16 * layer + n + 1)
                    dve.tensor_copy(scores[:, 0:NB * 2 * NK].rearrange("p (t n k) -> p t n k", t=NT, n=16)[:, :, n, :],
                                    bank[2 + n % 2][:, 0:NT * P].rearrange("p (t k) -> p t k", t=NT)
                                    ).then_inc(sem("s_ev"), 1)
                    if n == 0:
                        dve.memset(scores[:, NB * 2 * NK:], 0.0)
                ub, sb_ = layer * (US + NB * TOPK), layer * (NB + 2)
                choose(layer, 0, sb_ + 1)
                with dve.Fori(0, NT) as t:
                    with dve.Fori(0, PH // 2) as pr:
                        link.enter(t * (PH // 2) + pr, 2 * (CHOOSE + 6))
                        for par in range(2):
                            blk = t * PH + pr * 2 + par
                            for j in range(TOPK):
                                dve.wait_ge(u_in[j % US], blk * 32 + 16 * (layer * 2 * NB + j // US + 1))
                                dve.scalar_tensor_tensor(ubuf[j % US], ubuf[j % US], 1.0, xtok[:, bass.ds(t * D, D)],
                                                         ALU.mult, ALU.mult, accum_out=dots[par][:, j:j + 1]
                                                         ).then_inc(u_free, 1)
                            dve.wait_ge(u_free, blk * TOPK + (ub + US + TOPK))
                            link(dve.tensor_tensor(inner[par][:, :], dots[par][:, :], dots[par][:, :], ALU.mult))
                            link(dve.tensor_scalar(inner[par][:, :], inner[par][:, :], 0.044715, 1.0, ALU.mult,
                                                   ALU.add))
                            dve.tensor_tensor(inner[par][:, :], inner[par][:, :], dots[par][:, :], ALU.mult
                                              ).then_inc(sem("inner_ready"), 1)
                            dve.wait_ge(sem("exp_ready"), blk + (layer * (NB + 1) + 1))
                            link(dve.reciprocal(rz[par][:, :], esum[par][:, :]))
                            link(dve.tensor_scalar(ex[par][:, :], ex[par][:, :], rz[par][:, 0:1], 0.5, ALU.mult,
                                                   ALU.mult))
                            link(dve.tensor_tensor(ex[par][:, :], ex[par][:, :], dots[par][:, :], ALU.mult))
                            dve.wait_ge(sem("tanh_ready"), blk + (layer * NB + 1))
                            dve.wait_ge(sem("diag_ready"), blk * TOPK + layer * NB * TOPK)
                            link(dve.scalar_tensor_tensor(wts[par][:, :], tanh[par][:, :], 1.0, ex[par][:, :],
                                                          ALU.add, ALU.mult))
                            dve.memset(rz[par][:, :], 0.0).then_inc(sem("w_ready"), 1)
                            choose(layer, 1 - par, blk + (sb_ + 2), before=blk * 16 + layer * NB * 16)
                        link.leave(NB // 2)
                residual_peer(layer)

            ada(0)
            norm(0)
            dve.memset(A[2][:, 0:C * WPAD], 0.0).then_inc(sem("xpad_zero"), 1)
            for c in range(C):
                dve.wait_ge(sem("rg_in_ev"), C + c + 1)
                cw = [vec[:, V_CW + c * 4 + j:V_CW + c * 4 + j + 1] for j in range(4)]
                link(dve.tensor_scalar(xr[:, c, :], xpad[:, c, 0:WX], cw[0], vec[:, V_CB + c:V_CB + c + 1], ALU.mult,
                                       ALU.add))
                for j in range(1, 4):
                    ins = dve.scalar_tensor_tensor(xr[:, c, :], xpad[:, c, j:j + WX], cw[j], xr[:, c, :], ALU.mult,
                                                   ALU.add)
                    if j < 3:
                        link(ins)
                ins.then_inc(sem("xr_ready"), 1)
            for d in range(2):
                dve.wait_ge(sem("rg_tanh"), C * (d + 1))
                out = scan_out[d]
                link(dve.tensor_scalar(out, g_b, 1.0, None, ALU.add))
                link(dve.reciprocal(out, out))
                dve.tensor_tensor(g_b, g_b, out, ALU.mult).then_inc(sem("rg_ratio"), 1)
                dve.wait_ge(sem("rg_gate_ev"), 16 * (d + 1))
                link(dve.tensor_tensor(g_i, g_i, xr, ALU.mult))
                dve.wait_ge(sem("rg_sqrt"), d + 1)
                dve.wait_ge(sem("rg_a"), C * (d + 1))
                ins = dve.tensor_tensor(g_b, g_b, g_i, ALU.mult)
                ins.then_inc(sem("rg_b"), 1)
                dve.wait_ge(sem("rg_b"), d + 1)
                for c in range(C):
                    for s_, (a, b) in enumerate(((0, TP), (S0, WX))):
                        w_ = slice(a, b) if d == 0 else (slice(b - 1, a - 1, -1) if a else slice(b - 1, None, -1))
                        h0 = vec[:, V_H0 + d * C + c:V_H0 + d * C + c + 1] if s_ else 0.0
                        dve.tensor_tensor_scan(out[:, c, w_], g_a[:, c, w_], g_b[:, c, w_], h0, ALU.mult, ALU.add
                                               ).then_inc(sem("rg_scan"), 1)
            dve.wait_ge(sem("rg_scan"), 4 * C)
            dve.tensor_copy(rgfin[:, 0, :], scan_out[0][:, :, TP - 1])
            link(dve.tensor_copy(rgfin[:, 1, :], scan_out[1][:, :, 0]))
            link(dve.tensor_tensor(scan_out[0], scan_out[0], scan_out[1], ALU.add))
            dve.memset(work[:, 0:1], 0.0).then_inc(sem("rg_fin"), 1)
            link(dve.tensor_tensor(gate_br[:, :, 0:TP], gate_br[:, :, 0:TP], scan_out[0][:, :, 0:TP], ALU.mult))
            dve.tensor_tensor(gate_br[:, :, TP:T], gate_br[:, :, TP:T], scan_out[0][:, :, S0:WX], ALU.mult
                              ).then_inc(sem("hg_ready"), 1)
            for c in range(C):
                dve.wait_ge(sem("rg_out_mm"), c + 1)
                for s_, (a, b) in enumerate(SEG):
                    ins = dve.scalar_tensor_tensor(xT[:, c, a:b], bank[c % 4][:, a:b], mods[:, 2 * C + c, s_:s_ + 1],
                                                   xT[:, c, a:b], ALU.mult, ALU.add)
                ins.then_inc(sem("rg_out_ev"), 1)
            dve.wait_ge(sem("rg_out_ev"), C)
            dve.memset(work[:, 0:1], 0.0).then_inc(sem("x_ready"), 1)
            norm(1)
            peer(0)

            ada(1)
            norm(2)
            for d in range(2):
                dve.wait_ge(sem("z_mm"), d + 1)
                dve.tensor_copy(zT[:, d, :], bank[d][0:RANK, 0:T]).then_inc(sem("z_ev"), 1)
            keep = qin
            link(dve.memset(keep, 1.0))
            for d, col in ((0, 0), (1, CH - 1)):
                ins = dve.memset(keep[:, d * 1536:(d + 1) * 1536].rearrange("p (n i) -> p n i", i=CH)[:, :, col:col + 1],
                                 0.0)
            link(ins)
            dve.wait_ge(sem("la_ln"), 1)
            link(dve.scalar_tensor_tensor(la, la, 0.0, labs, ALU.min, ALU.subtract))
            dve.tensor_tensor_scan(bc[:, 0:1536], keep[:, 0:1536], la[:, 0:1536], 0.0, ALU.mult, ALU.add
                                   ).then_inc(sem("bc_ready"), 1)
            dve.tensor_tensor_scan(bc[:, 3071:1535:-1], keep[:, 3071:1535:-1], la[:, 3071:1535:-1], 0.0, ALU.mult,
                                   ALU.add).then_inc(sem("bc_ready"), 1)
            dve.wait_ge(sem("bc_ready"), 2)
            for d in range(2):
                b3 = bc[:, d * 1536:(d + 1) * 1536].rearrange("p (n i) -> p n i", i=CH)
                last = CH - 1 if d == 0 else 0
                dve.tensor_tensor(labs[:, d * 1536:(d + 1) * 1536].rearrange("p (n i) -> p n i", i=CH),
                                  b3[:, :, last:last + 1].to_broadcast([P, 24, CH]), b3, ALU.subtract
                                  ).then_inc(sem("dd_ready"), 1)
            for i in range(HEADS * NT):
                dve.wait_ge(sem("v_mm"), i + 1)
                h, t = i // NT, i % NT
                dve.tensor_copy(vtok[:, t, h * DV:(h + 1) * DV], bank[(2 + i) % 4][:, 0:DV]).then_inc(sem("v_ev"), 1)
            dve.wait_ge(sem("qk_ev"), 8)
            qv = A[3][:, 0:1536]
            kv = A[3][:, 1536:3072]
            halves = [slice(0, 1536), slice(1536, 3072)]
            dve.wait_ge(sem("gla_e"), 3)
            for d in range(2):
                dve.tensor_tensor(kst[:, halves[d]], kst[:, halves[d]], kv, ALU.mult).then_inc(sem("kst_ready"), 1)
            for d in range(2):
                dve.tensor_tensor(kin[:, halves[d]], kin[:, halves[d]], kv, ALU.mult).then_inc(sem("kin_ready"), 1)
            for d in range(2):
                dve.tensor_tensor(qin[:, halves[d]], la[:, halves[d]], qv, ALU.mult).then_inc(sem("qin_ready"), 1)
            dve.wait_ge(sem("gla_e"), 5)
            dve.wait_ge(sem("qin_ready"), 2)
            dve.wait_ge(sem("kin_ready"), 2)
            dve.wait_ge(sem("kst_ready"), 2)
            dve.memset(work[:, 0:1], 0.0).then_inc(sem("kst_used"), 1)
            link(dve.memset(att2, 0.0))
            dve.wait_ge(mask_in, 16)
            for t in range(NT):
                dve.wait_ge(sem("att_mm"), t + 1)
                link(dve.memset(attm, 0.0))
                link(dve.copy_predicated(attm, mask, bank[2 + t % 2][:, :]))
                for r in (0, CH):
                    link(dve.tensor_tensor(att2[r:r + CH, t, :, r:r + CH],
                                           attm[r:r + CH, 0:256].rearrange("p (h i) -> p h i", h=HEADS),
                                           attm[r:r + CH, 256:512].rearrange("p (h i) -> p h i", h=HEADS), ALU.add))
                dve.memset(work[:, 0:1], 0.0).then_inc(sem("att_ev"), 1)
            dve.wait_ge(s0_in, 16)
            n_u = 0

            def states(h):
                nonlocal n_u
                st = state[h % 2]
                if h >= 2:
                    dve.wait_ge(sem("o_mm"), h - 1)
                    dve.wait_ge(sem(f"st_gla_out{h % 2}"), 32 * (h // 2))
                for d, chunks in ((0, (0, 1, 2, 3, 4)), (1, (1, 0, 5, 4, 3))):
                    for i, n in enumerate(chunks):
                        nxt = (n + 1 if d == 0 else n - 1) if i != 1 else d
                        prev = s0_all[:, d, h, :] if i == 2 else st[:, d, n, :]
                        dve.wait_ge(sem("u_mm"), n_u + 1)
                        u = bank[n_u % 4][:, 0:DV]
                        if i == 0:
                            ins = dve.tensor_copy(st[:, d, nxt, :], u)
                        else:
                            g = gdec[:, d * 24 + h * NCH + n:d * 24 + h * NCH + n + 1]
                            ins = dve.scalar_tensor_tensor(st[:, d, nxt, :], prev, g, u, ALU.mult, ALU.add)
                        ins.then_inc(sem("gla_state"), 1)
                        n_u += 1
                        dve.wait_ge(sem("gla_state"), n_u)

            states(0)
            for h in range(HEADS):
                if h + 1 < HEADS:
                    states(h + 1)
                dve.wait_ge(sem("o_sd"), h + 1)
                link(dve.reciprocal(rstd[:, :], sd[:, :]))
                dve.memset(work[:, 0:1], 0.0).then_inc(sem("o_rstd"), 1)
                for v2 in range(2):
                    c = 2 * h + v2
                    link(dve.scalar_tensor_tensor(oT[:, c, :], oT[:, c, :], vec[:, V_GNG + c:V_GNG + c + 1],
                                                  rstd[:, :], ALU.mult, ALU.mult))
                    ins = dve.tensor_tensor(oT[:, c, :], oT[:, c, :], silu_g[:, c, :], ALU.mult)
                ins.then_inc(sem("og_ready"), 1)
                if h == HEADS - 1:
                    dve.wait_ge(sem("og_ready"), HEADS)
                    dve.memset(work[:, 0:1], 0.0).then_inc(sem("att_used"), 1)
            for c in range(C):
                dve.wait_ge(sem("gla_out_mm"), c + 1)
                dve.scalar_tensor_tensor(xT[:, c, 0:TP], bank[c % 4][:, 0:TP], mods[:, 2 * C + c, 0:1],
                                         xT[:, c, 0:TP], ALU.mult, ALU.add)
                xs = xT[:, c, TP:T].rearrange("p (r w) -> p r w", r=ROWS)
                dve.scalar_tensor_tensor(xs, bank[c % 4][:, TP:T].rearrange("p (w r) -> p r w", r=ROWS),
                                         mods[:, 2 * C + c, 1:2], xs, ALU.mult, ALU.add
                                         ).then_inc(sem("gla_out_ev"), 1)
            dve.wait_ge(sem("gla_out_ev"), C)
            dve.memset(work[:, 0:1], 0.0).then_inc(sem("x_ready"), 1)
            norm(3)
            peer(1)
            norm(4, final=True)


def kernel(**inputs):
    import numpy as np
    import concourse.bacc as bacc
    from concourse import mybir as mb
    from concourse.bass_utils import run_bass_kernel_spmd as run

    a = {k: np.asarray(v) for k, v in inputs.items()}

    def feat(v):
        v = v.reshape(-1, C, P)
        return v.transpose(2, 0, 1).reshape(P, -1)

    f = np.float32
    tt = np.arange(TS)
    nf = D // 4
    freq = (f(1.0) / (f(10000.0) ** (np.arange(nf, dtype=f) / f(nf)))).astype(f)
    ar = (tt // GRID_W).astype(f)[:, None] * freq
    ac = (tt % GRID_W).astype(f)[:, None] * freq
    pos = np.concatenate([np.sin(ar), np.cos(ar), np.sin(ac), np.cos(ac)], axis=-1).astype(f)

    def to_feat(x):
        return np.ascontiguousarray(x.T.reshape(C, P, -1).transpose(1, 0, 2))

    x = np.concatenate([a["x_prompt"][0], a["x_sample"][0]], axis=0)
    vecs = np.zeros((P, V_END), f)
    vecs[:, V_COND:V_COND + 8] = feat(a["c_ctx"])
    vecs[:, V_COND + 8:V_COND + 16] = feat(a["c"])
    vecs[:, V_N1:V_N1 + 16] = feat(a["norm1_g"])
    vecs[:, V_N2:V_N2 + 16] = feat(a["norm2_g"])
    vecs[:, V_ADAB:V_ADAB + 96] = feat(a["ada_b"])
    vecs[:, V_CW:V_CW + 32] = a["rg_conv_w"][0].reshape(4, C, P).transpose(2, 1, 0).reshape(P, 32)
    vecs[:, V_CB:V_CB + 8] = feat(a["rg_conv_b"])
    vecs[:, V_BA:V_BA + 16] = feat(a["rg_ba"][0])
    vecs[:, V_BI:V_BI + 16] = feat(a["rg_bi"][0])
    vecs[:, V_LAM:V_LAM + 16] = feat(a["rg_lambda"][0])
    vecs[:, V_H0:V_H0 + 16] = feat(a["state_rglru"][0, 0])
    vecs[:, V_BAL:V_BAL + 8] = a["gla_b_alpha"][0].reshape(8, P).T
    vecs[:, V_GNG:V_GNG + 8] = feat(a["gla_norm_g"])
    vecs[:, V_FG:V_FG + 8] = feat(a["final_norm_g"])
    vecs[:, V_EPS] = 1e-6
    keys = np.stack([a["peer_k1"], a["peer_k2"]], axis=2)
    keys = np.ascontiguousarray(keys.transpose(4, 0, 1, 2, 3).reshape(P, DEPTH, 2 * PH * NK))
    j, i = np.arange(P)[:, None] % CH, np.arange(CH)[None, :]
    mask = np.concatenate([np.tile(j <= i, (1, HEADS)), np.tile(j >= i, (1, HEADS))], axis=1).astype(np.uint32)
    arrays = {
        "x_t": to_feat(x), "pos_t": to_feat(pos), "vecs": vecs, "ident": np.eye(P, dtype=f), "mask": mask,
        "iota": np.tile(np.arange(TOPK, dtype=f), (P, 1)), "keys_t": keys,
        "ada_w": a["ada_w"], "peer_wq": a["peer_wq"], "peer_u": a["peer_u"], "peer_v": a["peer_v"],
        "rg_w_in": a["rg_w_in"], "rg_wa": a["rg_wa"], "rg_wi": a["rg_wi"], "rg_w_out": a["rg_w_out"],
        "gla_w_in": a["gla_w_in"], "w_alpha": a["gla_w_alpha"], "state_gla": a["state_gla"][0, 0],
        "gla_w_out": a["gla_w_out"],
    }
    arrays = {k: np.ascontiguousarray(v) for k, v in arrays.items()}
    nc = bacc.Bacc("TRN2", target_bir_lowering=False, num_devices=1)
    ins = [nc.dram_tensor("in_" + k, v.shape, mb.dt.from_np(v.dtype), kind="ExternalInput").ap() for k, v in arrays.items()]
    outs = [nc.dram_tensor("out_" + k, s, mb.dt.float32, kind="ExternalOutput").ap() for k, s in (
        ("y_t", (P, C, T)), ("st_rg", (P, 2, C)), ("st_gla", (2, HEADS, DK, DV)))]
    build(nc, *ins, *outs)
    r = run(nc, [{"in_" + k: v for k, v in arrays.items()}], core_ids=[0]).results[0]
    y = np.asarray(r["out_y_t"]).transpose(2, 1, 0).reshape(T, D)
    st_rg = np.asarray(r["out_st_rg"]).transpose(1, 2, 0).reshape(1, 1, 2, D)
    st_gla = np.asarray(r["out_st_gla"]).reshape(1, 1, 2, HEADS, DK, DV)
    return (np.ascontiguousarray(y[None, :TP]), np.ascontiguousarray(y[None, TP:]),
            np.ascontiguousarray(st_rg), np.ascontiguousarray(st_gla))
```

```python
from contextlib import ExitStack

import concourse.bass as bass
from concourse import mybir

P = 128
D = 1024
C = D // P
TP, TS = 128, 256
T = TP + TS
NT = T // P
DEPTH = 2
NMOD = 6
GRID_W = 64
ROWS = TS // GRID_W
EPS_COL = 0
SLABS = 4
SW = 256
PAD_L, PAD_R = 2, 1
WX = T + PAD_L + PAD_R
WPAD = WX + PAD_L + PAD_R
S0 = TP + PAD_L + PAD_R
HEADS, DK, DV = 4, 128, 256
CH = 64
NCH = T // CH
RANK = 16
TAU = 16.0
PH, NK, TOPK = 8, 128, 16
NEXP = NK * NK
NB = NT * PH
US, VS, DS = 8, 16, 8
RG_C = 8.0
GELU_C = 0.7978845608028654
AW = 3120
NEG = -3.0e38

F32 = mybir.dt.float32
U32 = mybir.dt.uint32
ALU = mybir.AluOpType
ACT = mybir.ActivationFunctionType
AX_X = mybir.AxisListType.X

V_COND, V_N1, V_N2, V_ADAB = 0, 16, 32, 48
V_CW, V_CB, V_BA, V_BI, V_LAM, V_H0, V_BAL, V_GNG, V_FG, V_EPS, V_END = (
    144, 176, 184, 200, 216, 232, 248, 256, 264, 272, 273)

STREAM = [("ada0", 24), ("rg_in", 8), ("ada1", 24), ("rg_out", 4), ("gla_in", 12), ("gla_out", 4)]
FIRST = {}
_n = 0
for _name, _k in STREAM:
    FIRST[_name] = _n
    _n += _k
FIRST_ADA = {"ada0": 0, "ada1": 24}


class Chain:

    def __init__(self, eng, sem):
        self.eng, self.sem, self.base, self.n = eng, sem, 0, 0

    def __call__(self, ins, apart=None):
        self.n += 1
        ins.then_inc(self.sem, 1)
        self.eng.wait_ge(self.sem, self.base + self.n)
        if apart:
            apart(self.eng)

    def enter(self, rounds_before, per_round):
        self.start, self.per, self.n = self.base + self.n, per_round, 0
        self.base = self.start + rounds_before * per_round

    def leave(self, rounds):
        assert self.n == self.per, (self.n, self.per)
        self.base, self.n = self.start + rounds * self.per, 0


def build(nc, x_t, pos_t, vecs, ident_d, mask_d, iota_d, keys_t, ada_w, peer_wq, peer_u, peer_v, rg_w_in,
          rg_wa, rg_wi, rg_w_out, gla_w_in, w_alpha, state_gla, gla_w_out, y_t, st_rg, st_gla):
    ctx = ExitStack()
    with ctx:
        def sb(name, shape, dt=F32):
            return ctx.enter_context(nc.sbuf_tensor(name, shape, dt))

        sems = {}

        def sem(name):
            if name not in sems:
                sems[name] = ctx.enter_context(nc.semaphore(name))
            return sems[name]

        xT = sb("xT", [P, C, T])
        slab = [sb(f"slab{i}", [P, C, SW]) for i in range(SLABS)]
        arena = sb("arena", [P, 8 * AW])
        xtok = sb("xtok", [P, C * WX])
        area = sb("area", [P, 6656])
        keys = sb("keys", [P, 2 * PH * NK])
        vec = sb("vec", [P, V_END])
        ident = sb("ident", [P, P])
        ones = sb("ones", [P, P])
        zrow = sb("zrow", [1, P])
        iota16 = sb("iota16", [P, TOPK])
        cond = sb("cond", [P, C, 2])
        mods_of = [sb(f"mods{i}", [P, NMOD * C, 2]) for i in range(DEPTH)]
        gs_of = [sb(f"gs{i}", [P, 2, C, 2]) for i in range(DEPTH)]
        sd = sb("sd", [P, T])
        rstd = sb("rstd", [P, T])
        lamv = sb("lamv", [P, 5, 2 * C])
        dec4 = sb("dec4", [P, 2 * C])
        ndec8 = sb("ndec8", [P, 2 * C])
        rgfin = sb("rgfin", [P, 2, C])
        wz = sb("wz", [P, C, 2 * RANK])
        small = sb("small", [P, 2 * T + 2 * HEADS * NCH])

        A = [arena[:, i * AW:(i + 1) * AW] for i in range(8)]

        def cols(a, n=T):
            return a[:, 0:C * n].rearrange("p (c t) -> p c t", c=C)

        hT = cols(A[0])
        gate_br = cols(A[1])
        xpad = cols(A[2], WPAD)[:, :, :]
        xr = cols(A[3], WX)
        g_a = [cols(A[4], WX), cols(A[7], WX)]
        g_i = [cols(A[5], WX), cols(xtok, WX)]
        g_b = [cols(A[6], WX), cols(A[2], WX)]
        sq = cols(A[7])
        xn = cols(A[6])
        ada_rows = A[4][:, 0:NMOD * SW]
        bd = area[:, 0:4 * C * P].rearrange("p (k c m) -> p k c m", k=4, c=C)
        vtok = A[1][:, 0:NT * D].rearrange("p (t v) -> p t v", t=NT)
        silu_g = cols(A[2])
        qk = cols(A[3])
        la, labs, bc, qin = A[4][:, 0:C * T], A[5][:, 0:C * T], A[6][:, 0:C * T], A[7][:, 0:C * T]
        kin = area[:, 0:C * T]
        kst = labs
        kst_tok = A[0][:, 0:C * T].rearrange("p (d t f) -> p d t f", d=2, t=NT)
        state = [A[4][:, 0:2 * NCH * DV].rearrange("p (d n v) -> p d n v", d=2, n=NCH),
                 area[:, C * T:C * T + 2 * NCH * DV].rearrange("p (d n v) -> p d n v", d=2, n=NCH)]
        oT = cols(A[6])
        osq = cols(A[3])
        s0_all = xtok[:, 0:2 * HEADS * DV].rearrange("p (d h v) -> p d h v", d=2, h=HEADS)
        wal = xtok[0:2 * RANK, 2 * D:3 * D].rearrange("r (d k) -> r d k", d=2)
        zT = small[0:2 * RANK, 0:T]
        gdec = small[:, 768:768 + 2 * HEADS * NCH]
        mask = keys[:, 0:8 * CH].bitcast(U32)
        attm = area[:, 2 * C * T:2 * C * T + 8 * CH]
        att2 = keys[:, 8 * CH:8 * CH + NT * HEADS * P].rearrange("p (t h i) -> p t h i", t=NT, h=HEADS)
        ubuf = [arena[:, i * D:(i + 1) * D] for i in range(US)]
        vbuf = [arena[:, (US + i) * D:(US + i + 1) * D] for i in range(VS)]
        hP = cols(area)
        score_sb = area[:, C * T:C * T + NT * 2 * NK].rearrange("p (t n k) -> p t n k", t=NT, n=2)
        wq_slab = area[:, 3840:3840 + C * SW].rearrange("p (c n) -> p c n", c=C)
        qT = [area[:, 5888 + i * T:5888 + (i + 1) * T] for i in range(2)]
        diag = [sb(f"diag{i}", [P, P]) for i in range(DS)]
        work = sb("work", [P, 2 * NK])
        cand, cand2 = sd[:, 0:TOPK * TOPK], rstd[:, 0:TOPK * TOPK]
        v12 = sb("v12", [P, 2, TOPK])
        i12u = sb("i12u", [P, 2, TOPK], U32)
        i12 = sb("i12", [P, 2, TOPK])
        posu = sb("posu", [P, TOPK], U32)
        abu = sb("abu", [P, 2, TOPK], U32)
        ab = sb("ab", [P, 2, TOPK])
        onehot = small[:, 0:2 * TOPK * TOPK]
        e12 = sb("e12", [P, 2, TOPK])
        sc = [sb(f"sc{i}", [P, TOPK]) for i in range(NT)]
        nmax = [sb(f"nmax{i}", [P, 1]) for i in range(NT)]
        esum = [sb(f"esum{i}", [P, 1]) for i in range(NT)]
        rz = [sb(f"rz{i}", [P, 1]) for i in range(NT)]
        ex = [sb(f"ex{i}", [P, TOPK]) for i in range(NT)]
        idx = [sb(f"idx{i}", [P, TOPK], U32) for i in range(NT)]
        dots = [sb(f"dots{i}", [P, TOPK]) for i in range(NT)]
        inner = [sb(f"inner{i}", [P, TOPK]) for i in range(NT)]
        tanh = [sb(f"tanh{i}", [P, TOPK]) for i in range(NT)]
        wts = [sb(f"wts{i}", [P, TOPK]) for i in range(NT)]

        psum = ctx.enter_context(nc.psum_tensor("psum", [P, 8 * 512], F32))
        bank = [psum[:, i * 512:(i + 1) * 512] for i in range(8)]
        acc = [psum[:, t * D:(t + 1) * D] for t in range(NT)]
        ada_ps = psum[:, 5 * 512:8 * 512]

        slab_in = [sem(f"slab_in{i}") for i in range(SLABS)]
        u_in = [sem(f"u_in{i}") for i in range(US)]
        v_in = [sem(f"v_in{i}") for i in range(VS)]
        u_free, v_free = sem("u_free"), sem("v_free")
        (vec_in, const_in, x_in, pos_in, bd_in, gla_small_in, mask_in, s0_in) = (
            sem(n) for n in ("vec_in", "const_in", "x_in", "pos_in", "bd_in", "gla_small_in", "mask_in", "s0_in"))
        keys_in, wq_in = sem("keys_in"), sem("wq_in")

        SEG = [(0, TP), (TP, T)]

        def slab_chunk(first, n):
            k = first + n // 2
            return k, slab[k % SLABS][:, :, (n % 2) * P:(n % 2 + 1) * P]

        def apart(eng):
            eng.sem_inc(sem("waited"), 1)

        block = ctx.enter_context(nc.Block())

        @block.sync
        def _(sp):
            def wait_used(k):
                name = max((m for m in FIRST if FIRST[m] <= k), key=FIRST.get)
                j = k - FIRST[name]
                if name.startswith("ada"):
                    sp.wait_ge(sem("ada_used"), FIRST_ADA[name] + j + 1)
                elif name != "gla_in":
                    sp.wait_ge(sem(name + "_mm"), 2 * j + 2)
                elif j < 4:
                    sp.wait_ge(sem("qk_mm"), 2 * j + 2)
                elif j < 8:
                    sp.wait_ge(sem("v_mm"), NT * (j - 3))
                else:
                    sp.wait_ge(sem("g_mm"), 2 * (j - 8) + 2)

            def load(k, src):
                sp.dma_start(slab[k % SLABS][:, :, :], src).then_inc(slab_in[k % SLABS], 16)

            def stream(name, w, width, turn=0):
                src = w.rearrange("(c p) n -> p c n", p=P)
                n = width // SW
                for j in range(n):
                    wait_used(FIRST[name] + j - SLABS)
                    a = (j + turn) % n * SW
                    load(FIRST[name] + j, src[:, :, a:a + SW])

            def stream_wq(layer):
                src = peer_wq[layer].rearrange("(c p) n -> p c n", p=P)
                sp.dma_start(wq_slab, src[:, :, 0:SW]).then_inc(wq_in, 16)
                with sp.Fori(1, PH) as h:
                    sp.wait_ge(sem("q_mm"), h * 2 + 2 * PH * layer)
                    sp.dma_start(wq_slab, src[:, :, bass.ds(h * SW, SW)]).then_inc(wq_in, 16)

            def stream_ada(layer):
                src = ada_w[layer].rearrange("(c p) n -> p c n", p=P)
                first = FIRST[f"ada{layer}"]
                for s in range(SLABS):
                    if first:
                        wait_used(first + s - SLABS)
                    load(s, src[:, :, s * SW:(s + 1) * SW])
                with sp.Fori(1, NMOD) as m:
                    for s in range(SLABS):
                        sp.wait_ge(sem("ada_used"), m * SLABS + (24 * layer + s - SLABS + 1))
                        load(s, src[:, :, bass.ds(m * D + s * SW, SW)])

            stream_ada(0)
            stream("rg_in", rg_w_in[0], 2 * D, turn=4)
            stream_ada(1)
            stream("rg_out", rg_w_out[0], D)
            sp.wait_ge(sem("rg_gate_mm"), 32)
            stream_wq(0)
            sp.wait_ge(sem("rg_fin"), 1)
            sp.dma_start(st_rg, rgfin[:, :, :]).then_inc(sem("st_rg_out"), 16)
            stream("gla_in", gla_w_in[0, :, 0:3 * D], 3 * D)
            stream("gla_out", gla_w_out[0], D)
            for h in range(HEADS):
                sp.wait_ge(sem("gla_state"), 10 * (h + 1))
                for d in range(2):
                    sp.dma_start(st_gla[d, h], state[h % 2][:, d, d, :]).then_inc(sem(f"st_gla_out{h % 2}"), 16)
            sp.wait_ge(sem("att_used"), 1)
            sp.dma_start(keys[:, :], keys_t[:, 1, :]).then_inc(keys_in, 16)
            for i in range(2):
                sp.wait_ge(sem(f"st_gla_out{i}"), 16 * HEADS)
            stream_wq(1)
            sp.wait_ge(sem("y_ready"), 1)
            sp.dma_start(y_t, hT).then_inc(sem("y_out"), 16)
            sp.wait_ge(sem("y_out"), 16)
            sp.wait_ge(sem("st_rg_out"), 16)

        @block.gpsimd
        def _(pool):
            pool.memset(area[:, 0:4 * C * P], 0.0).then_inc(sem("bd_zero"), 1)
            pool.memset(ones[:, :], 1.0).then_inc(sem("ones_set"), 1)
            pool.memset(zrow[:, :], 0.0).then_inc(sem("ones_set"), 1)

            def gathers(layer):
                u_rows = peer_u.rearrange("l n d -> (l n) d")
                v_rows = peer_v.rearrange("l n d -> (l n) d")
                pool.wait_ge(sem("xt_mm"), 6 * (layer + 1))
                pool.wait_ge(sem("xt_ev"), 6 * (layer + 1))
                pool.sem_inc(u_free, US)
                pool.sem_inc(v_free, VS)
                ur = layer * (US + NB * TOPK)
                vr = layer * (VS + NB * TOPK)
                with pool.Fori(0, PH) as h:
                    for t in range(NT):
                        pool.wait_ge(sem("idx_ready"), h * NT + (layer * NB + t + 1))
                        for j in range(TOPK):
                            pool.wait_ge(u_free, h * (NT * TOPK) + (ur + t * TOPK + j + 1))
                            pool.sem_inc(sem("pool_waited"), 1)
                            pool.indirect_dma_start(
                                ubuf[j % US], None, u_rows,
                                bass.IndirectOffsetOnAxis(ap=idx[t][:, j:j + 1], axis=0)).then_inc(u_in[j % US], 16)
                        for j in range(TOPK):
                            pool.wait_ge(v_free, h * (NT * TOPK) + (vr + t * TOPK + j + 1))
                            pool.sem_inc(sem("pool_waited"), 1)
                            pool.indirect_dma_start(
                                vbuf[j], None, v_rows,
                                bass.IndirectOffsetOnAxis(ap=idx[t][:, j:j + 1], axis=0)).then_inc(v_in[j], 16)

            gathers(0)
            gathers(1)

        @block.scalar
        def _(act):
            link = Chain(act, sem("act_step"))
            act.dma_start(vec[:, :], vecs).then_inc(vec_in, 16)
            act.dma_start(xT[:, :, :], x_t).then_inc(x_in, 16)
            act.dma_start(A[1][:, 0:C * TS].rearrange("p (c t) -> p c t", c=C), pos_t).then_inc(pos_in, 16)
            act.dma_start(ident[:, :], ident_d).then_inc(const_in, 16)
            act.dma_start(iota16[:, :], iota_d).then_inc(const_in, 16)
            act.dma_start(wz[:, :, :], gla_w_in[0].rearrange("(c p) n -> p c n", p=P)[:, :, 3 * D:3 * D + 2 * RANK]
                          ).then_inc(gla_small_in, 16)
            act.dma_start(keys[:, :], keys_t[:, 0, :]).then_inc(keys_in, 16)
            act.wait_ge(sem("bd_zero"), 1)
            for kind, w in enumerate((rg_wa, rg_wi)):
                for d in range(2):
                    for half in range(2):
                        act.dma_start(bd[64 * half:64 * half + 64, 2 * d + kind, :, 64 * half:64 * half + 64],
                                      w[0, d].rearrange("(c two) i j -> two i c j", two=2)[half]).then_inc(bd_in, 16)
            act.wait_ge(vec_in, 16)
            act.activation(cond[:, :, :].rearrange("p c s -> p s c"),
                           vec[:, V_COND:V_COND + 16].rearrange("p (s c) -> p s c", s=2),
                           ACT.Silu).then_inc(sem("cond_ready"), 1)
            link(act.activation(lamv[:, 0, :], vec[:, V_LAM:V_LAM + 2 * C], ACT.Abs))
            act.activation(lamv[:, 1, :], lamv[:, 0, :], ACT.Exp, scale=-1.0).then_inc(sem("lam_exp"), 1)

            def ada(layer):
                act.wait_ge(sem("ada_used"), 24 * (layer + 1))
                act.activation(ada_rows, ada_ps, ACT.Copy).then_inc(sem("ada_rows"), 1)

            def norm(n, modded=True, permuted=False):
                act.wait_ge(sem("x_ready"), n + 1)
                act.activation(sq, xT[:, :, :], ACT.Square).then_inc(sem("sq_ready"), 1)
                act.wait_ge(sem("ss_ready"), n + 1)
                act.activation(sd[:, :], bank[4][:, 0:T], ACT.Sqrt, scale=1.0 / D,
                               bias=vec[:, V_EPS:V_EPS + 1]).then_inc(sem("sd_ready"), 1)
                if not modded:
                    return
                if n == 0:
                    ada(0)
                act.wait_ge(sem("xn_ready"), n + 1)
                part = n % 2
                act.wait_ge(sem("gs_ready"), n // 2 + 1)
                to, gs, mods = (hP if part else hT), gs_of[n // 2], mods_of[n // 2]
                for c in range(C):
                    for s, (a, b) in enumerate(SEG):
                        src, dst = xn[:, c, a:b], to[:, c, a:b]
                        if permuted and s == 1:
                            src = src.rearrange("p (r w) -> p r w", r=ROWS)
                            dst = dst.rearrange("p (w r) -> p r w", r=ROWS)
                        act.activation(dst, src, ACT.Identity, scale=gs[:, part, c, s:s + 1],
                                       bias=mods[:, 3 * part * C + c, s:s + 1]).then_inc(sem("h_ready"), 1)

            def peer(layer):
                for g in range(6):
                    act.wait_ge(sem("xt_mm"), 6 * layer + g + 1)
                    act.activation(xtok[:, g * 512:(g + 1) * 512], bank[4 + g % 2][:, :], ACT.Copy
                                   ).then_inc(sem("xt_ev"), 1)
                ib, vr = layer * NB, layer * (VS + NB * TOPK)

                def queries(h):
                    for half in range(2):
                        act.wait_ge(sem("q_mm"), h * 2 + (2 * PH * layer + half + 1))
                        act.activation(qT[half], bank[6 + half][:, 0:T], ACT.Copy).then_inc(sem("q_ev"), 1)

                def scores(h):
                    for half in range(2):
                        act.wait_ge(sem("s_mm"), h * 2 + (2 * PH * layer + half + 1))
                        act.activation(score_sb[:, :, half, :],
                                       bank[6 + half][:, 0:NT * NK].rearrange("p (t k) -> p t k", t=NT), ACT.Copy
                                       ).then_inc(sem("s_ev"), 1)

                def exps(t):
                    act.activation(ex[t][:, :], sc[t][:, :], ACT.Exp, bias=nmax[t][:, 0:1],
                                   accum_out=esum[t][:, 0:1]).then_inc(sem("exp_ready"), 1)

                def head(h, last=False):
                    for t in range(NT):
                        blk = h * NT + t
                        act.wait_ge(sem("inner_ready"), blk + (layer * NB + 1))
                        act.activation(tanh[t][:, :], inner[t][:, :], ACT.Tanh, scale=GELU_C
                                       ).then_inc(sem("tanh_ready"), 1)
                        act.wait_ge(sem("w_ready"), blk + (layer * NB + 1))
                        for j in range(TOPK):
                            act.wait_ge(v_free, blk * TOPK + (vr + j + 1 + VS - DS))
                            act.activation(diag[j % DS][:, :], ident[:, :], ACT.Copy,
                                           scale=wts[t][:, j:j + 1]).then_inc(sem("diag_ready"), 1)
                        if last and t == NT - 1:
                            return
                        act.wait_ge(sem("idx_ready"), blk + (ib + 2))
                        exps((t + 1) % NT)
                        if t == 0 and not last:
                            queries(h + 1)
                        if t == 1 and not last:
                            scores(h + 1)

                queries(0)
                scores(0)
                act.wait_ge(sem("idx_ready"), ib + 1)
                exps(0)
                with act.Fori(0, PH - 1) as h:
                    head(h)
                head(PH - 1, last=True)
                for t in range(NT):
                    act.wait_ge(v_free, vr + VS + NB * TOPK)
                    act.activation(xtok[:, t * D:(t + 1) * D], acc[t], ACT.Copy).then_inc(sem("acc_ev"), 1)

            norm(0)
            act.wait_ge(sem("xpad_zero"), 1)
            for n in range(C):
                act.wait_ge(sem("rg_in_mm"), n + 1)
                act.activation(xpad[:, n, PAD_L:PAD_L + TP], bank[n % 4][:, 0:TP], ACT.Copy)
                act.activation(xpad[:, n, S0 + PAD_L:S0 + PAD_L + TS], bank[n % 4][:, TP:T], ACT.Copy
                               ).then_inc(sem("rg_in_ev"), 1)
            for d in range(2):
                for kind, dst, col in ((0, g_a[d], V_BA), (1, g_i[d], V_BI)):
                    for c in range(C):
                        n = (2 * d + kind) * C + c
                        act.wait_ge(sem("rg_gate_mm"), n + 1)
                        act.activation(dst[:, c, :], bank[n % 4][:, 0:WX], ACT.Sigmoid,
                                       bias=vec[:, col + d * C + c:col + d * C + c + 1]
                                       ).then_inc(sem("rg_gate_ev"), 1)
            act.wait_ge(sem("rg_gate_ev"), 32)
            act.wait_ge(sem("dec_ready"), 1)
            for d in range(2):
                if d == 1:
                    act.wait_ge(sem("xr_ready"), C)
                for c in range(C):
                    act.activation(g_b[d][:, c, :], g_a[d][:, c, :], ACT.Tanh, scale=dec4[:, d * C + c:d * C + c + 1]
                                   ).then_inc(sem("rg_tanh"), 1)
                act.wait_ge(sem("rg_tanh"), C * (d + 1))
                for c in range(C):
                    act.activation(g_a[d][:, c, :], g_a[d][:, c, :], ACT.Exp, scale=ndec8[:, d * C + c:d * C + c + 1]
                                   ).then_inc(sem("rg_a"), 1)
                act.activation(g_b[d], g_b[d], ACT.Sqrt).then_inc(sem("rg_sqrt"), 1)
            for n in range(C):
                act.wait_ge(sem("rg_in_mm"), C + n + 1)
                act.activation(gate_br[:, n, :], bank[n % 4][:, 0:T], ACT.Gelu_apprx_tanh
                               ).then_inc(sem("rg_in_ev"), 1)
            act.wait_ge(sem("rg_scan"), 4 * C)
            ada(1)
            norm(1)
            peer(0)

            act.wait_ge(sem("peer_mm"), C)
            act.dma_start(mask, mask_d).then_inc(mask_in, 16)
            act.dma_start(s0_all, state_gla.rearrange("d h k v -> k d h v")).then_inc(s0_in, 16)
            act.wait_ge(sem("wal_zero"), 1)
            for d in range(2):
                act.dma_start(wal[d * RANK:(d + 1) * RANK, d, :], w_alpha[0, d]).then_inc(gla_small_in, 16)
            norm(2, permuted=True)
            for i in range(8):
                bk = (2 + i) % 4
                act.wait_ge(sem("la_mm"), i + 1)
                act.activation(la[:, i * T:(i + 1) * T], bank[bk][:, 0:T], ACT.Identity,
                               bias=vec[:, V_BAL + i:V_BAL + i + 1]).then_inc(sem("la_ev"), 1)
            act.wait_ge(sem("la_ev"), 8)
            link(act.activation(labs, la, ACT.Abs))
            link(act.activation(labs, labs, ACT.Exp, scale=-1.0))
            act.activation(labs, labs, ACT.Ln, bias=1.0).then_inc(sem("la_ln"), 1)
            for i in range(8):
                bk = (10 + i) % 4
                act.wait_ge(sem("qk_mm"), i + 1)
                act.activation(qk[:, i, :], bank[bk][:, 0:T], ACT.Copy, scale=DK ** -0.5 if i < 4 else 1.0
                               ).then_inc(sem("qk_ev"), 1)
            act.wait_ge(sem("bc_ready"), 2)
            act.activation(la, bc, ACT.Exp, scale=1.0 / TAU).then_inc(sem("gla_e"), 1)
            act.activation(kin, bc, ACT.Exp, scale=-1.0 / TAU).then_inc(sem("gla_e"), 1)
            act.wait_ge(sem("dd_ready"), 2)
            act.activation(labs, labs, ACT.Exp, scale=1.0 / TAU).then_inc(sem("gla_e"), 1)
            for d in range(2):
                last = CH - 1 if d == 0 else 0
                act.activation(gdec[:, d * 24:(d + 1) * 24],
                               bc[:, d * 1536:(d + 1) * 1536].rearrange("p (n i) -> p n i", i=CH)[:, :, last],
                               ACT.Exp, scale=1.0 / TAU).then_inc(sem("gla_e"), 1)
            for i in range(8):
                act.wait_ge(sem("g_mm"), i + 1)
                act.activation(silu_g[:, i, :], bank[(2 + i) % 4][:, 0:T], ACT.Silu).then_inc(sem("g_ev"), 1)
            for n in range(6):
                act.wait_ge(sem("kt_mm"), n + 1)
                act.activation(kst_tok[:, n // 3, n % 3, :], bank[n % 2][:, :], ACT.Copy).then_inc(sem("kt_ev"), 1)
            for h in range(HEADS):
                act.wait_ge(sem("o_mm"), h + 1)
                if h == 0:
                    act.wait_ge(sem("kst_used"), 1)
                for v2 in range(2):
                    act.activation(oT[:, 2 * h + v2, :], bank[4 + v2][:, 0:T], ACT.Copy).then_inc(sem("o_ev"), 1)
                    act.activation(osq[:, 2 * h + v2, :], bank[4 + v2][:, 0:T], ACT.Square).then_inc(sem("o_ev"), 1)
                act.wait_ge(sem("oss_mm"), h + 1)
                if h >= 1:
                    act.wait_ge(sem("o_rstd"), h)
                act.activation(sd[:, :], bank[6][:, 0:T], ACT.Sqrt, scale=1.0 / DV,
                               bias=vec[:, V_EPS:V_EPS + 1]).then_inc(sem("o_sd"), 1)
            norm(3)
            peer(1)
            norm(4, modded=False)

        @block.tensor
        def _(pe):
            def wait_slab(k):
                pe.wait_ge(slab_in[k % SLABS], 16 * (k // SLABS + 1))

            def ada(layer):
                pe.wait_ge(sem("cond_ready"), 1)
                for b in range(3):
                    pe.matmul(ada_ps[:, b * 512:(b + 1) * 512], zrow[0:1, :], zrow[0:1, 0:1].to_broadcast([1, 512]),
                              start=True, stop=True, skip_group_check=True)
                for j in range(NMOD * SLABS):
                    m, s = j // SLABS, j % SLABS
                    wait_slab(FIRST[f"ada{layer}"] + j)
                    for k in range(C):
                        mm = pe.matmul(ada_ps[32 * s:32 * s + 2, m * SW:(m + 1) * SW], cond[:, k, :],
                                       slab[s][:, k, :], start=False, stop=(k == C - 1), skip_group_check=True)
                    mm.then_inc(sem("ada_used"), 1)

            def ada_columns(layer):
                pe.wait_ge(sem("ada_rows"), layer + 1)
                if layer == 0:
                    pe.wait_ge(const_in, 32)
                for b in range(3):
                    for i in range(4):
                        o = b * 512 + i * P
                        mm = pe.transpose(ada_ps[:, o:o + P], ada_rows[:, o:o + P], ident[:, :])
                mm.then_inc(sem("ada_cols"), 1)

            def norm(n):
                pe.wait_ge(sem("sq_ready"), n + 1)
                for c in range(C):
                    mm = pe.matmul(bank[4][:, 0:T], ones[:, :], sq[:, c, :], start=(c == 0), stop=(c == C - 1))
                mm.then_inc(sem("ss_ready"), 1)

            def project(first, n, out, rhs, signal):
                k, w = slab_chunk(first, n)
                if n % 2 == 0:
                    wait_slab(k)
                for c in range(C):
                    mm = pe.matmul(out, w[:, c, :], rhs[:, c, :], start=(c == 0), stop=(c == C - 1))
                mm.then_inc(signal, 1)

            def routing(layer):
                pe.wait_ge(sem("h_ready"), 16 * (2 * layer + 2))
                for g in range(6):
                    if g >= 2:
                        pe.wait_ge(sem("xt_ev"), 6 * layer + g - 1)
                    for i in range(4):
                        mm = pe.transpose(bank[4 + g % 2][:, i * P:(i + 1) * P],
                                          hP[:, (g % 2) * 4 + i, (g // 2) * P:(g // 2 + 1) * P], ident[:, :])
                    mm.then_inc(sem("xt_mm"), 1)

            def peer(layer):
                def queries(h):
                    pe.wait_ge(wq_in, h * 16 + 16 * (PH * layer + 1))
                    pe.wait_ge(sem("s_ev"), h * 2 + 2 * PH * layer)
                    for half in range(2):
                        for c in range(C):
                            mm = pe.matmul(bank[6 + half][:, 0:T], wq_slab[:, c, half * P:(half + 1) * P],
                                           hP[:, c, :], start=(c == 0), stop=(c == C - 1))
                        mm.then_inc(sem("q_mm"), 1)

                def scores(h):
                    for half in range(2):
                        pe.wait_ge(sem("q_ev"), h * 2 + (2 * PH * layer + half + 1))
                        for t in range(NT):
                            mm = pe.matmul(bank[6 + half][:, t * P:(t + 1) * P], qT[half][:, t * P:(t + 1) * P],
                                           keys[:, bass.ds(h * (2 * NK) + half * NK, NK)], start=True, stop=True)
                        mm.then_inc(sem("s_mm"), 1)

                def head(h, last=False):
                    for t in range(NT):
                        blk = h * NT + t
                        for j in range(TOPK):
                            pe.wait_ge(v_in[j], blk * 16 + 16 * (layer * NB + 1))
                            pe.wait_ge(sem("diag_ready"), blk * TOPK + (layer * NB * TOPK + j + 1))
                            for half in range(2):
                                mm = pe.matmul(acc[t][:, half * 512:(half + 1) * 512], diag[j % DS][:, :],
                                               vbuf[j][:, half * 512:(half + 1) * 512], start=False, stop=True,
                                               skip_group_check=True)
                            mm.then_inc(v_free, 1)
                        if t == 0 and not last:
                            queries(h + 1)
                        if t == 1 and not last:
                            scores(h + 1)

                pe.wait_ge(keys_in, 16 * (layer + 1))
                queries(0)
                scores(0)
                pe.wait_ge(sem("xt_ev"), 6 * (layer + 1))
                for t in range(NT):
                    for half in range(2):
                        pe.matmul(acc[t][:, half * 512:(half + 1) * 512], zrow[0:1, :],
                                  zrow[0:1, 0:1].to_broadcast([1, 512]), start=True, stop=True, skip_group_check=True)
                with pe.Fori(0, PH - 1) as h:
                    head(h)
                head(PH - 1, last=True)
                pe.wait_ge(sem("acc_ev"), NT * (layer + 1))
                for c in range(C):
                    if c >= 4:
                        pe.wait_ge(sem("peer_add"), C * layer + c - 3)
                    for t in range(NT):
                        mm = pe.transpose(bank[c % 4][:, t * P:(t + 1) * P],
                                          xtok[:, t * D + c * P:t * D + (c + 1) * P], ident[:, :])
                    mm.then_inc(sem("peer_mm"), 1)

            pe.wait_ge(sem("ones_set"), 2)
            norm(0)
            ada(0)
            ada_columns(0)
            pe.wait_ge(sem("h_ready"), 16)
            for n in range(C):
                if n >= 4:
                    pe.wait_ge(sem("rg_in_ev"), n - 3)
                project(FIRST["rg_in"], n, bank[n % 4][:, 0:T], hT, sem("rg_in_mm"))
            pe.wait_ge(bd_in, 16 * 8)
            for n in range(4 * C):
                c = n % C
                if n < C:
                    pe.wait_ge(sem("xr_ready"), c + 1)
                if n >= 4:
                    pe.wait_ge(sem("rg_gate_ev"), n - 3)
                else:
                    pe.wait_ge(sem("rg_in_ev"), n + 5)
                pe.matmul(bank[n % 4][:, 0:WX], bd[:, n // C, c, :], xr[:, c, :], start=True, stop=True
                          ).then_inc(sem("rg_gate_mm"), 1)
            for n in range(C, 2 * C):
                if n < C + 4:
                    pe.wait_ge(sem("rg_gate_ev"), n - C + 29)
                else:
                    pe.wait_ge(sem("rg_in_ev"), n - 3)
                project(FIRST["rg_in"], n, bank[n % 4][:, 0:T], hT, sem("rg_in_mm"))
            ada(1)
            pe.wait_ge(sem("hg_ready"), 1)
            for n in range(C):
                if n < 4:
                    pe.wait_ge(sem("rg_in_ev"), n + 13)
                else:
                    pe.wait_ge(sem("rg_out_ev"), n - 3)
                project(FIRST["rg_out"], n, bank[n % 4][:, 0:T], gate_br, sem("rg_out_mm"))
            ada_columns(1)
            norm(1)
            routing(0)
            peer(0)

            norm(2)
            pe.wait_ge(sem("h_ready"), 48)
            pe.wait_ge(gla_small_in, 48)
            for c in range(C):
                mm = pe.matmul(bank[0][0:2 * RANK, 0:T], wz[:, c, :], hT[:, c, :], start=(c == 0), stop=(c == C - 1))
            mm.then_inc(sem("z_mm"), 1)
            pe.wait_ge(sem("z_ev"), 1)
            for i in range(8):
                if i >= 4:
                    pe.wait_ge(sem("la_ev"), i - 3)
                pe.matmul(bank[(2 + i) % 4][:, 0:T], wal[:, i // 4, (i % 4) * DK:(i % 4 + 1) * DK],
                          zT, start=True, stop=True).then_inc(sem("la_mm"), 1)
            for i in range(8):
                if i < 4:
                    pe.wait_ge(sem("la_ev"), i + 5)
                else:
                    pe.wait_ge(sem("qk_ev"), i - 3)
                project(FIRST["gla_in"], i, bank[(10 + i) % 4][:, 0:T], hT, sem("qk_mm"))
            for i in range(HEADS * NT):
                if i < 4:
                    pe.wait_ge(sem("qk_ev"), i + 5)
                else:
                    pe.wait_ge(sem("v_ev"), i - 3)
                k = FIRST["gla_in"] + 4 + i // NT
                t = i % NT
                if t == 0:
                    wait_slab(k)
                for c in range(C):
                    mm = pe.matmul(bank[(2 + i) % 4][:, 0:SW], hT[:, c, t * P:(t + 1) * P], slab[k % SLABS][:, c, :],
                                   start=(c == 0), stop=(c == C - 1))
                mm.then_inc(sem("v_mm"), 1)
            for i in range(8):
                if i < 4:
                    pe.wait_ge(sem("v_ev"), i + 9)
                else:
                    pe.wait_ge(sem("g_ev"), i - 3)
                project(FIRST["gla_in"] + 8, i, bank[(2 + i) % 4][:, 0:T], hT, sem("g_mm"))
            pe.wait_ge(sem("kst_ready"), 2)
            pe.wait_ge(sem("g_ev"), 8)
            for n in range(6):
                if n >= 2:
                    pe.wait_ge(sem("kt_ev"), n - 1)
                d, t = n // 3, n % 3
                for h in range(HEADS):
                    o = d * 1536 + h * T + t * P
                    mm = pe.transpose(bank[n % 2][:, h * P:(h + 1) * P], kst[:, o:o + P], ident[:, :])
                mm.then_inc(sem("kt_mm"), 1)
            pe.wait_ge(sem("qin_ready"), 2)
            pe.wait_ge(sem("kin_ready"), 2)
            for t in range(NT):
                bk = bank[2 + t % 2]
                if t >= 2:
                    pe.wait_ge(sem("att_ev"), t - 1)
                for odd in range(2):
                    for d in range(2):
                        for h in range(HEADS):
                            o = d * 1536 + h * T + t * P + odd * CH
                            mm = pe.matmul(bk[odd * CH:(odd + 1) * CH, (4 * d + h) * CH:(4 * d + h + 1) * CH],
                                           kin[:, o:o + CH], qin[:, o:o + CH], start=True, stop=True)
                mm.then_inc(sem("att_mm"), 1)
            pe.wait_ge(sem("kt_ev"), 6)
            pe.wait_ge(s0_in, 16)
            n_u = 0

            def updates(h):
                nonlocal n_u
                for d, chunks in ((0, (0, 1, 2, 3, 4)), (1, (1, 0, 5, 4, 3))):
                    for n in chunks:
                        if n_u >= 4:
                            pe.wait_ge(sem("gla_state"), n_u - 3)
                        elif n_u < 2:
                            pe.wait_ge(sem("kt_ev"), 6)
                        else:
                            pe.wait_ge(sem("att_ev"), 3)
                        r = (n % 2) * CH
                        pe.matmul(bank[n_u % 4][:, 0:DV], kst_tok[r:r + CH, d, n // 2, h * P:(h + 1) * P],
                                  vtok[r:r + CH, n // 2, h * DV:(h + 1) * DV], start=True, stop=True
                                  ).then_inc(sem("u_mm"), 1)
                        n_u += 1

            def outputs(h):
                pe.wait_ge(sem("gla_state"), 10 * (h + 1))
                if h >= 1:
                    pe.wait_ge(sem("o_ev"), 4 * h)
                st = state[h % 2]
                for v2 in range(2):
                    vs = slice(v2 * P, (v2 + 1) * P)
                    for t in range(NT):
                        terms = [(t * P, P, vtok[:, t, h * DV + v2 * P:h * DV + (v2 + 1) * P], att2[:, t, h, :])]
                        for n in (2 * t, 2 * t + 1):
                            for d in range(2):
                                o = d * 1536 + h * T + n * CH
                                if n == (2, 5)[d]:
                                    terms.append((n * CH, CH, s0_all[:, d, h, vs], qin[:, o:o + CH]))
                                elif n != d:
                                    terms.append((n * CH, CH, st[:, d, n, vs], qin[:, o:o + CH]))
                        for i, (o, width, l, r) in enumerate(terms):
                            mm = pe.matmul(bank[4 + v2][:, o:o + width], l, r, start=(i == 0),
                                           stop=(i == len(terms) - 1), skip_group_check=True)
                mm.then_inc(sem("o_mm"), 1)

            def head_norm(h):
                pe.wait_ge(sem("o_ev"), 4 * (h + 1))
                if h >= 1:
                    pe.wait_ge(sem("o_sd"), h)
                for v2 in range(2):
                    mm = pe.matmul(bank[6][:, 0:T], ones[:, :], osq[:, 2 * h + v2, :], start=(v2 == 0), stop=(v2 == 1))
                mm.then_inc(sem("oss_mm"), 1)

            updates(0)
            for h in range(HEADS):
                outputs(h)
                if h + 1 < HEADS:
                    updates(h + 1)
                head_norm(h)
            pe.wait_ge(sem("og_ready"), HEADS)
            for n in range(C):
                if n >= 4:
                    pe.wait_ge(sem("gla_out_ev"), n - 3)
                project(FIRST["gla_out"], n, bank[n % 4][:, 0:T], oT, sem("gla_out_mm"))
            norm(3)
            routing(1)
            peer(1)
            norm(4)

        @block.vector
        def _(dve):
            link = Chain(dve, sem("dve_step"))

            dve.wait_ge(sem("lam_exp"), 1)
            e, den, w, w2, s = (lamv[:, i, :] for i in (1, 2, 3, 4, 0))
            link(dve.tensor_scalar(den, e, 2.0, None, ALU.add))
            link(dve.reciprocal(den, den))
            link(dve.tensor_tensor(w, e, den, ALU.mult))
            link(dve.tensor_tensor(w2, w, w, ALU.mult))
            link(dve.tensor_scalar(s, w2, 1.0 / 17, 1.0 / 15, ALU.mult, ALU.add))
            for k in (13, 11, 9, 7, 5, 3, 1):
                link(dve.tensor_tensor(s, s, w2, ALU.mult))
                link(dve.tensor_scalar(s, s, 1.0 / k, None, ALU.add))
            link(dve.tensor_tensor(s, s, w, ALU.mult))
            link(dve.tensor_scalar(den, vec[:, V_LAM:V_LAM + 2 * C], -1.0, 0.0, ALU.mult, ALU.max))
            link(dve.scalar_tensor_tensor(s, s, 2.0, den, ALU.mult, ALU.add))
            dve.tensor_scalar(ndec8[:, :], s, -RG_C, None, ALU.mult)
            dve.tensor_scalar(dec4[:, :], s, RG_C / 2, None, ALU.mult).then_inc(sem("dec_ready"), 1)

            dve.wait_ge(x_in, 16)
            dve.wait_ge(pos_in, 16)
            dve.tensor_tensor(xT[:, :, TP:T], xT[:, :, TP:T], A[1][:, 0:C * TS].rearrange("p (c t) -> p c t", c=C),
                              ALU.add).then_inc(sem("x_ready"), 1)

            def ada(layer):
                dve.wait_ge(sem("ada_cols"), layer + 1)
                mods, gs = mods_of[layer], gs_of[layer]
                for m in range(NMOD):
                    b = vec[:, V_ADAB + layer * 48 + m * C:V_ADAB + layer * 48 + (m + 1) * C]
                    src = ada_ps[:, m * SW:(m + 1) * SW].rearrange("p (f s x) -> p s f x", f=2, s=4)[:, :, :, 0:2]
                    ins = dve.tensor_tensor(mods[:, m * C:(m + 1) * C, :].rearrange("p (s f) x -> p s f x", f=2), src,
                                            b.rearrange("p (s f) -> p s f", f=2).unsqueeze(3).to_broadcast([P, 4, 2, 2]),
                                            ALU.add)
                link(ins)
                for part, col in ((0, V_N1), (1, V_N2)):
                    g = vec[:, col + layer * C:col + (layer + 1) * C].unsqueeze(2).to_broadcast([P, C, 2])
                    r = (1 + 3 * part) * C
                    ins = dve.scalar_tensor_tensor(gs[:, part, :, :], mods[:, r:r + C, :], 1.0, g, ALU.add, ALU.mult)
                ins.then_inc(sem("gs_ready"), 1)

            def norm(n, final=False):
                dve.wait_ge(sem("sd_ready"), n + 1)
                link(dve.reciprocal(rstd[:, :], sd[:, :]))
                ins = dve.tensor_tensor(xn, xT[:, :, :], rstd[:, :].unsqueeze(1).to_broadcast([P, C, T]), ALU.mult)
                if final:
                    link(ins)
                    ins = dve.tensor_tensor(hT, xn, vec[:, V_FG:V_FG + C].unsqueeze(2).to_broadcast([P, C, T]),
                                            ALU.mult)
                    ins.then_inc(sem("y_ready"), 1)
                else:
                    ins.then_inc(sem("xn_ready"), 1)

            def top16(vals, spare, out_v, out_i):
                link(dve.max(out_v[:, 0:8], vals), apart)
                dve.max_index(out_i[:, 0:8], out_v[:, 0:8], vals)
                link(dve.match_replace(spare, out_v[:, 0:8], vals, NEG), apart)
                link(dve.max(out_v[:, 8:16], spare), apart)
                return dve.max_index(out_i[:, 8:16], out_v[:, 8:16], spare)

            def choose(layer, q):
                for half in range(2):
                    r = slice(half * NK, (half + 1) * NK)
                    link(top16(score_sb[:, q, half, :], work[:, r], v12[:, half, :], i12u[:, half, :]), apart)
                link(dve.tensor_tensor(cand[:, :].rearrange("p (a b) -> p a b", a=TOPK),
                                       v12[:, 0, :].unsqueeze(2).to_broadcast([P, TOPK, TOPK]),
                                       v12[:, 1, :].unsqueeze(1).to_broadcast([P, TOPK, TOPK]), ALU.add))
                dve.tensor_scalar(i12[:, 0, :], i12u[:, 0, :], float(NK * layer), None, ALU.add)
                dve.tensor_copy(i12[:, 1, :], i12u[:, 1, :])
                link(top16(cand[:, :], cand2[:, :], sc[q], posu))
                dve.tensor_scalar(nmax[q][:, :], sc[q][:, 0:1], -1.0, None, ALU.mult)
                dve.tensor_scalar(abu[:, 0, :], posu[:, :], 4, None, ALU.logical_shift_right)
                link(dve.tensor_scalar(abu[:, 1, :], posu[:, :], 15, None, ALU.bitwise_and))
                link(dve.tensor_copy(ab[:, :, :], abu[:, :, :]))
                oh = onehot[:, :].rearrange("p (h j a) -> p h j a", h=2, j=TOPK)
                link(dve.tensor_tensor(oh, ab[:, :, :].unsqueeze(3).to_broadcast([P, 2, TOPK, TOPK]),
                                       iota16[:, :].unsqueeze(1).unsqueeze(1).to_broadcast([P, 2, TOPK, TOPK]),
                                       ALU.is_equal))
                link(dve.tensor_tensor(oh, oh, i12[:, :, :].unsqueeze(2).to_broadcast([P, 2, TOPK, TOPK]), ALU.mult))
                link(dve.tensor_reduce(e12[:, :, :], oh, AX_X, ALU.add))
                dve.scalar_tensor_tensor(idx[q][:, :], e12[:, 0, :], float(NK), e12[:, 1, :], ALU.mult, ALU.add
                                         ).then_inc(sem("idx_ready"), 1)

            CHOOSE = 18

            def residual_peer(layer):
                for c in range(C):
                    dve.wait_ge(sem("peer_mm"), C * layer + c + 1)
                    for sgm, (a, b) in enumerate(SEG):
                        ins = dve.scalar_tensor_tensor(xT[:, c, a:b], bank[c % 4][:, a:b],
                                                       mods_of[layer][:, 5 * C + c, sgm:sgm + 1], xT[:, c, a:b],
                                                       ALU.mult, ALU.add)
                    ins.then_inc(sem("peer_add"), 1)
                if layer == 0:
                    dve.memset(wal, 0.0).then_inc(sem("wal_zero"), 1)
                dve.wait_ge(sem("peer_add"), C * (layer + 1))
                dve.memset(work[:, 0:1], 0.0).then_inc(sem("x_ready"), 1)

            def peer(layer):
                ub, vb, sb_ = layer * (US + NB * TOPK), layer * (VS + NB * TOPK), 2 * PH * layer

                def head(h, last=False):
                    for t in range(NT):
                        blk = h * NT + t
                        for j in range(TOPK):
                            dve.wait_ge(u_in[j % US], blk * 32 + 16 * (layer * 2 * NB + j // US + 1))
                            dve.scalar_tensor_tensor(ubuf[j % US], ubuf[j % US], 1.0, xtok[:, t * D:(t + 1) * D],
                                                     ALU.mult, ALU.mult, accum_out=dots[t][:, j:j + 1]
                                                     ).then_inc(u_free, 1)
                        dve.wait_ge(u_free, blk * TOPK + (ub + US + TOPK))
                        link(dve.tensor_tensor(inner[t][:, :], dots[t][:, :], dots[t][:, :], ALU.mult))
                        link(dve.tensor_scalar(inner[t][:, :], inner[t][:, :], 0.044715, 1.0, ALU.mult, ALU.add))
                        dve.tensor_tensor(inner[t][:, :], inner[t][:, :], dots[t][:, :], ALU.mult
                                          ).then_inc(sem("inner_ready"), 1)
                        dve.wait_ge(sem("exp_ready"), blk + (layer * NB + 1))
                        link(dve.reciprocal(rz[t][:, :], esum[t][:, :]))
                        link(dve.tensor_scalar(ex[t][:, :], ex[t][:, :], rz[t][:, 0:1], 0.5, ALU.mult, ALU.mult))
                        link(dve.tensor_tensor(ex[t][:, :], ex[t][:, :], dots[t][:, :], ALU.mult))
                        dve.wait_ge(sem("tanh_ready"), blk + (layer * NB + 1))
                        dve.wait_ge(v_free, blk * TOPK + (vb + VS - TOPK))
                        dve.scalar_tensor_tensor(wts[t][:, :], tanh[t][:, :], 1.0, ex[t][:, :], ALU.add, ALU.mult
                                                 ).then_inc(sem("w_ready"), 1)
                        if last and t == NT - 1:
                            return
                        if t == NT - 1:
                            dve.wait_ge(sem("s_ev"), h * 2 + (sb_ + 4))
                            apart(dve)
                        choose(layer, (t + 1) % NT)

                dve.wait_ge(sem("s_ev"), sb_ + 2)
                choose(layer, 0)
                with dve.Fori(0, PH - 1) as h:
                    link.enter(h, NT * (CHOOSE + 5))
                    head(h)
                    link.leave(PH - 1)
                head(PH - 1, last=True)
                residual_peer(layer)

            norm(0)
            ada(0)
            dve.memset(A[2][:, 0:C * WPAD], 0.0).then_inc(sem("xpad_zero"), 1)
            for c in range(C):
                dve.wait_ge(sem("rg_in_ev"), c + 1)
                cw = [vec[:, V_CW + c * 4 + j:V_CW + c * 4 + j + 1] for j in range(4)]
                link(dve.tensor_scalar(xr[:, c, :], xpad[:, c, 0:WX], cw[0], vec[:, V_CB + c:V_CB + c + 1], ALU.mult,
                                       ALU.add))
                for j in range(1, 4):
                    ins = dve.scalar_tensor_tensor(xr[:, c, :], xpad[:, c, j:j + WX], cw[j], xr[:, c, :], ALU.mult,
                                                   ALU.add)
                    if j < 3:
                        link(ins)
                ins.then_inc(sem("xr_ready"), 1)
            for d in range(2):
                dve.wait_ge(sem("rg_gate_ev"), 16 * (d + 1))
                link(dve.tensor_tensor(g_i[d], g_i[d], xr, ALU.mult))
                dve.wait_ge(sem("rg_sqrt"), d + 1)
                dve.wait_ge(sem("rg_a"), C * (d + 1))
                link(dve.scalar_tensor_tensor(g_b[d], g_a[d], 1.0, g_b[d], ALU.add, ALU.mult))
                link(dve.tensor_tensor(g_b[d], g_b[d], g_i[d], ALU.mult))
                for c in range(C):
                    for s_, (a, b) in enumerate(((0, TP), (S0, WX))):
                        w_ = slice(a, b) if d == 0 else (slice(b - 1, a - 1, -1) if a else slice(b - 1, None, -1))
                        h0 = vec[:, V_H0 + d * C + c:V_H0 + d * C + c + 1] if s_ else 0.0
                        dve.tensor_tensor_scan(g_i[d][:, c, w_], g_a[d][:, c, w_], g_b[d][:, c, w_], h0, ALU.mult,
                                               ALU.add).then_inc(sem("rg_scan"), 1)
            dve.wait_ge(sem("rg_scan"), 4 * C)
            h_sum = g_i[0]
            dve.tensor_copy(rgfin[:, 0, :], g_i[0][:, :, TP - 1])
            link(dve.tensor_copy(rgfin[:, 1, :], g_i[1][:, :, 0]))
            link(dve.tensor_tensor(h_sum, g_i[0], g_i[1], ALU.add))
            dve.memset(work[:, 0:1], 0.0).then_inc(sem("rg_fin"), 1)
            dve.wait_ge(sem("rg_in_ev"), 2 * C)
            link(dve.tensor_tensor(gate_br[:, :, 0:TP], gate_br[:, :, 0:TP], h_sum[:, :, 0:TP], ALU.mult))
            dve.tensor_tensor(gate_br[:, :, TP:T], gate_br[:, :, TP:T], h_sum[:, :, S0:WX], ALU.mult
                              ).then_inc(sem("hg_ready"), 1)
            for c in range(C):
                dve.wait_ge(sem("rg_out_mm"), c + 1)
                for s_, (a, b) in enumerate(SEG):
                    ins = dve.scalar_tensor_tensor(xT[:, c, a:b], bank[c % 4][:, a:b], mods_of[0][:, 2 * C + c, s_:s_ + 1],
                                                   xT[:, c, a:b], ALU.mult, ALU.add)
                ins.then_inc(sem("rg_out_ev"), 1)
            dve.wait_ge(sem("rg_out_ev"), C)
            dve.memset(work[:, 0:1], 0.0).then_inc(sem("x_ready"), 1)
            ada(1)
            norm(1)
            peer(0)

            norm(2)
            dve.wait_ge(sem("z_mm"), 1)
            dve.tensor_copy(zT, bank[0][0:2 * RANK, 0:T]).then_inc(sem("z_ev"), 1)
            keep = qin
            link(dve.memset(keep, 1.0))
            for d, col in ((0, 0), (1, CH - 1)):
                ins = dve.memset(keep[:, d * 1536:(d + 1) * 1536].rearrange("p (n i) -> p n i", i=CH)[:, :, col:col + 1],
                                 0.0)
            link(ins)
            dve.wait_ge(sem("la_ln"), 1)
            link(dve.scalar_tensor_tensor(la, la, 0.0, labs, ALU.min, ALU.subtract))
            dve.tensor_tensor_scan(bc[:, 0:1536], keep[:, 0:1536], la[:, 0:1536], 0.0, ALU.mult, ALU.add
                                   ).then_inc(sem("bc_ready"), 1)
            dve.tensor_tensor_scan(bc[:, 3071:1535:-1], keep[:, 3071:1535:-1], la[:, 3071:1535:-1], 0.0, ALU.mult,
                                   ALU.add).then_inc(sem("bc_ready"), 1)
            dve.wait_ge(sem("bc_ready"), 2)
            for d in range(2):
                b3 = bc[:, d * 1536:(d + 1) * 1536].rearrange("p (n i) -> p n i", i=CH)
                last = CH - 1 if d == 0 else 0
                dve.tensor_tensor(labs[:, d * 1536:(d + 1) * 1536].rearrange("p (n i) -> p n i", i=CH),
                                  b3[:, :, last:last + 1].to_broadcast([P, 24, CH]), b3, ALU.subtract
                                  ).then_inc(sem("dd_ready"), 1)
            for i in range(HEADS * NT):
                dve.wait_ge(sem("v_mm"), i + 1)
                h, t = i // NT, i % NT
                dve.tensor_copy(vtok[:, t, h * DV:(h + 1) * DV], bank[(2 + i) % 4][:, 0:DV]).then_inc(sem("v_ev"), 1)
            dve.wait_ge(sem("qk_ev"), 8)
            qv = A[3][:, 0:1536]
            kv = A[3][:, 1536:3072]
            halves = [slice(0, 1536), slice(1536, 3072)]
            dve.wait_ge(sem("gla_e"), 3)
            for d in range(2):
                dve.tensor_tensor(kst[:, halves[d]], kst[:, halves[d]], kv, ALU.mult).then_inc(sem("kst_ready"), 1)
            for d in range(2):
                dve.tensor_tensor(kin[:, halves[d]], kin[:, halves[d]], kv, ALU.mult).then_inc(sem("kin_ready"), 1)
            for d in range(2):
                dve.tensor_tensor(qin[:, halves[d]], la[:, halves[d]], qv, ALU.mult).then_inc(sem("qin_ready"), 1)
            dve.wait_ge(sem("gla_e"), 5)
            dve.wait_ge(sem("qin_ready"), 2)
            dve.wait_ge(sem("kin_ready"), 2)
            dve.wait_ge(sem("kst_ready"), 2)
            dve.memset(work[:, 0:1], 0.0).then_inc(sem("kst_used"), 1)
            link(dve.memset(att2, 0.0))
            dve.wait_ge(mask_in, 16)
            for t in range(NT):
                dve.wait_ge(sem("att_mm"), t + 1)
                link(dve.memset(attm, 0.0))
                link(dve.copy_predicated(attm, mask, bank[2 + t % 2][:, :]))
                for r in (0, CH):
                    link(dve.tensor_tensor(att2[r:r + CH, t, :, r:r + CH],
                                           attm[r:r + CH, 0:256].rearrange("p (h i) -> p h i", h=HEADS),
                                           attm[r:r + CH, 256:512].rearrange("p (h i) -> p h i", h=HEADS), ALU.add))
                dve.memset(work[:, 0:1], 0.0).then_inc(sem("att_ev"), 1)
            dve.wait_ge(s0_in, 16)
            n_u = 0

            def states(h):
                nonlocal n_u
                st = state[h % 2]
                if h >= 2:
                    dve.wait_ge(sem("o_mm"), h - 1)
                    dve.wait_ge(sem(f"st_gla_out{h % 2}"), 32 * (h // 2))
                for d, chunks in ((0, (0, 1, 2, 3, 4)), (1, (1, 0, 5, 4, 3))):
                    for i, n in enumerate(chunks):
                        nxt = (n + 1 if d == 0 else n - 1) if i != 1 else d
                        prev = s0_all[:, d, h, :] if i == 2 else st[:, d, n, :]
                        dve.wait_ge(sem("u_mm"), n_u + 1)
                        u = bank[n_u % 4][:, 0:DV]
                        if i == 0:
                            ins = dve.tensor_copy(st[:, d, nxt, :], u)
                        else:
                            g = gdec[:, d * 24 + h * NCH + n:d * 24 + h * NCH + n + 1]
                            ins = dve.scalar_tensor_tensor(st[:, d, nxt, :], prev, g, u, ALU.mult, ALU.add)
                        ins.then_inc(sem("gla_state"), 1)
                        n_u += 1
                        dve.wait_ge(sem("gla_state"), n_u)

            states(0)
            for h in range(HEADS):
                if h + 1 < HEADS:
                    states(h + 1)
                dve.wait_ge(sem("o_sd"), h + 1)
                link(dve.reciprocal(rstd[:, :], sd[:, :]))
                dve.memset(work[:, 0:1], 0.0).then_inc(sem("o_rstd"), 1)
                for v2 in range(2):
                    c = 2 * h + v2
                    link(dve.scalar_tensor_tensor(oT[:, c, :], oT[:, c, :], vec[:, V_GNG + c:V_GNG + c + 1],
                                                  rstd[:, :], ALU.mult, ALU.mult))
                    ins = dve.tensor_tensor(oT[:, c, :], oT[:, c, :], silu_g[:, c, :], ALU.mult)
                ins.then_inc(sem("og_ready"), 1)
                if h == HEADS - 1:
                    dve.wait_ge(sem("og_ready"), HEADS)
                    dve.memset(work[:, 0:1], 0.0).then_inc(sem("att_used"), 1)
            for c in range(C):
                dve.wait_ge(sem("gla_out_mm"), c + 1)
                dve.scalar_tensor_tensor(xT[:, c, 0:TP], bank[c % 4][:, 0:TP], mods_of[1][:, 2 * C + c, 0:1],
                                         xT[:, c, 0:TP], ALU.mult, ALU.add)
                xs = xT[:, c, TP:T].rearrange("p (r w) -> p r w", r=ROWS)
                dve.scalar_tensor_tensor(xs, bank[c % 4][:, TP:T].rearrange("p (w r) -> p r w", r=ROWS),
                                         mods_of[1][:, 2 * C + c, 1:2], xs, ALU.mult, ALU.add
                                         ).then_inc(sem("gla_out_ev"), 1)
            dve.wait_ge(sem("gla_out_ev"), C)
            dve.memset(work[:, 0:1], 0.0).then_inc(sem("x_ready"), 1)
            norm(3)
            peer(1)
            norm(4, final=True)


def kernel(**inputs):
    import numpy as np
    import concourse.bacc as bacc
    from concourse import mybir as mb
    from concourse.bass_utils import run_bass_kernel_spmd as run

    a = {k: np.asarray(v) for k, v in inputs.items()}

    def feat(v):
        v = v.reshape(-1, C, P)
        return v.transpose(2, 0, 1).reshape(P, -1)

    f = np.float32
    tt = np.arange(TS)
    nf = D // 4
    freq = (f(1.0) / (f(10000.0) ** (np.arange(nf, dtype=f) / f(nf)))).astype(f)
    ar = (tt // GRID_W).astype(f)[:, None] * freq
    ac = (tt % GRID_W).astype(f)[:, None] * freq
    pos = np.concatenate([np.sin(ar), np.cos(ar), np.sin(ac), np.cos(ac)], axis=-1).astype(f)

    def to_feat(x):
        return np.ascontiguousarray(x.T.reshape(C, P, -1).transpose(1, 0, 2))

    x = np.concatenate([a["x_prompt"][0], a["x_sample"][0]], axis=0)
    vecs = np.zeros((P, V_END), f)
    vecs[:, V_COND:V_COND + 8] = feat(a["c_ctx"])
    vecs[:, V_COND + 8:V_COND + 16] = feat(a["c"])
    vecs[:, V_N1:V_N1 + 16] = feat(a["norm1_g"])
    vecs[:, V_N2:V_N2 + 16] = feat(a["norm2_g"])
    vecs[:, V_ADAB:V_ADAB + 96] = feat(a["ada_b"])
    vecs[:, V_CW:V_CW + 32] = a["rg_conv_w"][0].reshape(4, C, P).transpose(2, 1, 0).reshape(P, 32)
    vecs[:, V_CB:V_CB + 8] = feat(a["rg_conv_b"])
    vecs[:, V_BA:V_BA + 16] = feat(a["rg_ba"][0])
    vecs[:, V_BI:V_BI + 16] = feat(a["rg_bi"][0])
    vecs[:, V_LAM:V_LAM + 16] = feat(a["rg_lambda"][0])
    vecs[:, V_H0:V_H0 + 16] = feat(a["state_rglru"][0, 0])
    vecs[:, V_BAL:V_BAL + 8] = a["gla_b_alpha"][0].reshape(8, P).T
    vecs[:, V_GNG:V_GNG + 8] = feat(a["gla_norm_g"])
    vecs[:, V_FG:V_FG + 8] = feat(a["final_norm_g"])
    vecs[:, V_EPS] = 1e-6
    keys = np.stack([a["peer_k1"], a["peer_k2"]], axis=2)
    keys = np.ascontiguousarray(keys.transpose(4, 0, 1, 2, 3).reshape(P, DEPTH, 2 * PH * NK))
    j, i = np.arange(P)[:, None] % CH, np.arange(CH)[None, :]
    mask = np.concatenate([np.tile(j <= i, (1, HEADS)), np.tile(j >= i, (1, HEADS))], axis=1).astype(np.uint32)
    arrays = {
        "x_t": to_feat(x), "pos_t": to_feat(pos), "vecs": vecs, "ident": np.eye(P, dtype=f), "mask": mask,
        "iota": np.tile(np.arange(TOPK, dtype=f), (P, 1)), "keys_t": keys,
        "ada_w": a["ada_w"], "peer_wq": a["peer_wq"], "peer_u": a["peer_u"], "peer_v": a["peer_v"],
        "rg_w_in": a["rg_w_in"], "rg_wa": a["rg_wa"], "rg_wi": a["rg_wi"], "rg_w_out": a["rg_w_out"],
        "gla_w_in": a["gla_w_in"], "w_alpha": a["gla_w_alpha"], "state_gla": a["state_gla"][0, 0],
        "gla_w_out": a["gla_w_out"],
    }
    arrays = {k: np.ascontiguousarray(v) for k, v in arrays.items()}
    nc = bacc.Bacc("TRN2", target_bir_lowering=False, num_devices=1)
    ins = [nc.dram_tensor("in_" + k, v.shape, mb.dt.from_np(v.dtype), kind="ExternalInput").ap() for k, v in arrays.items()]
    outs = [nc.dram_tensor("out_" + k, s, mb.dt.float32, kind="ExternalOutput").ap() for k, s in (
        ("y_t", (P, C, T)), ("st_rg", (P, 2, C)), ("st_gla", (2, HEADS, DK, DV)))]
    build(nc, *ins, *outs)
    r = run(nc, [{"in_" + k: v for k, v in arrays.items()}], core_ids=[0]).results[0]
    y = np.asarray(r["out_y_t"]).transpose(2, 1, 0).reshape(T, D)
    st_rg = np.asarray(r["out_st_rg"]).transpose(1, 2, 0).reshape(1, 1, 2, D)
    st_gla = np.asarray(r["out_st_gla"]).reshape(1, 1, 2, HEADS, DK, DV)
    return (np.ascontiguousarray(y[None, :TP]), np.ascontiguousarray(y[None, TP:]),
            np.ascontiguousarray(st_rg), np.ascontiguousarray(st_gla))
```

```python
from contextlib import ExitStack

import concourse.bass as bass
from concourse import mybir

P = 128
D = 1024
C = D // P
TP, TS = 128, 256
T = TP + TS
NT = T // P
DEPTH = 2
NMOD = 6
GRID_W = 64
ROWS = TS // GRID_W
SLABS = 4
SW = 256
PAD_L, PAD_R = 2, 1
WX = T + PAD_L + PAD_R
WPAD = WX + PAD_L + PAD_R
S0 = TP + PAD_L + PAD_R
HEADS, DK, DV = 4, 128, 256
CH = 64
NCH = T // CH
RANK = 16
TAU = 16.0
PH, NK, TOPK = 8, 128, 16
NB = NT * PH
US, VS, DS = 8, 16, 8
LAST_PARTS = (range(0, 8), range(8, 12), range(12, 16))
NSTEP = NB - 1 + len(LAST_PARTS)
RG_C = 8.0
GELU_C = 0.7978845608028654
AW = 3120
NEG = -3.0e38

F32 = mybir.dt.float32
U32 = mybir.dt.uint32
ALU = mybir.AluOpType
ACT = mybir.ActivationFunctionType
AX_X = mybir.AxisListType.X

V_COND, V_N1, V_N2, V_ADAB = 0, 16, 32, 48
V_CW, V_CB, V_BA, V_BI, V_LAM, V_H0, V_BAL, V_GNG, V_FG, V_EPS, V_END = (
    144, 176, 184, 200, 216, 232, 248, 256, 264, 272, 273)

SEQ = [("ada", j) for j in range(8)]
_ada = iter(range(8, 48))
for _j in range(4):
    SEQ += [("rg_in", _j)] + [("ada", next(_ada)) for _ in range(4)]
SEQ += [("ada", next(_ada)) for _ in range(8)]
for _j in range(4, 8):
    SEQ += [("rg_in", _j)] + [("ada", next(_ada)) for _ in range(4)]
SEQ += [("rg_out", _j) for _j in range(4)] + [("gla_in", _j) for _j in range(12)]
SEQ += [("gla_out", _j) for _j in range(4)]
PLACE = {item: k for k, item in enumerate(SEQ)}
_more = PLACE["rg_out", 0]
SLOT = [k % (SLABS + 2) if k < _more else (k - _more) % SLABS for k in range(len(SEQ))]
TURN = [SLOT[:k].count(SLOT[k]) for k in range(len(SEQ))]
BEFORE = [max([i for i in range(k) if SLOT[i] == SLOT[k]], default=None) for k in range(len(SEQ))]
LAST_IN = {slot: max(k for k in range(_more) if SLOT[k] == slot) for slot in (SLABS, SLABS + 1)}
GLA_PLAN = ["g0", "g1", "kt", "g2", "att", "g3", "g4", "u0", "g5", "u1", "g6", "o0", "g7", "n0",
            "o1", "u2", "n1", "o2", "u3", "n2", "o3", "n3"]


class Chain:

    def __init__(self, eng, sem):
        self.eng, self.sem, self.base, self.n = eng, sem, 0, 0

    def __call__(self, ins, apart=None):
        self.n += 1
        ins.then_inc(self.sem, 1)
        self.eng.wait_ge(self.sem, self.base + self.n)
        if apart:
            apart(self.eng)

    def enter(self, rounds_before, per_round):
        self.start, self.per, self.n = self.base + self.n, per_round, 0
        self.base = self.start + rounds_before * per_round

    def leave(self, rounds):
        assert self.n == self.per, (self.n, self.per)
        self.base, self.n = self.start + rounds * self.per, 0


def build(nc, x_t, pos_t, vecs, ident_d, mask_d, iota_d, keys_t, ada_w, peer_wq, peer_u, peer_v, rg_w_in,
          rg_wa, rg_wi, rg_w_out, gla_w_in, w_alpha, state_gla, gla_w_out, y_t, st_rg, st_gla):
    ctx = ExitStack()
    with ctx:
        def sb(name, shape, dt=F32):
            return ctx.enter_context(nc.sbuf_tensor(name, shape, dt))

        sems = {}

        def sem(name):
            if name not in sems:
                sems[name] = ctx.enter_context(nc.semaphore(name))
            return sems[name]

        xT = sb("xT", [P, C, T])
        slab = [sb(f"slab{i}", [P, C, SW]) for i in range(SLABS)]
        arena = sb("arena", [P, 8 * AW])
        xtok = sb("xtok", [P, C * WX])
        area = sb("area", [P, 6656])
        keys = sb("keys", [P, 2 * PH * NK])
        vec = sb("vec", [P, V_END])
        ident = sb("ident", [P, P])
        ones = sb("ones", [P, P])
        zrow = sb("zrow", [1, P])
        iota16 = sb("iota16", [P, TOPK])
        cond = sb("cond", [P, C, 2])
        mods_of = [sb(f"mods{i}", [P, NMOD * C, 2]) for i in range(DEPTH)]
        gs_of = [sb(f"gs{i}", [P, 2, C, 2]) for i in range(DEPTH)]
        sd = sb("sd", [P, T])
        rstd = sb("rstd", [P, T])
        lamv = sb("lamv", [P, 5, 2 * C])
        dec4 = sb("dec4", [P, 2 * C])
        ndec8 = sb("ndec8", [P, 2 * C])
        rgfin = sb("rgfin", [P, 2, C])
        wz = sb("wz", [P, C, 2 * RANK])
        small = sb("small", [P, 2 * T + 2 * HEADS * NCH])

        slab += [keys[:, :].rearrange("p (c n) -> p c n", c=C),
                 area[:, 4 * C * P + 512:4 * C * P + 512 + C * SW].rearrange("p (c n) -> p c n", c=C)]
        A = [arena[:, i * AW:(i + 1) * AW] for i in range(8)]

        def cols(a, n=T):
            return a[:, 0:C * n].rearrange("p (c t) -> p c t", c=C)

        hT = cols(A[0])
        gate_br = cols(A[1])
        xpad = cols(A[2], WPAD)[:, :, :]
        xr = cols(A[3], WX)
        g_a = [cols(A[4], WX), cols(A[7], WX)]
        g_i = [cols(A[5], WX), cols(xtok, WX)]
        g_b = [cols(A[6], WX), cols(A[2], WX)]
        sq = cols(A[7])
        xn = cols(A[6])
        bd = area[:, 0:4 * C * P].rearrange("p (k c m) -> p k c m", k=4, c=C)
        vtok = A[1][:, 0:NT * D].rearrange("p (t v) -> p t v", t=NT)
        silu_g = cols(A[2])
        qk = cols(A[3])
        la, labs, bc, qin = A[4][:, 0:C * T], A[5][:, 0:C * T], A[6][:, 0:C * T], A[7][:, 0:C * T]
        kin = area[:, 0:C * T]
        kst = labs
        kst_tok = A[3][:, 0:C * T].rearrange("p (d t f) -> p d t f", d=2, t=NT)
        state = [A[4][:, 0:2 * NCH * DV].rearrange("p (d n v) -> p d n v", d=2, n=NCH),
                 area[:, C * T:C * T + 2 * NCH * DV].rearrange("p (d n v) -> p d n v", d=2, n=NCH)]
        oT = cols(A[6])
        osq = xtok[:, 2 * D:2 * D + 2 * T].rearrange("p (v t) -> p v t", v=2)
        s0_all = xtok[:, 0:2 * HEADS * DV].rearrange("p (d h v) -> p d h v", d=2, h=HEADS)
        wal = xtok[0:2 * RANK, 2 * D:3 * D].rearrange("r (d k) -> r d k", d=2)
        zT = small[0:2 * RANK, 0:T]
        ada_rows = small[:, 0:512]
        gdec = small[:, 768:768 + 2 * HEADS * NCH]
        mask = keys[:, 0:8 * CH].bitcast(U32)
        attm = area[:, 2 * C * T:2 * C * T + 8 * CH]
        att2 = keys[:, 8 * CH:8 * CH + NT * HEADS * P].rearrange("p (t h i) -> p t h i", t=NT, h=HEADS)
        ubuf = [arena[:, i * D:(i + 1) * D] for i in range(US)]
        vbuf = [arena[:, (US + i) * D:(US + i + 1) * D] for i in range(VS)]
        hP = cols(area)
        score_sb = area[:, C * T:C * T + NT * 2 * NK].rearrange("p (t n k) -> p t n k", t=NT, n=2)
        wq_slab = area[:, 3840:3840 + C * SW].rearrange("p (c n) -> p c n", c=C)
        qT = [area[:, 5888 + i * T:5888 + (i + 1) * T] for i in range(2)]
        diag = [sb(f"diag{i}", [P, P]) for i in range(DS)]
        work = sb("work", [P, 2 * NK])
        cand, cand2 = sd[:, 0:TOPK * TOPK], rstd[:, 0:TOPK * TOPK]
        v12 = sb("v12", [P, 2, TOPK])
        i12u = sb("i12u", [P, 2, TOPK], U32)
        i12 = sb("i12", [P, 2, TOPK])
        posu = sb("posu", [P, TOPK], U32)
        abu = sb("abu", [P, 2, TOPK], U32)
        ab = sb("ab", [P, 2, TOPK])
        onehot = small[:, 0:2 * TOPK * TOPK]
        e12 = sb("e12", [P, 2, TOPK])
        sc = [sb(f"sc{i}", [P, TOPK]) for i in range(NT)]
        nmax = [sb(f"nmax{i}", [P, 1]) for i in range(NT)]
        esum = [sb(f"esum{i}", [P, 1]) for i in range(NT)]
        rz = [sb(f"rz{i}", [P, 1]) for i in range(NT)]
        ex = [sb(f"ex{i}", [P, TOPK]) for i in range(NT)]
        idx = [sb(f"idx{i}", [P, TOPK], U32) for i in range(NT)]
        dots = [sb(f"dots{i}", [P, TOPK]) for i in range(NT)]
        inner = [sb(f"inner{i}", [P, TOPK]) for i in range(NT)]
        tanh = [sb(f"tanh{i}", [P, TOPK]) for i in range(NT)]
        wts = [sb(f"wts{i}", [P, TOPK]) for i in range(NT)]

        psum = ctx.enter_context(nc.psum_tensor("psum", [P, 8 * 512], F32))
        bank = [psum[:, i * 512:(i + 1) * 512] for i in range(8)]
        acc = [psum[:, t * D:(t + 1) * D] for t in range(NT)]

        slab_in = [sem(f"slab_in{i}") for i in range(SLABS + 2)]
        u_in = [sem(f"u_in{i}") for i in range(US)]
        v_in = [sem(f"v_in{i}") for i in range(VS)]
        u_free, v_free = sem("u_free"), sem("v_free")
        (vec_in, const_in, x_in, pos_in, bd_in, gla_small_in, mask_in, s0_in) = (
            sem(n) for n in ("vec_in", "const_in", "x_in", "pos_in", "bd_in", "gla_small_in", "mask_in", "s0_in"))
        keys_in, wq_in = sem("keys_in"), sem("wq_in")

        SEG = [(0, TP), (TP, T)]

        def apart(eng):
            eng.sem_inc(sem("waited"), 1)

        def parts(last, t):
            return LAST_PARTS if last and t == NT - 1 else (range(TOPK),)

        block = ctx.enter_context(nc.Block())

        @block.sync
        def _(sp):
            def wait_used(k):
                name, j = SEQ[k]
                if name == "ada":
                    sp.wait_ge(sem("ada_used"), j + 1)
                elif name != "gla_in":
                    sp.wait_ge(sem(name + "_mm"), 2 * j + 2)
                elif j < 4:
                    sp.wait_ge(sem("qk_mm"), 2 * j + 2)
                elif j < 8:
                    sp.wait_ge(sem("v_mm"), NT * (j - 3))
                else:
                    sp.wait_ge(sem("g_mm"), 2 * (j - 8) + 2)

            sources = {"rg_in": rg_w_in[0], "rg_out": rg_w_out[0], "gla_in": gla_w_in[0, :, 0:3 * D],
                       "gla_out": gla_w_out[0]}

            def stream(first, end):
                for k in range(first, end):
                    name, j = SEQ[k]
                    w = ada_w[j // 24] if name == "ada" else sources[name]
                    n = j % 24 if name == "ada" else (j + 4) % 8 if name == "rg_in" else j
                    if BEFORE[k] is not None:
                        wait_used(BEFORE[k])
                    sp.dma_start(slab[SLOT[k]][:, :, :],
                                 w.rearrange("(c p) n -> p c n", p=P)[:, :, n * SW:(n + 1) * SW]
                                 ).then_inc(slab_in[SLOT[k]], 16)

            def stream_wq(layer):
                src = peer_wq[layer].rearrange("(c p) n -> p c n", p=P)
                sp.dma_start(wq_slab, src[:, :, 0:SW]).then_inc(wq_in, 16)
                with sp.Fori(1, PH) as h:
                    sp.wait_ge(sem("q_mm"), h * 2 + 2 * PH * layer)
                    sp.dma_start(wq_slab, src[:, :, bass.ds(h * SW, SW)]).then_inc(wq_in, 16)

            stream(0, PLACE["gla_in", 0])
            wait_used(LAST_IN[SLABS])
            sp.dma_start(keys[:, :], keys_t[:, 0, :]).then_inc(keys_in, 16)
            wait_used(LAST_IN[SLABS + 1])
            sp.wait_ge(sem("rg_gate_mm"), 32)
            stream_wq(0)
            sp.wait_ge(sem("rg_fin"), 1)
            sp.dma_start(st_rg, rgfin[:, :, :]).then_inc(sem("st_rg_out"), 16)
            stream(PLACE["gla_in", 0], len(SEQ))
            for h in range(HEADS):
                sp.wait_ge(sem("gla_state"), 10 * (h + 1))
                for d in range(2):
                    sp.dma_start(st_gla[d, h], state[h % 2][:, d, d, :]).then_inc(sem(f"st_gla_out{h % 2}"), 16)
            sp.wait_ge(sem("att_used"), 1)
            sp.dma_start(keys[:, :], keys_t[:, 1, :]).then_inc(keys_in, 16)
            for i in range(2):
                sp.wait_ge(sem(f"st_gla_out{i}"), 16 * HEADS)
            stream_wq(1)
            for i in range(4):
                sp.wait_ge(sem("y_ready"), 2 * (i + 1))
                sp.dma_start(y_t[:, 2 * i:2 * i + 2, :], hT[:, 2 * i:2 * i + 2, :]).then_inc(sem("y_out"), 16)
            sp.wait_ge(sem("y_out"), 64)
            sp.wait_ge(sem("st_rg_out"), 16)

        @block.gpsimd
        def _(pool):
            pool.memset(area[:, 0:4 * C * P], 0.0).then_inc(sem("bd_zero"), 1)
            pool.memset(ones[:, :], 1.0).then_inc(sem("ones_set"), 1)
            pool.memset(zrow[:, :], 0.0).then_inc(sem("ones_set"), 1)

            def gathers(layer):
                u_rows = peer_u.rearrange("l n d -> (l n) d")
                v_rows = peer_v.rearrange("l n d -> (l n) d")
                pool.wait_ge(sem("h_ready"), 32 * (layer + 1))
                pool.sem_inc(u_free, US)
                pool.sem_inc(v_free, VS)
                ur = layer * (US + NB * TOPK)
                vr = layer * (VS + NB * TOPK)

                def head(h, last=False):
                    for t in range(NT):
                        pool.wait_ge(sem("idx_ready"), h * NT + (layer * NB + t + 1))
                        for part in parts(last, t):
                            for j in part:
                                pool.wait_ge(u_free, h * (NT * TOPK) + (ur + t * TOPK + j + 1))
                                pool.sem_inc(sem("pool_waited"), 1)
                                pool.indirect_dma_start(
                                    ubuf[j % US], None, u_rows,
                                    bass.IndirectOffsetOnAxis(ap=idx[t][:, j:j + 1], axis=0)).then_inc(u_in[j % US], 16)
                            for j in part:
                                pool.wait_ge(v_free, h * (NT * TOPK) + (vr + t * TOPK + j + 1))
                                pool.sem_inc(sem("pool_waited"), 1)
                                pool.indirect_dma_start(
                                    vbuf[j], None, v_rows,
                                    bass.IndirectOffsetOnAxis(ap=idx[t][:, j:j + 1], axis=0)).then_inc(v_in[j], 16)

                with pool.Fori(0, PH - 1) as h:
                    head(h)
                head(PH - 1, last=True)

            gathers(0)
            gathers(1)

        @block.scalar
        def _(act):
            link = Chain(act, sem("act_step"))
            act.dma_start(vec[:, :], vecs).then_inc(vec_in, 16)
            act.dma_start(xT[:, :, :], x_t).then_inc(x_in, 16)
            act.dma_start(A[1][:, 0:C * TS].rearrange("p (c t) -> p c t", c=C), pos_t).then_inc(pos_in, 16)
            act.wait_ge(vec_in, 16)
            act.activation(cond[:, :, :].rearrange("p c s -> p s c"),
                           vec[:, V_COND:V_COND + 16].rearrange("p (s c) -> p s c", s=2),
                           ACT.Silu).then_inc(sem("cond_ready"), 1)
            act.dma_start(ident[:, :], ident_d).then_inc(const_in, 16)
            act.dma_start(iota16[:, :], iota_d).then_inc(const_in, 16)
            act.dma_start(wz[:, :, :], gla_w_in[0].rearrange("(c p) n -> p c n", p=P)[:, :, 3 * D:3 * D + 2 * RANK]
                          ).then_inc(gla_small_in, 16)
            act.wait_ge(sem("bd_zero"), 1)
            for kind, w in enumerate((rg_wa, rg_wi)):
                for d in range(2):
                    for half in range(2):
                        act.dma_start(bd[64 * half:64 * half + 64, 2 * d + kind, :, 64 * half:64 * half + 64],
                                      w[0, d].rearrange("(c two) i j -> two i c j", two=2)[half]).then_inc(bd_in, 16)
            link(act.activation(lamv[:, 0, :], vec[:, V_LAM:V_LAM + 2 * C], ACT.Abs))
            act.activation(lamv[:, 1, :], lamv[:, 0, :], ACT.Exp, scale=-1.0).then_inc(sem("lam_exp"), 1)

            def rows(group):
                act.wait_ge(sem("ada_used"), 8 * (group + 1))
                if group:
                    act.wait_ge(sem("ada_cols"), group)
                act.activation(ada_rows, bank[5 + group % 3], ACT.Copy).then_inc(sem("ada_rows"), 1)

            def squares(n):
                for c in range(C):
                    act.wait_ge(sem("x_ev"), C * n + c + 1)
                    act.activation(sq[:, c, :], xT[:, c, :], ACT.Square).then_inc(sem("sq_ready"), 1)

            def deviation(n):
                act.wait_ge(sem("ss_ready"), n + 1)
                act.activation(sd[:, :], bank[4][:, 0:T], ACT.Sqrt, scale=1.0 / D,
                               bias=vec[:, V_EPS:V_EPS + 1]).then_inc(sem("sd_ready"), 1)

            def modulate_segment(n, c, s, permuted=False):
                layer, part = n // 2, n % 2
                a, b = SEG[s]
                src, dst = xn[:, c, a:b], (hP if part else hT)[:, c, a:b]
                if permuted and s == 1:
                    src = src.rearrange("p (r w) -> p r w", r=ROWS)
                    dst = dst.rearrange("p (w r) -> p r w", r=ROWS)
                act.activation(dst, src, ACT.Identity, scale=gs_of[layer][:, part, c, s:s + 1],
                               bias=mods_of[layer][:, 3 * part * C + c, s:s + 1]).then_inc(sem("h_ready"), 1)

            def modulate(n, permuted=False):
                act.wait_ge(sem("gs_ready"), n + 1)
                for c in range(C):
                    if c % 2 == 0:
                        act.wait_ge(sem("xn_ready"), 9 * (n // 2) + c // 2 + 1)
                    for s in range(2):
                        modulate_segment(n, c, s, permuted)

            def modulate_for_peer(layer):
                n = 2 * layer + 1

                def sample(chunks):
                    for c in chunks:
                        if c % 2 == 0:
                            act.wait_ge(sem("xn_ready"), 9 * layer + 6 + c // 2)
                        modulate_segment(n, c, 1)

                def query(half):
                    act.wait_ge(sem("first_q_mm"), 2 * layer + half + 1)
                    act.activation(qT[half][:, 0:P], bank[6 + half][:, 0:P], ACT.Copy).then_inc(sem("first_q_ev"), 1)

                act.wait_ge(sem("gs_ready"), n + 1)
                act.wait_ge(sem("xn_ready"), 9 * layer + 5)
                for c in range(C):
                    modulate_segment(n, c, 0)
                query(0)
                sample(range(0, 2))
                query(1)
                for half in range(2):
                    act.wait_ge(sem("first_s_mm"), 2 * layer + half + 1)
                    act.activation(score_sb[:, 0, half, :], bank[6 + half][:, 0:NK], ACT.Copy
                                   ).then_inc(sem("first_s_ev"), 1)
                sample(range(2, C))

            def peer(layer):
                ib, vr = layer * NB, layer * (VS + NB * TOPK)

                def queries(h, t0=0):
                    for half in range(2):
                        act.wait_ge(sem("q_mm"), h * 2 + (2 * PH * layer + half + 1))
                        act.activation(qT[half][:, t0 * P:T], bank[6 + half][:, t0 * P:T], ACT.Copy
                                       ).then_inc(sem("q_ev"), 1)

                def scores(h, t0=0):
                    for half in range(2):
                        act.wait_ge(sem("s_mm"), h * 2 + (2 * PH * layer + half + 1))
                        act.activation(score_sb[:, t0:NT, half, :],
                                       bank[6 + half][:, t0 * NK:NT * NK].rearrange("p (t k) -> p t k", k=NK), ACT.Copy
                                       ).then_inc(sem("s_ev"), 1)

                def exps(t):
                    act.activation(ex[t][:, :], sc[t][:, :], ACT.Exp, bias=nmax[t][:, 0:1],
                                   accum_out=esum[t][:, 0:1]).then_inc(sem("exp_ready"), 1)

                def head(h, last=False):
                    for t in range(NT):
                        blk = h * NT + t
                        for i, part in enumerate(parts(last, t)):
                            p = slice(part[0], part[-1] + 1)
                            act.wait_ge(sem("inner_ready"), blk + (layer * NSTEP + i + 1))
                            act.activation(tanh[t][:, p], inner[t][:, p], ACT.Tanh, scale=GELU_C
                                           ).then_inc(sem("tanh_ready"), 1)
                            act.wait_ge(sem("w_ready"), blk + (layer * NSTEP + i + 1))
                            for j in part:
                                act.wait_ge(v_free, blk * TOPK + (vr + j + 1 + VS - DS))
                                act.activation(diag[j % DS][:, :], ident[:, :], ACT.Copy,
                                               scale=wts[t][:, j:j + 1]).then_inc(sem("diag_ready"), 1)
                        if last and t >= 1:
                            total(t - 1)
                        if last and t == NT - 1:
                            return
                        act.wait_ge(sem("idx_ready"), blk + (ib + 2))
                        exps((t + 1) % NT)
                        if t == 0 and not last:
                            queries(h + 1)
                        if t == 1 and not last:
                            scores(h + 1)

                def total(t):
                    act.wait_ge(v_free, vr + VS + (NB - NT + t + 1) * TOPK)
                    act.activation(xtok[:, t * D:(t + 1) * D], acc[t], ACT.Copy).then_inc(sem("acc_ev"), 1)

                for g in range(6):
                    act.wait_ge(sem("xt_mm"), 6 * layer + g + 1)
                    act.activation(xtok[:, g * 512:(g + 1) * 512], bank[4 + g % 2], ACT.Copy
                                   ).then_inc(sem("xt_ev"), 1)
                queries(0, 1)
                scores(0, 1)
                act.wait_ge(sem("idx_ready"), ib + 1)
                exps(0)
                with act.Fori(0, PH - 1) as h:
                    head(h)
                head(PH - 1, last=True)
                total(NT - 1)

            squares(0)
            deviation(0)
            rows(0)
            modulate(0)
            act.wait_ge(sem("xpad_zero"), 1)
            for n in range(C):
                act.wait_ge(sem("rg_in_mm"), n + 1)
                act.activation(xpad[:, n, PAD_L:PAD_L + TP], bank[n % 4][:, 0:TP], ACT.Copy)
                act.activation(xpad[:, n, S0 + PAD_L:S0 + PAD_L + TS], bank[n % 4][:, TP:T], ACT.Copy
                               ).then_inc(sem("rg_in_ev"), 1)
            rows(1)
            for d in range(2):
                if d == 1:
                    rows(2)
                for kind, dst, col in ((0, g_a[d], V_BA), (1, g_i[d], V_BI)):
                    for c in range(C):
                        n = (2 * d + kind) * C + c
                        act.wait_ge(sem("rg_gate_mm"), n + 1)
                        act.activation(dst[:, c, :], bank[n % 4][:, 0:WX], ACT.Sigmoid,
                                       bias=vec[:, col + d * C + c:col + d * C + c + 1]
                                       ).then_inc(sem("rg_gate_ev"), 1)
            act.wait_ge(sem("rg_gate_ev"), 32)
            act.wait_ge(sem("dec_ready"), 1)
            for d in range(2):
                if d == 1:
                    act.wait_ge(sem("xr_ready"), C)
                for c in range(C):
                    act.activation(g_b[d][:, c, :], g_a[d][:, c, :], ACT.Tanh, scale=dec4[:, d * C + c:d * C + c + 1]
                                   ).then_inc(sem("rg_tanh"), 1)
                act.wait_ge(sem("rg_tanh"), C * (d + 1))
                for c in range(C):
                    act.activation(g_a[d][:, c, :], g_a[d][:, c, :], ACT.Exp, scale=ndec8[:, d * C + c:d * C + c + 1]
                                   ).then_inc(sem("rg_a"), 1)
                act.activation(g_b[d], g_b[d], ACT.Sqrt).then_inc(sem("rg_sqrt"), 1)
            rows(3)
            for n in range(C):
                act.wait_ge(sem("rg_in_mm"), C + n + 1)
                act.activation(gate_br[:, n, :], bank[n % 4][:, 0:T], ACT.Gelu_apprx_tanh
                               ).then_inc(sem("rg_in_ev"), 1)
            rows(4)
            rows(5)
            squares(1)
            deviation(1)
            modulate_for_peer(0)
            peer(0)

            squares(2)
            deviation(2)
            act.wait_ge(sem("peer_mm"), C)
            act.dma_start(mask, mask_d).then_inc(mask_in, 16)
            act.dma_start(s0_all, state_gla.rearrange("d h k v -> k d h v")).then_inc(s0_in, 16)
            act.wait_ge(sem("wal_zero"), 1)
            for d in range(2):
                act.dma_start(wal[d * RANK:(d + 1) * RANK, d, :], w_alpha[0, d]).then_inc(gla_small_in, 16)
            modulate(2, permuted=True)
            for i in range(8):
                bk = (2 + i) % 4
                act.wait_ge(sem("la_mm"), i + 1)
                act.activation(la[:, i * T:(i + 1) * T], bank[bk][:, 0:T], ACT.Identity,
                               bias=vec[:, V_BAL + i:V_BAL + i + 1]).then_inc(sem("la_ev"), 1)
            act.wait_ge(sem("la_ev"), 8)
            link(act.activation(labs, la, ACT.Abs))
            link(act.activation(labs, labs, ACT.Exp, scale=-1.0))
            act.activation(labs, labs, ACT.Ln, bias=1.0).then_inc(sem("la_ln"), 1)
            for i in range(8):
                bk = (10 + i) % 4
                act.wait_ge(sem("qk_mm"), i + 1)
                act.activation(qk[:, i, :], bank[bk][:, 0:T], ACT.Copy, scale=DK ** -0.5 if i < 4 else 1.0
                               ).then_inc(sem("qk_ev"), 1)
            act.wait_ge(sem("bc_ready"), 2)
            act.activation(la, bc, ACT.Exp, scale=1.0 / TAU).then_inc(sem("gla_e"), 1)
            act.activation(kin, bc, ACT.Exp, scale=-1.0 / TAU).then_inc(sem("gla_e"), 1)
            act.wait_ge(sem("dd_ready"), 2)
            act.activation(labs, labs, ACT.Exp, scale=1.0 / TAU).then_inc(sem("gla_e"), 1)
            for d in range(2):
                last = CH - 1 if d == 0 else 0
                act.activation(gdec[:, d * 24:(d + 1) * 24],
                               bc[:, d * 1536:(d + 1) * 1536].rearrange("p (n i) -> p n i", i=CH)[:, :, last],
                               ACT.Exp, scale=1.0 / TAU).then_inc(sem("gla_e"), 1)
            for step in GLA_PLAN:
                h = int(step[1:]) if step[1:].isdigit() else 0
                if step[0] == "g":
                    act.wait_ge(sem("g_mm"), h + 1)
                    act.activation(silu_g[:, h, :], bank[h % 2][:, 0:T], ACT.Silu).then_inc(sem("g_ev"), 1)
                elif step == "kt":
                    act.wait_ge(sem("kst_used"), 1)
                    for n in range(6):
                        act.wait_ge(sem("kt_mm"), n + 1)
                        act.activation(kst_tok[:, n // 3, n % 3, :], bank[2 + n % 2], ACT.Copy
                                       ).then_inc(sem("kt_ev"), 1)
                elif step[0] == "o":
                    act.wait_ge(sem("o_mm"), h + 1)
                    for v2 in range(2):
                        act.activation(osq[:, v2, :], bank[6 + v2][:, 0:T], ACT.Square
                                       ).then_inc(sem("o_ev"), 1)
                    for v2 in range(2):
                        act.activation(oT[:, 2 * h + v2, :], bank[6 + v2][:, 0:T], ACT.Copy).then_inc(sem("o_ev"), 1)
                elif step[0] == "n":
                    act.wait_ge(sem("oss_mm"), h + 1)
                    if h >= 1:
                        act.wait_ge(sem("o_rstd"), h)
                    act.activation(sd[:, :], bank[h % 2][:, 0:T], ACT.Sqrt, scale=1.0 / DV,
                                   bias=vec[:, V_EPS:V_EPS + 1]).then_inc(sem("o_sd"), 1)
            squares(3)
            deviation(3)
            modulate_for_peer(1)
            peer(1)
            squares(4)
            deviation(4)

        @block.tensor
        def _(pe):
            def wait_slab(k):
                pe.wait_ge(slab_in[SLOT[k]], 16 * (TURN[k] + 1))

            ada_at = 0

            def ada_slabs(n):
                nonlocal ada_at
                for pair in range(ada_at, ada_at + n, 2):
                    group = pair // 8
                    out = bank[5 + group % 3]
                    if pair % 8 == 0:
                        if group >= 3:
                            pe.wait_ge(sem("ada_rows"), group - 2)
                        pe.matmul(out, zrow[0:1, :], zrow[0:1, 0:1].to_broadcast([1, 512]), start=True, stop=True,
                                  skip_group_check=True)
                    o = pair // SLABS % 2 * SW
                    for c in range(C):
                        for a in (pair, pair + 1):
                            s, k = a % SLABS, PLACE["ada", a]
                            if c == 0:
                                wait_slab(k)
                            mm = pe.matmul(out[32 * s:32 * s + 2, o:o + SW], cond[:, c, :], slab[SLOT[k]][:, c, :],
                                           start=False, stop=(c == C - 1), skip_group_check=True)
                            if c == C - 1:
                                mm.then_inc(sem("ada_used"), 1)
                ada_at += n

            def ada_columns(group):
                pe.wait_ge(sem("ada_rows"), group + 1)
                if group == 0:
                    pe.wait_ge(const_in, 32)
                    pe.wait_ge(sem("sd_ready"), 1)
                else:
                    pe.wait_ge(sem("ada_mod"), group)
                for i in range(4):
                    mm = pe.transpose(bank[4][:, i * P:(i + 1) * P], ada_rows[:, i * P:(i + 1) * P], ident[:, :])
                mm.then_inc(sem("ada_cols"), 1)

            def square_sum(n, c):
                pe.wait_ge(sem("sq_ready"), C * n + c + 1)
                if n == 1 and c == 0:
                    pe.wait_ge(sem("ada_mod"), 6)
                mm = pe.matmul(bank[4][:, 0:T], ones[:, :], sq[:, c, :], start=(c == 0), stop=(c == C - 1))
                if c == C - 1:
                    mm.then_inc(sem("ss_ready"), 1)

            def project(name, n, out, rhs, signal, ready=None, chunks=range(C)):
                k = PLACE[name, n // 2]
                if n % 2 == 0 and chunks[0] == 0:
                    wait_slab(k)
                for c in chunks:
                    if ready is not None:
                        pe.wait_ge(ready[0], ready[1][c])
                    mm = pe.matmul(out, slab[SLOT[k]][:, c, (n % 2) * P:(n % 2 + 1) * P], rhs[:, c, :],
                                   start=(c == 0), stop=(c == C - 1))
                if chunks[-1] == C - 1:
                    mm.then_inc(signal, 1)

            def routing(layer):
                for g in range(6):
                    if g == 0:
                        pe.wait_ge(sem("sd_ready"), 2 * layer + 2)
                    if g >= 2:
                        pe.wait_ge(sem("xt_ev"), 6 * layer + g - 1)
                    for i in range(4):
                        mm = pe.transpose(bank[4 + g % 2][:, i * P:(i + 1) * P],
                                          hP[:, (g % 2) * 4 + i, (g // 2) * P:(g // 2 + 1) * P], ident[:, :])
                    mm.then_inc(sem("xt_mm"), 1)

            def peer(layer):
                def first_tile():
                    pe.wait_ge(wq_in, 16 * (PH * layer + 1))
                    for half in range(2):
                        for c in range(C):
                            pe.wait_ge(sem("h_ready"), 16 * (2 * layer + 1) + c + 1)
                            mm = pe.matmul(bank[6 + half][:, 0:P], wq_slab[:, c, half * P:(half + 1) * P],
                                           hP[:, c, 0:P], start=(c == 0), stop=(c == C - 1))
                        mm.then_inc(sem("first_q_mm"), 1)
                    for half in range(2):
                        pe.wait_ge(sem("first_q_ev"), 2 * layer + half + 1)
                        pe.matmul(bank[6 + half][:, 0:P], qT[half][:, 0:P], keys[:, half * NK:(half + 1) * NK],
                                  start=True, stop=True).then_inc(sem("first_s_mm"), 1)

                def queries(h, t0=0):
                    pe.wait_ge(wq_in, h * 16 + 16 * (PH * layer + 1))
                    pe.wait_ge(sem("s_ev"), h * 2 + 2 * PH * layer)
                    for half in range(2):
                        for c in range(C):
                            mm = pe.matmul(bank[6 + half][:, t0 * P:T], wq_slab[:, c, half * P:(half + 1) * P],
                                           hP[:, c, t0 * P:T], start=(c == 0), stop=(c == C - 1))
                        mm.then_inc(sem("q_mm"), 1)

                def scores(h, t0=0):
                    for half in range(2):
                        pe.wait_ge(sem("q_ev"), h * 2 + (2 * PH * layer + half + 1))
                        for t in range(t0, NT):
                            mm = pe.matmul(bank[6 + half][:, t * P:(t + 1) * P], qT[half][:, t * P:(t + 1) * P],
                                           keys[:, bass.ds(h * (2 * NK) + half * NK, NK)], start=True, stop=True)
                        mm.then_inc(sem("s_mm"), 1)

                def head(h, last=False):
                    for t in range(NT):
                        blk = h * NT + t
                        for j in range(TOPK):
                            pe.wait_ge(v_in[j], blk * 16 + 16 * (layer * NB + 1))
                            pe.wait_ge(sem("diag_ready"), blk * TOPK + (layer * NB * TOPK + j + 1))
                            for half in range(2):
                                mm = pe.matmul(acc[t][:, half * 512:(half + 1) * 512], diag[j % DS][:, :],
                                               vbuf[j][:, half * 512:(half + 1) * 512], start=False, stop=True,
                                               skip_group_check=True)
                            mm.then_inc(v_free, 1)
                        if t == 0 and not last:
                            queries(h + 1)
                        if t == 1 and not last:
                            scores(h + 1)

                pe.wait_ge(keys_in, 16 * (layer + 1))
                first_tile()
                pe.wait_ge(sem("first_s_ev"), 2 * (layer + 1))
                pe.wait_ge(sem("h_ready"), 32 * (layer + 1))
                routing(layer)
                queries(0, 1)
                scores(0, 1)
                pe.wait_ge(sem("xt_ev"), 6 * (layer + 1))
                for t in range(NT):
                    for half in range(2):
                        pe.matmul(acc[t][:, half * 512:(half + 1) * 512], zrow[0:1, :],
                                  zrow[0:1, 0:1].to_broadcast([1, 512]), start=True, stop=True, skip_group_check=True)
                with pe.Fori(0, PH - 1) as h:
                    head(h)
                head(PH - 1, last=True)
                pe.wait_ge(sem("acc_ev"), NT * (layer + 1))
                for c in range(C):
                    if c >= 4:
                        pe.wait_ge(sem("x_ev"), C * (2 * layer + 2) + c - 3)
                    for t in range(NT):
                        mm = pe.transpose(bank[c % 4][:, t * P:(t + 1) * P],
                                          xtok[:, t * D + c * P:t * D + (c + 1) * P], ident[:, :])
                    mm.then_inc(sem("peer_mm"), 1)
                    if c >= 2:
                        square_sum(2 * layer + 2, c - 2)
                square_sum(2 * layer + 2, C - 2)
                square_sum(2 * layer + 2, C - 1)

            pe.wait_ge(sem("ones_set"), 2)
            pe.wait_ge(sem("cond_ready"), 1)
            ada_slabs(4)
            for c in range(C):
                square_sum(0, c)
            ada_slabs(4)
            ada_columns(0)
            for n in range(C):
                if n >= 4:
                    pe.wait_ge(sem("rg_in_ev"), n - 3)
                project("rg_in", n, bank[n % 4][:, 0:T], hT, sem("rg_in_mm"),
                        ready=(sem("h_ready"), [2 * (c + 1) for c in range(C)]) if n == 0 else None)
                if n % 2:
                    ada_slabs(4)
            pe.wait_ge(bd_in, 16 * 8)
            for n in range(4 * C):
                c = n % C
                if n < C:
                    pe.wait_ge(sem("xr_ready"), c + 1)
                if n >= 4:
                    pe.wait_ge(sem("rg_gate_ev"), n - 3)
                else:
                    pe.wait_ge(sem("rg_in_ev"), n + 5)
                pe.matmul(bank[n % 4][:, 0:WX], bd[:, n // C, c, :], xr[:, c, :], start=True, stop=True
                          ).then_inc(sem("rg_gate_mm"), 1)
                if n % 8 == 7:
                    ada_slabs(2)
                if n in (12, 24):
                    ada_columns(n // 12)
            for n in range(C, 2 * C):
                if n < C + 4:
                    pe.wait_ge(sem("rg_gate_ev"), n - C + 29)
                else:
                    pe.wait_ge(sem("rg_in_ev"), n - 3)
                project("rg_in", n, bank[n % 4][:, 0:T], hT, sem("rg_in_mm"))
                if n % 2:
                    ada_slabs(4)
                if n == C + 5:
                    ada_columns(3)
            ada_columns(4)
            for n in range(C):
                if n < 4:
                    pe.wait_ge(sem("rg_in_ev"), n + 13)
                else:
                    pe.wait_ge(sem("x_ev"), C + n - 3)
                project("rg_out", n, bank[n % 4][:, 0:T], gate_br, sem("rg_out_mm"),
                        ready=(sem("hg_ready"), [2 * (c // 2 + 1) for c in range(C)]) if n == 0 else None)
                if n == 3:
                    ada_columns(5)
                if n >= 5:
                    square_sum(1, n - 5)
            for c in range(3, C):
                square_sum(1, c)
            peer(0)

            pe.wait_ge(gla_small_in, 16)
            for c in range(C):
                pe.wait_ge(sem("h_ready"), 32 + 2 * (c + 1))
                mm = pe.matmul(bank[0][0:2 * RANK, 0:T], wz[:, c, :], hT[:, c, :], start=(c == 0), stop=(c == C - 1))
            mm.then_inc(sem("z_mm"), 1)
            pe.wait_ge(sem("z_ev"), 1)
            pe.wait_ge(gla_small_in, 48)
            for i in range(8):
                if i >= 4:
                    pe.wait_ge(sem("la_ev"), i - 3)
                pe.matmul(bank[(2 + i) % 4][:, 0:T], wal[:, i // 4, (i % 4) * DK:(i % 4 + 1) * DK],
                          zT, start=True, stop=True).then_inc(sem("la_mm"), 1)
            for i in range(8):
                if i < 4:
                    pe.wait_ge(sem("la_ev"), i + 5)
                else:
                    pe.wait_ge(sem("qk_ev"), i - 3)
                project("gla_in", i, bank[(10 + i) % 4][:, 0:T], hT, sem("qk_mm"))
            for i in range(HEADS * NT):
                if i < 4:
                    pe.wait_ge(sem("qk_ev"), i + 5)
                else:
                    pe.wait_ge(sem("v_ev"), i - 3)
                k = PLACE["gla_in", 4 + i // NT]
                t = i % NT
                if t == 0:
                    wait_slab(k)
                for c in range(C):
                    mm = pe.matmul(bank[(2 + i) % 4][:, 0:SW], hT[:, c, t * P:(t + 1) * P], slab[SLOT[k]][:, c, :],
                                   start=(c == 0), stop=(c == C - 1))
                mm.then_inc(sem("v_mm"), 1)
            def gate(i):
                if i < 2:
                    pe.wait_ge(sem("v_ev"), 12)
                else:
                    pe.wait_ge(sem("g_ev"), i - 1)
                project("gla_in", 16 + i, bank[i % 2][:, 0:T], hT, sem("g_mm"))

            def turn_kst():
                pe.wait_ge(sem("kst_ready"), 2)
                pe.wait_ge(sem("v_ev"), 12)
                for n in range(6):
                    if n >= 2:
                        pe.wait_ge(sem("kt_ev"), n - 1)
                    d, t = n // 3, n % 3
                    for h in range(HEADS):
                        o = d * 1536 + h * T + t * P
                        mm = pe.transpose(bank[2 + n % 2][:, h * P:(h + 1) * P], kst[:, o:o + P], ident[:, :])
                    mm.then_inc(sem("kt_mm"), 1)

            def attention():
                pe.wait_ge(sem("qin_ready"), 2)
                pe.wait_ge(sem("kin_ready"), 2)
                for t in range(NT):
                    if t >= 2:
                        pe.wait_ge(sem("att_ev"), t - 1)
                    for odd in range(2):
                        for d in range(2):
                            for h in range(HEADS):
                                o = d * 1536 + h * T + t * P + odd * CH
                                mm = pe.matmul(bank[4 + t % 2][odd * CH:(odd + 1) * CH,
                                                               (4 * d + h) * CH:(4 * d + h + 1) * CH],
                                               kin[:, o:o + CH], qin[:, o:o + CH], start=True, stop=True)
                    mm.then_inc(sem("att_mm"), 1)

            n_u = 0

            def updates(h):
                nonlocal n_u
                for d, chunks in ((0, (0, 1, 2, 3, 4)), (1, (1, 0, 5, 4, 3))):
                    for n in chunks:
                        if n_u >= 4:
                            pe.wait_ge(sem("gla_state"), n_u - 3)
                        elif n_u < 2:
                            pe.wait_ge(sem("kt_ev"), 6)
                        else:
                            pe.wait_ge(sem("att_ev"), 3)
                        r = (n % 2) * CH
                        pe.matmul(bank[2 + n_u % 4][:, 0:DV], kst_tok[r:r + CH, d, n // 2, h * P:(h + 1) * P],
                                  vtok[r:r + CH, n // 2, h * DV:(h + 1) * DV], start=True, stop=True
                                  ).then_inc(sem("u_mm"), 1)
                        n_u += 1

            def outputs(h):
                pe.wait_ge(sem("gla_state"), 10 * (h + 1))
                if h >= 1:
                    pe.wait_ge(sem("o_ev"), 4 * h)
                else:
                    pe.wait_ge(s0_in, 16)
                st = state[h % 2]
                for v2 in range(2):
                    vs = slice(v2 * P, (v2 + 1) * P)
                    for t in range(NT):
                        terms = [(t * P, P, vtok[:, t, h * DV + v2 * P:h * DV + (v2 + 1) * P], att2[:, t, h, :])]
                        for n in (2 * t, 2 * t + 1):
                            for d in range(2):
                                o = d * 1536 + h * T + n * CH
                                if n == (2, 5)[d]:
                                    terms.append((n * CH, CH, s0_all[:, d, h, vs], qin[:, o:o + CH]))
                                elif n != d:
                                    terms.append((n * CH, CH, st[:, d, n, vs], qin[:, o:o + CH]))
                        for i, (o, width, l, r) in enumerate(terms):
                            mm = pe.matmul(bank[6 + v2][:, o:o + width], l, r, start=(i == 0),
                                           stop=(i == len(terms) - 1), skip_group_check=True)
                mm.then_inc(sem("o_mm"), 1)

            def head_norm(h):
                pe.wait_ge(sem("o_ev"), 4 * h + 2)
                if h < 2:
                    pe.wait_ge(sem("g_ev"), 8)
                else:
                    pe.wait_ge(sem("o_sd"), h - 1)
                for v2 in range(2):
                    mm = pe.matmul(bank[h % 2][:, 0:T], ones[:, :], osq[:, v2, :], start=(v2 == 0),
                                   stop=(v2 == 1))
                mm.then_inc(sem("oss_mm"), 1)

            for step in GLA_PLAN:
                if step == "kt":
                    turn_kst()
                elif step == "att":
                    attention()
                else:
                    {"g": gate, "u": updates, "o": outputs, "n": head_norm}[step[0]](int(step[1:]))
            head_done = (sem("og_ready"), [c // 2 + 1 for c in range(C)])
            for n in range(2):
                if n == 1:
                    pe.wait_ge(sem("o_sd"), HEADS)
                project("gla_out", n, bank[n][:, 0:T], oT, sem("gla_out_mm"), head_done, range(0, C - 2))
            for n in range(C):
                if n >= 4:
                    pe.wait_ge(sem("x_ev"), 3 * C + n - 3)
                project("gla_out", n, bank[n % 4][:, 0:T], oT, sem("gla_out_mm"), head_done,
                        range(C - 2, C) if n < 2 else range(C))
                if n >= 2:
                    square_sum(3, n - 2)
            square_sum(3, C - 2)
            square_sum(3, C - 1)
            peer(1)

        @block.vector
        def _(dve):
            link = Chain(dve, sem("dve_step"))

            dve.wait_ge(sem("lam_exp"), 1)
            e, den, w, w2, s = (lamv[:, i, :] for i in (1, 2, 3, 4, 0))
            link(dve.tensor_scalar(den, e, 2.0, None, ALU.add))
            link(dve.reciprocal(den, den))
            link(dve.tensor_tensor(w, e, den, ALU.mult))
            link(dve.tensor_tensor(w2, w, w, ALU.mult))
            link(dve.tensor_scalar(s, w2, 1.0 / 17, 1.0 / 15, ALU.mult, ALU.add))
            for k in (13, 11, 9, 7, 5, 3, 1):
                link(dve.tensor_tensor(s, s, w2, ALU.mult))
                link(dve.tensor_scalar(s, s, 1.0 / k, None, ALU.add))
            link(dve.tensor_tensor(s, s, w, ALU.mult))
            link(dve.tensor_scalar(den, vec[:, V_LAM:V_LAM + 2 * C], -1.0, 0.0, ALU.mult, ALU.max))
            link(dve.scalar_tensor_tensor(s, s, 2.0, den, ALU.mult, ALU.add))
            dve.tensor_scalar(ndec8[:, :], s, -RG_C, None, ALU.mult)
            dve.tensor_scalar(dec4[:, :], s, RG_C / 2, None, ALU.mult).then_inc(sem("dec_ready"), 1)

            dve.wait_ge(x_in, 16)
            dve.wait_ge(pos_in, 16)
            for c in range(C):
                dve.tensor_tensor(xT[:, c, TP:T], xT[:, c, TP:T], A[1][:, c * TS:(c + 1) * TS], ALU.add
                                  ).then_inc(sem("x_ev"), 1)

            def modulation(group):
                dve.wait_ge(sem("ada_cols"), group + 1)
                layer = group // 3
                mods = mods_of[layer]
                for i in range(2):
                    m = group % 3 * 2 + i
                    b = vec[:, V_ADAB + layer * 48 + m * C:V_ADAB + layer * 48 + (m + 1) * C]
                    src = bank[4][:, i * SW:(i + 1) * SW].rearrange("p (f s x) -> p s f x", f=2, s=4)[:, :, :, 0:2]
                    ins = dve.tensor_tensor(mods[:, m * C:(m + 1) * C, :].rearrange("p (s f) x -> p s f x", f=2), src,
                                            b.rearrange("p (s f) -> p s f", f=2).unsqueeze(3).to_broadcast([P, 4, 2, 2]),
                                            ALU.add)
                ins.then_inc(sem("ada_mod"), 1)
                if group % 3 != 1:
                    part = group % 3 // 2
                    dve.wait_ge(sem("ada_mod"), group + 1)
                    col = (V_N1, V_N2)[part]
                    g = vec[:, col + layer * C:col + (layer + 1) * C].unsqueeze(2).to_broadcast([P, C, 2])
                    r = (1 + 3 * part) * C
                    dve.scalar_tensor_tensor(gs_of[layer][:, part, :, :], mods[:, r:r + C, :], 1.0, g, ALU.add,
                                             ALU.mult).then_inc(sem("gs_ready"), 1)

            def norm(n):
                dve.wait_ge(sem("sd_ready"), n + 1)
                if n % 2 == 0:
                    pieces = [(0, T, c, 2) for c in range(0, C, 2)]
                else:
                    pieces = [(0, TP, 0, C)] + [(TP, T, c, 2) for c in range(0, C, 2)]
                for a, b, c, width in pieces:
                    if c == 0:
                        link(dve.reciprocal(rstd[:, a:b], sd[:, a:b]))
                    dve.tensor_tensor(xn[:, c:c + width, a:b], xT[:, c:c + width, a:b],
                                      rstd[:, a:b].unsqueeze(1).to_broadcast([P, width, b - a]), ALU.mult
                                      ).then_inc(sem("xn_ready"), 1)

            def top16(vals, spare, out_v, out_i):
                link(dve.max(out_v[:, 0:8], vals), apart)
                dve.max_index(out_i[:, 0:8], out_v[:, 0:8], vals)
                link(dve.match_replace(spare, out_v[:, 0:8], vals, NEG), apart)
                link(dve.max(out_v[:, 8:16], spare), apart)
                return dve.max_index(out_i[:, 8:16], out_v[:, 8:16], spare)

            def choose(layer, q):
                for half in range(2):
                    r = slice(half * NK, (half + 1) * NK)
                    link(top16(score_sb[:, q, half, :], work[:, r], v12[:, half, :], i12u[:, half, :]), apart)
                link(dve.tensor_tensor(cand[:, :].rearrange("p (a b) -> p a b", a=TOPK),
                                       v12[:, 0, :].unsqueeze(2).to_broadcast([P, TOPK, TOPK]),
                                       v12[:, 1, :].unsqueeze(1).to_broadcast([P, TOPK, TOPK]), ALU.add))
                dve.tensor_scalar(i12[:, 0, :], i12u[:, 0, :], float(NK * layer), None, ALU.add)
                dve.tensor_copy(i12[:, 1, :], i12u[:, 1, :])
                link(top16(cand[:, :], cand2[:, :], sc[q], posu))
                dve.tensor_scalar(nmax[q][:, :], sc[q][:, 0:1], -1.0, None, ALU.mult)
                dve.tensor_scalar(abu[:, 0, :], posu[:, :], 4, None, ALU.logical_shift_right)
                link(dve.tensor_scalar(abu[:, 1, :], posu[:, :], 15, None, ALU.bitwise_and))
                link(dve.tensor_copy(ab[:, :, :], abu[:, :, :]))
                oh = onehot[:, :].rearrange("p (h j a) -> p h j a", h=2, j=TOPK)
                link(dve.tensor_tensor(oh, ab[:, :, :].unsqueeze(3).to_broadcast([P, 2, TOPK, TOPK]),
                                       iota16[:, :].unsqueeze(1).unsqueeze(1).to_broadcast([P, 2, TOPK, TOPK]),
                                       ALU.is_equal))
                link(dve.tensor_tensor(oh, oh, i12[:, :, :].unsqueeze(2).to_broadcast([P, 2, TOPK, TOPK]), ALU.mult))
                link(dve.tensor_reduce(e12[:, :, :], oh, AX_X, ALU.add))
                dve.scalar_tensor_tensor(idx[q][:, :], e12[:, 0, :], float(NK), e12[:, 1, :], ALU.mult, ALU.add
                                         ).then_inc(sem("idx_ready"), 1)

            CHOOSE = 18

            def residual_peer(layer):
                if layer == 0:
                    dve.wait_ge(sem("acc_ev"), NT)
                for c in range(C):
                    dve.wait_ge(sem("peer_mm"), C * layer + c + 1)
                    for sgm, (a, b) in enumerate(SEG):
                        ins = dve.scalar_tensor_tensor(xT[:, c, a:b], bank[c % 4][:, a:b],
                                                       mods_of[layer][:, 5 * C + c, sgm:sgm + 1], xT[:, c, a:b],
                                                       ALU.mult, ALU.add)
                    ins.then_inc(sem("x_ev"), 1)
                if layer == 0:
                    dve.memset(wal, 0.0).then_inc(sem("wal_zero"), 1)

            def peer(layer):
                ub, vb, sb_ = layer * (US + NB * TOPK), layer * (VS + NB * TOPK), 2 * PH * layer

                def head(h, last=False):
                    for t in range(NT):
                        blk = h * NT + t
                        for i, part in enumerate(parts(last, t)):
                            p = slice(part[0], part[-1] + 1)
                            for j in part:
                                dve.wait_ge(u_in[j % US], blk * 32 + 16 * (layer * 2 * NB + j // US + 1))
                                dve.scalar_tensor_tensor(ubuf[j % US], ubuf[j % US], 1.0, xtok[:, t * D:(t + 1) * D],
                                                         ALU.mult, ALU.mult, accum_out=dots[t][:, j:j + 1]
                                                         ).then_inc(u_free, 1)
                            dve.wait_ge(u_free, blk * TOPK + (ub + US + part[-1] + 1))
                            link(dve.tensor_tensor(inner[t][:, p], dots[t][:, p], dots[t][:, p], ALU.mult))
                            link(dve.tensor_scalar(inner[t][:, p], inner[t][:, p], 0.044715, 1.0, ALU.mult, ALU.add))
                            dve.tensor_tensor(inner[t][:, p], inner[t][:, p], dots[t][:, p], ALU.mult
                                              ).then_inc(sem("inner_ready"), 1)
                            if i == 0:
                                dve.wait_ge(sem("exp_ready"), blk + (layer * NB + 1))
                                link(dve.reciprocal(rz[t][:, :], esum[t][:, :]))
                                link(dve.tensor_scalar(ex[t][:, :], ex[t][:, :], rz[t][:, 0:1], 0.5, ALU.mult,
                                                       ALU.mult))
                            link(dve.tensor_tensor(ex[t][:, p], ex[t][:, p], dots[t][:, p], ALU.mult))
                            dve.wait_ge(sem("tanh_ready"), blk + (layer * NSTEP + i + 1))
                            dve.wait_ge(v_free, blk * TOPK + (vb + VS - TOPK))
                            dve.scalar_tensor_tensor(wts[t][:, p], tanh[t][:, p], 1.0, ex[t][:, p], ALU.add, ALU.mult
                                                     ).then_inc(sem("w_ready"), 1)
                        if last and t == NT - 1:
                            return
                        if t == 0:
                            dve.wait_ge(sem("s_ev"), h * 2 + (sb_ + 2))
                            apart(dve)
                        if t == NT - 1:
                            dve.wait_ge(sem("s_ev"), h * 2 + (sb_ + 4))
                            apart(dve)
                        choose(layer, (t + 1) % NT)

                dve.wait_ge(sem("first_s_ev"), 2 * (layer + 1))
                choose(layer, 0)
                dve.wait_ge(sem("xt_ev"), 6 * (layer + 1))
                with dve.Fori(0, PH - 1) as h:
                    link.enter(h, NT * (CHOOSE + 5))
                    head(h)
                    link.leave(PH - 1)
                head(PH - 1, last=True)
                residual_peer(layer)

            norm(0)
            modulation(0)
            dve.memset(A[2][:, 0:C * WPAD], 0.0).then_inc(sem("xpad_zero"), 1)
            for c in range(C):
                dve.wait_ge(sem("rg_in_ev"), c + 1)
                cw = [vec[:, V_CW + c * 4 + j:V_CW + c * 4 + j + 1] for j in range(4)]
                link(dve.tensor_scalar(xr[:, c, :], xpad[:, c, 0:WX], cw[0], vec[:, V_CB + c:V_CB + c + 1], ALU.mult,
                                       ALU.add))
                for j in range(1, 4):
                    ins = dve.scalar_tensor_tensor(xr[:, c, :], xpad[:, c, j:j + WX], cw[j], xr[:, c, :], ALU.mult,
                                                   ALU.add)
                    if j < 3:
                        link(ins)
                ins.then_inc(sem("xr_ready"), 1)
            modulation(1)
            modulation(2)
            for d in range(2):
                dve.wait_ge(sem("rg_gate_ev"), 16 * (d + 1))
                link(dve.tensor_tensor(g_i[d], g_i[d], xr, ALU.mult))
                dve.wait_ge(sem("rg_sqrt"), d + 1)
                dve.wait_ge(sem("rg_a"), C * (d + 1))
                link(dve.scalar_tensor_tensor(g_b[d], g_a[d], 1.0, g_b[d], ALU.add, ALU.mult))
                link(dve.tensor_tensor(g_b[d], g_b[d], g_i[d], ALU.mult))
                for c in range(C):
                    for s_, (a, b) in enumerate(((0, TP), (S0, WX))):
                        w_ = slice(a, b) if d == 0 else (slice(b - 1, a - 1, -1) if a else slice(b - 1, None, -1))
                        h0 = vec[:, V_H0 + d * C + c:V_H0 + d * C + c + 1] if s_ else 0.0
                        dve.tensor_tensor_scan(g_i[d][:, c, w_], g_a[d][:, c, w_], g_b[d][:, c, w_], h0, ALU.mult,
                                               ALU.add).then_inc(sem("rg_scan"), 1)
                if d == 0:
                    modulation(3)
            dve.wait_ge(sem("rg_scan"), 4 * C)
            h_sum = g_i[0]
            dve.tensor_copy(rgfin[:, 0, :], g_i[0][:, :, TP - 1])
            link(dve.tensor_copy(rgfin[:, 1, :], g_i[1][:, :, 0]))
            dve.wait_ge(sem("rg_in_ev"), 2 * C)
            for c in range(0, C, 2):
                cc = slice(c, c + 2)
                link(dve.tensor_tensor(h_sum[:, cc, :], g_i[0][:, cc, :], g_i[1][:, cc, :], ALU.add))
                dve.tensor_tensor(gate_br[:, cc, 0:TP], gate_br[:, cc, 0:TP], h_sum[:, cc, 0:TP], ALU.mult
                                  ).then_inc(sem("hg_ready"), 1)
                dve.tensor_tensor(gate_br[:, cc, TP:T], gate_br[:, cc, TP:T], h_sum[:, cc, S0:WX], ALU.mult
                                  ).then_inc(sem("hg_ready"), 1)
            dve.memset(work[:, 0:1], 0.0).then_inc(sem("rg_fin"), 1)
            modulation(4)
            for c in range(C):
                if c == 4:
                    modulation(5)
                dve.wait_ge(sem("rg_out_mm"), c + 1)
                for s_, (a, b) in enumerate(SEG):
                    ins = dve.scalar_tensor_tensor(xT[:, c, a:b], bank[c % 4][:, a:b], mods_of[0][:, 2 * C + c, s_:s_ + 1],
                                                   xT[:, c, a:b], ALU.mult, ALU.add)
                ins.then_inc(sem("x_ev"), 1)
            norm(1)
            peer(0)

            norm(2)
            dve.wait_ge(sem("z_mm"), 1)
            dve.tensor_copy(zT, bank[0][0:2 * RANK, 0:T]).then_inc(sem("z_ev"), 1)
            keep = qin
            link(dve.memset(keep, 1.0))
            for d, col in ((0, 0), (1, CH - 1)):
                ins = dve.memset(keep[:, d * 1536:(d + 1) * 1536].rearrange("p (n i) -> p n i", i=CH)[:, :, col:col + 1],
                                 0.0)
            link(ins)
            dve.wait_ge(sem("la_ln"), 1)
            link(dve.scalar_tensor_tensor(la, la, 0.0, labs, ALU.min, ALU.subtract))
            dve.tensor_tensor_scan(bc[:, 0:1536], keep[:, 0:1536], la[:, 0:1536], 0.0, ALU.mult, ALU.add
                                   ).then_inc(sem("bc_ready"), 1)
            dve.tensor_tensor_scan(bc[:, 3071:1535:-1], keep[:, 3071:1535:-1], la[:, 3071:1535:-1], 0.0, ALU.mult,
                                   ALU.add).then_inc(sem("bc_ready"), 1)
            dve.wait_ge(sem("bc_ready"), 2)
            for d in range(2):
                b3 = bc[:, d * 1536:(d + 1) * 1536].rearrange("p (n i) -> p n i", i=CH)
                last = CH - 1 if d == 0 else 0
                dve.tensor_tensor(labs[:, d * 1536:(d + 1) * 1536].rearrange("p (n i) -> p n i", i=CH),
                                  b3[:, :, last:last + 1].to_broadcast([P, 24, CH]), b3, ALU.subtract
                                  ).then_inc(sem("dd_ready"), 1)
            for i in range(HEADS * NT):
                dve.wait_ge(sem("v_mm"), i + 1)
                h, t = i // NT, i % NT
                dve.tensor_copy(vtok[:, t, h * DV:(h + 1) * DV], bank[(2 + i) % 4][:, 0:DV]).then_inc(sem("v_ev"), 1)
            dve.wait_ge(sem("qk_ev"), 8)
            qv = A[3][:, 0:1536]
            kv = A[3][:, 1536:3072]
            halves = [slice(0, 1536), slice(1536, 3072)]
            dve.wait_ge(sem("gla_e"), 3)
            for d in range(2):
                dve.tensor_tensor(kst[:, halves[d]], kst[:, halves[d]], kv, ALU.mult).then_inc(sem("kst_ready"), 1)
            for d in range(2):
                dve.tensor_tensor(kin[:, halves[d]], kin[:, halves[d]], kv, ALU.mult).then_inc(sem("kin_ready"), 1)
            for d in range(2):
                dve.tensor_tensor(qin[:, halves[d]], la[:, halves[d]], qv, ALU.mult).then_inc(sem("qin_ready"), 1)
            dve.wait_ge(sem("gla_e"), 5)
            dve.wait_ge(sem("qin_ready"), 2)
            dve.wait_ge(sem("kin_ready"), 2)
            dve.wait_ge(sem("kst_ready"), 2)
            dve.memset(work[:, 0:1], 0.0).then_inc(sem("kst_used"), 1)
            link(dve.memset(att2, 0.0))
            dve.wait_ge(mask_in, 16)
            for t in range(NT):
                dve.wait_ge(sem("att_mm"), t + 1)
                link(dve.memset(attm, 0.0))
                link(dve.copy_predicated(attm, mask, bank[4 + t % 2]))
                for r in (0, CH):
                    link(dve.tensor_tensor(att2[r:r + CH, t, :, r:r + CH],
                                           attm[r:r + CH, 0:256].rearrange("p (h i) -> p h i", h=HEADS),
                                           attm[r:r + CH, 256:512].rearrange("p (h i) -> p h i", h=HEADS), ALU.add))
                dve.memset(work[:, 0:1], 0.0).then_inc(sem("att_ev"), 1)
            dve.wait_ge(s0_in, 16)
            n_u = 0

            def states(h):
                nonlocal n_u
                st = state[h % 2]
                if h >= 2:
                    dve.wait_ge(sem("o_mm"), h - 1)
                    dve.wait_ge(sem(f"st_gla_out{h % 2}"), 32 * (h // 2))
                for d, chunks in ((0, (0, 1, 2, 3, 4)), (1, (1, 0, 5, 4, 3))):
                    for i, n in enumerate(chunks):
                        nxt = (n + 1 if d == 0 else n - 1) if i != 1 else d
                        prev = s0_all[:, d, h, :] if i == 2 else st[:, d, n, :]
                        dve.wait_ge(sem("u_mm"), n_u + 1)
                        u = bank[2 + n_u % 4][:, 0:DV]
                        if i == 0:
                            ins = dve.tensor_copy(st[:, d, nxt, :], u)
                        else:
                            g = gdec[:, d * 24 + h * NCH + n:d * 24 + h * NCH + n + 1]
                            ins = dve.scalar_tensor_tensor(st[:, d, nxt, :], prev, g, u, ALU.mult, ALU.add)
                        ins.then_inc(sem("gla_state"), 1)
                        n_u += 1
                        dve.wait_ge(sem("gla_state"), n_u)

            states(0)
            for h in range(HEADS):
                if h + 1 < HEADS:
                    states(h + 1)
                dve.wait_ge(sem("o_ev"), 4 * (h + 1))
                dve.wait_ge(sem("g_ev"), 8)
                dve.wait_ge(sem("o_sd"), h + 1)
                link(dve.reciprocal(rstd[:, :], sd[:, :]))
                dve.memset(work[:, 0:1], 0.0).then_inc(sem("o_rstd"), 1)
                for v2 in range(2):
                    c = 2 * h + v2
                    link(dve.scalar_tensor_tensor(oT[:, c, :], oT[:, c, :], vec[:, V_GNG + c:V_GNG + c + 1],
                                                  rstd[:, :], ALU.mult, ALU.mult))
                    ins = dve.tensor_tensor(oT[:, c, :], oT[:, c, :], silu_g[:, c, :], ALU.mult)
                ins.then_inc(sem("og_ready"), 1)
                if h == HEADS - 1:
                    dve.wait_ge(sem("og_ready"), HEADS)
                    dve.memset(work[:, 0:1], 0.0).then_inc(sem("att_used"), 1)
            for c in range(C):
                dve.wait_ge(sem("gla_out_mm"), c + 1)
                dve.scalar_tensor_tensor(xT[:, c, 0:TP], bank[c % 4][:, 0:TP], mods_of[1][:, 2 * C + c, 0:1],
                                         xT[:, c, 0:TP], ALU.mult, ALU.add)
                xs = xT[:, c, TP:T].rearrange("p (r w) -> p r w", r=ROWS)
                dve.scalar_tensor_tensor(xs, bank[c % 4][:, TP:T].rearrange("p (w r) -> p r w", r=ROWS),
                                         mods_of[1][:, 2 * C + c, 1:2], xs, ALU.mult, ALU.add
                                         ).then_inc(sem("x_ev"), 1)
            norm(3)
            peer(1)
            dve.wait_ge(sem("sd_ready"), 5)
            link(dve.reciprocal(rstd[:, :], sd[:, :]))
            for c in range(C):
                dve.scalar_tensor_tensor(hT[:, c, :], xT[:, c, :], vec[:, V_FG + c:V_FG + c + 1], rstd[:, :], ALU.mult,
                                         ALU.mult).then_inc(sem("y_ready"), 1)


def kernel(**inputs):
    import numpy as np
    import concourse.bacc as bacc
    from concourse import mybir as mb
    from concourse.bass_utils import run_bass_kernel_spmd as run

    a = {k: np.asarray(v) for k, v in inputs.items()}

    def feat(v):
        v = v.reshape(-1, C, P)
        return v.transpose(2, 0, 1).reshape(P, -1)

    f = np.float32
    tt = np.arange(TS)
    nf = D // 4
    freq = (f(1.0) / (f(10000.0) ** (np.arange(nf, dtype=f) / f(nf)))).astype(f)
    ar = (tt // GRID_W).astype(f)[:, None] * freq
    ac = (tt % GRID_W).astype(f)[:, None] * freq
    pos = np.concatenate([np.sin(ar), np.cos(ar), np.sin(ac), np.cos(ac)], axis=-1).astype(f)

    def to_feat(x):
        return np.ascontiguousarray(x.T.reshape(C, P, -1).transpose(1, 0, 2))

    x = np.concatenate([a["x_prompt"][0], a["x_sample"][0]], axis=0)
    vecs = np.zeros((P, V_END), f)
    vecs[:, V_COND:V_COND + 8] = feat(a["c_ctx"])
    vecs[:, V_COND + 8:V_COND + 16] = feat(a["c"])
    vecs[:, V_N1:V_N1 + 16] = feat(a["norm1_g"])
    vecs[:, V_N2:V_N2 + 16] = feat(a["norm2_g"])
    vecs[:, V_ADAB:V_ADAB + 96] = feat(a["ada_b"])
    vecs[:, V_CW:V_CW + 32] = a["rg_conv_w"][0].reshape(4, C, P).transpose(2, 1, 0).reshape(P, 32)
    vecs[:, V_CB:V_CB + 8] = feat(a["rg_conv_b"])
    vecs[:, V_BA:V_BA + 16] = feat(a["rg_ba"][0])
    vecs[:, V_BI:V_BI + 16] = feat(a["rg_bi"][0])
    vecs[:, V_LAM:V_LAM + 16] = feat(a["rg_lambda"][0])
    vecs[:, V_H0:V_H0 + 16] = feat(a["state_rglru"][0, 0])
    vecs[:, V_BAL:V_BAL + 8] = a["gla_b_alpha"][0].reshape(8, P).T
    vecs[:, V_GNG:V_GNG + 8] = feat(a["gla_norm_g"])
    vecs[:, V_FG:V_FG + 8] = feat(a["final_norm_g"])
    vecs[:, V_EPS] = 1e-6
    keys = np.stack([a["peer_k1"], a["peer_k2"]], axis=2)
    keys = np.ascontiguousarray(keys.transpose(4, 0, 1, 2, 3).reshape(P, DEPTH, 2 * PH * NK))
    j, i = np.arange(P)[:, None] % CH, np.arange(CH)[None, :]
    mask = np.concatenate([np.tile(j <= i, (1, HEADS)), np.tile(j >= i, (1, HEADS))], axis=1).astype(np.uint32)
    arrays = {
        "x_t": to_feat(x), "pos_t": to_feat(pos), "vecs": vecs, "ident": np.eye(P, dtype=f), "mask": mask,
        "iota": np.tile(np.arange(TOPK, dtype=f), (P, 1)), "keys_t": keys,
        "ada_w": a["ada_w"], "peer_wq": a["peer_wq"], "peer_u": a["peer_u"], "peer_v": a["peer_v"],
        "rg_w_in": a["rg_w_in"], "rg_wa": a["rg_wa"], "rg_wi": a["rg_wi"], "rg_w_out": a["rg_w_out"],
        "gla_w_in": a["gla_w_in"], "w_alpha": a["gla_w_alpha"], "state_gla": a["state_gla"][0, 0],
        "gla_w_out": a["gla_w_out"],
    }
    arrays = {k: np.ascontiguousarray(v) for k, v in arrays.items()}
    nc = bacc.Bacc("TRN2", target_bir_lowering=False, num_devices=1)
    ins = [nc.dram_tensor("in_" + k, v.shape, mb.dt.from_np(v.dtype), kind="ExternalInput").ap() for k, v in arrays.items()]
    outs = [nc.dram_tensor("out_" + k, s, mb.dt.float32, kind="ExternalOutput").ap() for k, s in (
        ("y_t", (P, C, T)), ("st_rg", (P, 2, C)), ("st_gla", (2, HEADS, DK, DV)))]
    build(nc, *ins, *outs)
    r = run(nc, [{"in_" + k: v for k, v in arrays.items()}], core_ids=[0]).results[0]
    y = np.asarray(r["out_y_t"]).transpose(2, 1, 0).reshape(T, D)
    st_rg = np.asarray(r["out_st_rg"]).transpose(1, 2, 0).reshape(1, 1, 2, D)
    st_gla = np.asarray(r["out_st_gla"]).reshape(1, 1, 2, HEADS, DK, DV)
    return (np.ascontiguousarray(y[None, :TP]), np.ascontiguousarray(y[None, TP:]),
            np.ascontiguousarray(st_rg), np.ascontiguousarray(st_gla))
```
